# Optimizing a Trainium2 kernel written in Bass

```python
import math
import jax, jax.numpy as jnp
from jax import lax
import numpy as np
import jax
import jax.numpy as jnp

D_MODEL = 1024
BATCH = 1
SEQ = 256
DEPTH = 2

D_MIX = D_MODEL
HG_WIDTH = D_MIX // 2
HG_HEAD_DIM = 128
HG_HEADS = HG_WIDTH // HG_HEAD_DIM
HG_CHUNK = 64
NSA_WIDTH = D_MIX - HG_WIDTH
NSA_HEAD_DIM = 64
NSA_HEADS = NSA_WIDTH // NSA_HEAD_DIM
NSA_KV_GROUPS = 2
NSA_HPG = NSA_HEADS // NSA_KV_GROUPS
CMP_BLOCK = 32
CMP_STRIDE = 16
CMP_HIDDEN = 128
SLC_BLOCK = 64
SLC_TOPK = 16
SLC_LOCAL = 2
WINDOW = 512
Q_BLOCK = 64
N_BUCKETS = 32
MAX_DISTANCE = 128
D_FF = ((8 * D_MODEL // 3 + 255) // 256) * 256
ALPHA = (2.0 * DEPTH) ** 0.25
BETA = (8.0 * DEPTH) ** -0.25
KV_W = NSA_KV_GROUPS * NSA_HEAD_DIM
SPLIT_SIZES = (HG_WIDTH, HG_WIDTH, HG_WIDTH, HG_WIDTH, NSA_WIDTH, KV_W, KV_W, KV_W, KV_W, KV_W, KV_W, 3 * NSA_HEADS)
D_IN = sum(SPLIT_SIZES)
NEG = -1e30
BIG = 1e9


def _split_points():
    pts, acc = [], 0
    for s in SPLIT_SIZES[:-1]:
        acc += s
        pts.append(acc)
    return pts

def layer_norm(x, g, b, eps=1e-5):
    xf = x.astype(jnp.float32)
    mu = jnp.mean(xf, -1, keepdims=True)
    var = jnp.mean(jnp.square(xf - mu), -1, keepdims=True)
    return ((xf - mu) * lax.rsqrt(var + eps) * g + b).astype(x.dtype)

def hgrn2_lower_bounds(lb_param):
    p = jax.nn.softmax(lb_param.astype(jnp.float32), axis=0)
    c = jnp.cumsum(p, axis=0)
    return c - c[0:1]

def hgrn2_mixer(q, f_logit, i, g, lb, gnorm_w):
    B, S, _ = q.shape
    H, Dk, C = HG_HEADS, HG_HEAD_DIM, HG_CHUNK
    N = S // C
    f32 = jnp.float32
    logf = jnp.logaddexp(jnp.log(lb), jnp.log1p(-lb) + jax.nn.log_sigmoid(f_logit.astype(f32)))
    k = -jnp.expm1(logf)

    def to_chunks(t):
        return t.astype(f32).reshape(B, N, C, H, -1).transpose(1, 0, 3, 2, 4)

    qc, kc, vc = to_chunks(q), to_chunks(k), to_chunks(i)
    bc = jnp.cumsum(to_chunks(logf), axis=3)
    causal = jnp.tril(jnp.ones((C, C), bool))

    def step(state, xs):
        qb, kb, vb, bb = xs
        rel = bb[:, :, :, None, :] - bb[:, :, None, :, :]
        decay = jnp.exp(jnp.where(causal[:, :, None], rel, -jnp.inf))
        scores = jnp.einsum('bhtd,bhsd,bhtsd->bhts', qb, kb, decay)
        o_intra = jnp.einsum('bhts,bhsv->bhtv', scores, vb)
        o_inter = jnp.einsum('bhtd,bhdv->bhtv', qb * jnp.exp(bb), state)
        b_last = bb[:, :, -1:, :]
        k_dec = kb * jnp.exp(b_last - bb)
        new_state = state * jnp.exp(b_last[:, :, 0, :, None]) + jnp.einsum('bhsd,bhsv->bhdv', k_dec, vb)
        return new_state, o_intra + o_inter

    s0 = jnp.zeros((B, H, Dk, Dk), f32)
    _, o = lax.scan(step, s0, (qc, kc, vc, bc))
    o = o.transpose(1, 0, 3, 2, 4).reshape(B, S, H, Dk)
    o = o * lax.rsqrt(jnp.mean(o * o, -1, keepdims=True) + 1e-6) * gnorm_w
    o = o.reshape(B, S, HG_WIDTH) * jax.nn.silu(g.astype(f32))
    return o.astype(q.dtype)

def t5_bucket(n):
    n = jnp.maximum(n, 0)
    max_exact = N_BUCKETS // 2
    nf = jnp.maximum(n, 1).astype(jnp.float32)
    large = max_exact + (jnp.log(nf / max_exact) / math.log(MAX_DISTANCE / max_exact)
                         * (N_BUCKETS - max_exact)).astype(jnp.int32)
    large = jnp.minimum(large, N_BUCKETS - 1)
    return jnp.where(n < max_exact, n, large)

def masked_softmax(s, valid):
    s = jnp.where(valid, s, NEG)
    p = jax.nn.softmax(s, axis=-1)
    return jnp.where(valid, p, 0.0)

def nsa_mixer(q, k_cmp, v_cmp, k_slc, v_slc, k_win, v_win, gates,
              cmp_pos_k, cmp_w1_k, cmp_w2_k, cmp_pos_v, cmp_w1_v, cmp_w2_v, rel_bias):
    B, S, _ = q.shape
    G, HPG, Dh = NSA_KV_GROUPS, NSA_HPG, NSA_HEAD_DIM
    f32 = jnp.float32
    scale = Dh ** -0.5
    rb = rel_bias.astype(f32)
    qh = q.astype(f32).reshape(B, S, G, HPG, Dh).transpose(0, 2, 3, 1, 4)
    gh = jax.nn.sigmoid(gates.astype(f32)).reshape(B, S, 3, G, HPG).transpose(0, 3, 4, 1, 2)

    def kv(t):
        return t.astype(f32).reshape(B, S, G, Dh).transpose(0, 2, 1, 3)

    n_cmp = (S - CMP_BLOCK) // CMP_STRIDE + 1

    def compress(t, pos, w1, w2):
        c = kv(t).reshape(B, G, S // CMP_STRIDE, CMP_STRIDE, Dh)
        blocks = jnp.concatenate([c[:, :, :-1], c[:, :, 1:]], axis=3)
        blocks = (blocks + pos).reshape(B, G, n_cmp, CMP_BLOCK * Dh)
        return jax.nn.gelu(blocks @ w1) @ w2

    kc = compress(k_cmp, cmp_pos_k, cmp_w1_k, cmp_w2_k)
    vc = compress(v_cmp, cmp_pos_v, cmp_w1_v, cmp_w2_v)
    cmp_start = jnp.arange(n_cmp) * CMP_STRIDE
    cmp_end = cmp_start + CMP_BLOCK - 1

    n_slc = S // SLC_BLOCK
    n_sel = min(SLC_TOPK, n_slc)
    ks_blocks = kv(k_slc).reshape(B, G, n_slc, SLC_BLOCK, Dh)
    vs_blocks = kv(v_slc).reshape(B, G, n_slc, SLC_BLOCK, Dh)
    slc_start = jnp.arange(n_slc) * SLC_BLOCK
    overlap = jnp.clip(jnp.minimum(cmp_start[:, None] + CMP_BLOCK, slc_start[None, :] + SLC_BLOCK)
                       - jnp.maximum(cmp_start[:, None], slc_start[None, :]), 0, None)
    agg = overlap.astype(f32) / CMP_STRIDE

    kw_pad = jnp.pad(kv(k_win), ((0, 0), (0, 0), (WINDOW, 0), (0, 0)))
    vw_pad = jnp.pad(kv(v_win), ((0, 0), (0, 0), (WINDOW, 0), (0, 0)))
    tab_g = rb.reshape(N_BUCKETS, G, HPG)
    bi = jnp.arange(B)[:, None, None, None]
    gi = jnp.arange(G)[None, :, None, None]

    def head_bias(dist):
        bsh = rb[t5_bucket(dist)]
        return bsh.reshape(dist.shape + (G, HPG)).transpose(2, 3, 0, 1)

    def block_fn(qb_idx):
        t0 = qb_idx * Q_BLOCK
        t_pos = t0 + jnp.arange(Q_BLOCK)
        qblk = lax.dynamic_slice_in_dim(qh, t0, Q_BLOCK, axis=3)
        gblk = lax.dynamic_slice_in_dim(gh, t0, Q_BLOCK, axis=3)
        s_c = jnp.einsum('bghtd,bgnd->bghtn', qblk, kc) * scale + head_bias(t_pos[:, None] - cmp_end[None, :])
        valid_c = cmp_end[None, :] <= t_pos[:, None]
        p_c = masked_softmax(s_c, valid_c)
        o_c = jnp.einsum('bghtn,bgnd->bghtd', p_c, vc)
        imp = jnp.einsum('bghtn,nj->bgtj', p_c, agg)
        cur = t_pos // SLC_BLOCK
        j = jnp.arange(n_slc)
        diff = cur[:, None] - j[None, :]
        forced = (j[None, :] == 0) | ((diff >= 0) & (diff < SLC_LOCAL))
        causal_blk = slc_start[None, :] <= t_pos[:, None]
        score = jnp.where(forced, BIG, jnp.where(causal_blk, imp, -BIG))
        _, idx = lax.top_k(score, n_sel)
        L = n_sel * SLC_BLOCK
        ks_g = ks_blocks[bi, gi, idx].reshape(B, G, Q_BLOCK, L, Dh)
        vs_g = vs_blocks[bi, gi, idx].reshape(B, G, Q_BLOCK, L, Dh)
        key_pos = (idx[..., None] * SLC_BLOCK + jnp.arange(SLC_BLOCK)).reshape(B, G, Q_BLOCK, L)
        dist_s = t_pos[None, None, :, None] - key_pos
        bias_s = jax.vmap(lambda tb, bk: tb[bk], in_axes=(1, 1), out_axes=1)(tab_g, t5_bucket(dist_s))
        bias_s = bias_s.transpose(0, 1, 4, 2, 3)
        s_s = jnp.einsum('bghtd,bgtld->bghtl', qblk, ks_g) * scale + bias_s
        p_s = masked_softmax(s_s, (dist_s >= 0)[:, :, None])
        o_s = jnp.einsum('bghtl,bgtld->bghtd', p_s, vs_g)
        kw = lax.dynamic_slice_in_dim(kw_pad, t0, WINDOW + Q_BLOCK, axis=2)
        vw = lax.dynamic_slice_in_dim(vw_pad, t0, WINDOW + Q_BLOCK, axis=2)
        kpos = t0 - WINDOW + jnp.arange(WINDOW + Q_BLOCK)
        dist_w = t_pos[:, None] - kpos[None, :]
        valid_w = (dist_w >= 0) & (dist_w < WINDOW) & (kpos[None, :] >= 0)
        s_w = jnp.einsum('bghtd,bgkd->bghtk', qblk, kw) * scale + head_bias(dist_w)
        p_w = masked_softmax(s_w, valid_w)
        o_w = jnp.einsum('bghtk,bgkd->bghtd', p_w, vw)
        return gblk[..., 0:1] * o_c + gblk[..., 1:2] * o_s + gblk[..., 2:3] * o_w

    o = lax.map(block_fn, jnp.arange(S // Q_BLOCK))
    o = o.transpose(1, 0, 4, 2, 3, 5).reshape(B, S, NSA_WIDTH)
    return o.astype(q.dtype)

def first_inputs(seed: int = 0) -> dict:
    key = jax.random.key(seed)
    ks = jax.random.split(key, 20)
    f32 = jnp.float32

    def nrm(k, shape, fan_in, scale=1.0):
        return jax.random.normal(k, shape, f32) * (scale * fan_in ** -0.5)

    def small(k, shape, s):
        return jax.random.normal(k, shape, f32) * s

    return {
        "x": jax.random.normal(ks[0], (BATCH, SEQ, D_MODEL), f32),
        "w_in": nrm(ks[1], (DEPTH, D_MODEL, D_IN), D_MODEL),
        "hg_lb_param": small(ks[2], (DEPTH, HG_WIDTH), 0.1),
        "hg_norm_w": 1.0 + small(ks[3], (DEPTH, HG_HEAD_DIM), 0.02),
        "cmp_pos_k": small(ks[4], (DEPTH, CMP_BLOCK, NSA_HEAD_DIM), 0.02),
        "cmp_w1_k": nrm(ks[5], (DEPTH, CMP_BLOCK * NSA_HEAD_DIM, CMP_HIDDEN), CMP_BLOCK * NSA_HEAD_DIM),
        "cmp_w2_k": nrm(ks[6], (DEPTH, CMP_HIDDEN, NSA_HEAD_DIM), CMP_HIDDEN),
        "cmp_pos_v": small(ks[7], (DEPTH, CMP_BLOCK, NSA_HEAD_DIM), 0.02),
        "cmp_w1_v": nrm(ks[8], (DEPTH, CMP_BLOCK * NSA_HEAD_DIM, CMP_HIDDEN), CMP_BLOCK * NSA_HEAD_DIM),
        "cmp_w2_v": nrm(ks[9], (DEPTH, CMP_HIDDEN, NSA_HEAD_DIM), CMP_HIDDEN),
        "rel_bias": small(ks[10], (N_BUCKETS, NSA_HEADS), 0.1),
        "w_out": nrm(ks[11], (DEPTH, D_MIX, D_MODEL), D_MIX, BETA),
        "ln1_g": 1.0 + small(ks[12], (DEPTH, D_MODEL), 0.02),
        "ln1_b": small(ks[13], (DEPTH, D_MODEL), 0.02),
        "w_ffn_gate": nrm(ks[14], (DEPTH, D_MODEL, D_FF), D_MODEL),
        "w_ffn_up": nrm(ks[15], (DEPTH, D_MODEL, D_FF), D_MODEL),
        "w_ffn_down": nrm(ks[16], (DEPTH, D_FF, D_MODEL), D_FF, BETA),
        "ln2_g": 1.0 + small(ks[17], (DEPTH, D_MODEL), 0.02),
        "ln2_b": small(ks[18], (DEPTH, D_MODEL), 0.02),
    }

def first_block(x, w_in, hg_lb_param, hg_norm_w, cmp_pos_k, cmp_w1_k, cmp_w2_k,
              cmp_pos_v, cmp_w1_v, cmp_w2_v, rel_bias, w_out, ln1_g, ln1_b,
              w_ffn_gate, w_ffn_up, w_ffn_down, ln2_g, ln2_b):
    lbs = hgrn2_lower_bounds(hg_lb_param)
    pts = _split_points()
    for l in range(DEPTH):
        proj = x @ w_in[l]
        hq, hf, hi, hg, nq, kc, vc, ks, vs, kw, vw, gt = jnp.split(proj, pts, axis=-1)
        o_a = hgrn2_mixer(hq, hf, hi, hg, lbs[l], hg_norm_w[l])
        o_b = nsa_mixer(nq, kc, vc, ks, vs, kw, vw, gt,
                        cmp_pos_k[l], cmp_w1_k[l], cmp_w2_k[l],
                        cmp_pos_v[l], cmp_w1_v[l], cmp_w2_v[l], rel_bias)
        mix = jnp.concatenate([o_a, o_b], axis=-1) @ w_out[l]
        x = layer_norm(ALPHA * x + mix, ln1_g[l], ln1_b[l])
        ffn = (jax.nn.silu(x @ w_ffn_gate[l]) * (x @ w_ffn_up[l])) @ w_ffn_down[l]
        x = layer_norm(ALPHA * x + ffn, ln2_g[l], ln2_b[l])
    return x


N_HEADS = 16
HEAD_DIM = 64
A_HEADS = 8
B_HEADS = 8
MOBA_BLOCK = 256
MOBA_TOPK = 3
MOBA_Q_CHUNK = 64
IDX_HEADS = 16
IDX_DIM = 64
DSA_TOPK_MAX = 256
DSA_Q_CHUNK = 128
DILATED_PATTERNS = ((128, 1), (512, 4), (2048, 16))
REL_BUCKETS = 32
REL_MAX_DIST = 128
D_FF_2 = 2816
CONV_WIDTH = 3
RMS_EPS = 1e-6


def rmsnorm(x, g):
    x32 = x.astype(jnp.float32)
    y = x32 * lax.rsqrt(jnp.mean(x32 * x32, axis=-1, keepdims=True) + RMS_EPS)
    return (y * g.astype(jnp.float32)).astype(x.dtype)

def t5_bucket_2(dist):
    n = jnp.maximum(dist, 0)
    max_exact = REL_BUCKETS // 2
    nf = jnp.maximum(n, max_exact).astype(jnp.float32)
    large = max_exact + (jnp.log(nf / max_exact) / math.log(REL_MAX_DIST / max_exact)
                         * (REL_BUCKETS - max_exact)).astype(jnp.int32)
    large = jnp.minimum(large, REL_BUCKETS - 1)
    return jnp.where(n < max_exact, n, large)

def split_cols(a, sizes):
    out, off = [], 0
    for s in sizes:
        out.append(a[..., off:off + s])
        off += s
    return out

def moba_attention(q, k, v, table_hk):
    B, H, S, Dh = q.shape
    nb = -(-S // MOBA_BLOCK)
    pad = nb * MOBA_BLOCK - S
    kb = jnp.pad(k, ((0, 0), (0, 0), (0, pad), (0, 0))).reshape(B, H, nb, MOBA_BLOCK, Dh)
    vb = jnp.pad(v, ((0, 0), (0, 0), (0, pad), (0, 0))).reshape(B, H, nb, MOBA_BLOCK, Dh)
    kmean = jnp.mean(kb.astype(jnp.float32), axis=3).astype(k.dtype)
    n_sel = min(MOBA_TOPK, nb - 1)
    scale = Dh ** -0.5
    nq = S // MOBA_Q_CHUNK
    qc = jnp.moveaxis(q.reshape(B, H, nq, MOBA_Q_CHUNK, Dh), 2, 0)
    bi = jnp.arange(B)[:, None, None, None]
    hi = jnp.arange(H)[None, :, None, None]
    offs = jnp.arange(MOBA_BLOCK)
    blk_ids = jnp.arange(nb)

    def chunk(args):
        qi, c = args
        q0 = c * MOBA_Q_CHUNK
        t = q0 + jnp.arange(MOBA_Q_CHUNK)
        own = q0 // MOBA_BLOCK
        k_own = lax.dynamic_index_in_dim(kb, own, axis=2, keepdims=False)
        v_own = lax.dynamic_index_in_dim(vb, own, axis=2, keepdims=False)
        d_own = t[:, None] - (own * MOBA_BLOCK + offs)[None, :]
        l_own = jnp.einsum('bhqd,bhkd->bhqk', qi, k_own).astype(jnp.float32) * scale
        l_own = jnp.where(d_own >= 0, l_own + table_hk[:, t5_bucket_2(d_own)], -jnp.inf)
        if n_sel == 0:
            p = jax.nn.softmax(l_own, axis=-1).astype(v.dtype)
            return jnp.einsum('bhqk,bhkd->bhqd', p, v_own)
        gate = jnp.einsum('bhqd,bhnd->bhqn', qi, kmean).astype(jnp.float32)
        gate = jnp.where(blk_ids < own, gate, -jnp.inf)
        _, sel = lax.top_k(gate, n_sel)
        k_sel = kb[bi, hi, sel]
        v_sel = vb[bi, hi, sel]
        d_sel = t[None, None, :, None, None] - (sel[..., None] * MOBA_BLOCK + offs)
        l_sel = jnp.einsum('bhqd,bhqnkd->bhqnk', qi, k_sel).astype(jnp.float32) * scale
        l_sel = l_sel + table_hk[hi[..., None], t5_bucket_2(d_sel)]
        l_sel = jnp.where((sel < own)[..., None], l_sel, -jnp.inf)
        n_k = n_sel * MOBA_BLOCK
        logits = jnp.concatenate([l_sel.reshape(B, H, MOBA_Q_CHUNK, n_k), l_own], axis=-1)
        p = jax.nn.softmax(logits, axis=-1).astype(v.dtype)
        p_sel = p[..., :n_k].reshape(B, H, MOBA_Q_CHUNK, n_sel, MOBA_BLOCK)
        p_own = p[..., n_k:]
        return (jnp.einsum('bhqnk,bhqnkd->bhqd', p_sel, v_sel)
                + jnp.einsum('bhqk,bhkd->bhqd', p_own, v_own))

    out = lax.map(chunk, (qc, jnp.arange(nq, dtype=jnp.int32)))
    return jnp.moveaxis(out, 0, 2).reshape(B, H, S, Dh)

def dsa_attention(q, k, v, q_idx, k_idx, w_idx, table_hk):
    B, S, H, Dh = q.shape
    n_keep = min(DSA_TOPK_MAX, S // 4)
    nq = S // DSA_Q_CHUNK
    scale = Dh ** -0.5
    key_pos = jnp.arange(S)
    bi = jnp.arange(B)[:, None, None]

    def chunkify(a):
        return jnp.moveaxis(a.reshape((B, nq, DSA_Q_CHUNK) + a.shape[2:]), 1, 0)

    def chunk(args):
        qi, qii, wi, c = args
        t = c * DSA_Q_CHUNK + jnp.arange(DSA_Q_CHUNK)
        rel = jax.nn.relu(jnp.einsum('bqhd,bsd->bqhs', qii, k_idx) * (IDX_DIM ** -0.5))
        score = jnp.einsum('bqhs,bqh->bqs', rel, wi).astype(jnp.float32)
        score = jnp.where(key_pos[None, :] <= t[:, None], score, -jnp.inf)
        _, sel = lax.top_k(score, n_keep)
        k_sel = k[bi, sel]
        v_sel = v[bi, sel]
        d = t[None, :, None] - sel
        logits = jnp.einsum('bqhd,bqkhd->bhqk', qi, k_sel).astype(jnp.float32) * scale
        logits = logits + jnp.moveaxis(table_hk[:, t5_bucket_2(d)], 0, 1)
        logits = jnp.where((d >= 0)[:, None], logits, -jnp.inf)
        p = jax.nn.softmax(logits, axis=-1).astype(v.dtype)
        return jnp.einsum('bhqk,bqkhd->bqhd', p, v_sel)

    out = lax.map(chunk, (chunkify(q), chunkify(q_idx), chunkify(w_idx),
                          jnp.arange(nq, dtype=jnp.int32)))
    return jnp.moveaxis(out, 0, 1).reshape(B, S, H, Dh)

def dilated_branch(q, k, v, table_hk, window, dilation):
    B, H, S, Dh = q.shape
    w_sub = window // dilation
    bb = w_sub
    n = S // dilation
    nbk = -(-n // bb)
    npad = nbk * bb
    scale = Dh ** -0.5

    def to_sub(a):
        a = jnp.swapaxes(a.reshape(B, H, n, dilation, Dh), 2, 3)
        return jnp.pad(a, ((0, 0), (0, 0), (0, 0), (0, npad - n), (0, 0)))

    def band(a):
        ap = jnp.pad(a, ((0, 0), (0, 0), (0, 0), (bb, 0), (0, 0)))
        prev = ap[:, :, :, :npad].reshape(B, H, dilation, nbk, bb, Dh)
        cur = a.reshape(B, H, dilation, nbk, bb, Dh)
        return jnp.concatenate([prev, cur], axis=4)

    qs = to_sub(q).reshape(B, H, dilation, nbk, bb, Dh)
    kband = band(to_sub(k))
    vband = band(to_sub(v))
    logits = jnp.einsum('bhrnqd,bhrnkd->bhrnqk', qs, kband).astype(jnp.float32) * scale
    a_i = jnp.arange(bb)
    m_i = jnp.arange(2 * bb)
    di = a_i[:, None] + bb - m_i[None, :]
    band_ok = (di >= 0) & (di <= w_sub)
    j_idx = jnp.arange(nbk)[:, None] * bb - bb + m_i[None, :]
    mask = band_ok[None] & (j_idx >= 0)[:, None, :]
    bias = table_hk[:, t5_bucket_2(di * dilation)][:, None, None]
    logits = jnp.where(mask, logits + bias, -jnp.inf)
    mx = jnp.max(logits, axis=-1, keepdims=True)
    e = jnp.exp(logits - mx)
    den = jnp.sum(e, axis=-1, keepdims=True)
    o = jnp.einsum('bhrnqk,bhrnkd->bhrnqd', (e / den).astype(v.dtype), vband)
    lse = (mx + jnp.log(den))[..., 0]
    o = jnp.swapaxes(o.reshape(B, H, dilation, npad, Dh)[:, :, :, :n], 2, 3).reshape(B, H, S, Dh)
    lse = jnp.swapaxes(lse.reshape(B, H, dilation, npad)[:, :, :, :n], 2, 3).reshape(B, H, S)
    return o, lse

def dilated_mixture(q, k, v, table_hk):
    outs, lses = [], []
    for window, dilation in DILATED_PATTERNS:
        o, l = dilated_branch(q, k, v, table_hk, window, dilation)
        outs.append(o)
        lses.append(l)
    alpha = jax.nn.softmax(jnp.stack(lses, axis=0), axis=0)
    return jnp.einsum('pbhs,pbhsd->bhsd', alpha.astype(v.dtype), jnp.stack(outs, axis=0))

def conv_ffn(h, w_up, conv_w, conv_b, w_down):
    S = h.shape[1]
    u = h @ w_up
    up = jnp.pad(u, ((0, 0), (CONV_WIDTH - 1, 0), (0, 0)))
    c = conv_b
    for j in range(CONV_WIDTH):
        c = c + conv_w[j] * up[:, j:j + S]
    val, gate = jnp.split(c, 2, axis=-1)
    return (jax.nn.silu(gate) * val) @ w_down

def second_inputs(seed: int = 0) -> dict:
    key = jax.random.key(seed)
    ks = jax.random.split(key, 13)
    n_even = (DEPTH + 1) // 2
    n_odd = DEPTH // 2
    even_in = 3 * A_HEADS * HEAD_DIM + 3 * B_HEADS * HEAD_DIM + IDX_HEADS * IDX_DIM + IDX_DIM + IDX_HEADS
    odd_in = 3 * N_HEADS * HEAD_DIM
    mix = N_HEADS * HEAD_DIM

    def nrm(k, shape, s):
        return jax.random.normal(k, shape, jnp.float32) * s

    return {
        'x': nrm(ks[0], (BATCH, SEQ, D_MODEL), 1.0),
        'w_in_even': nrm(ks[1], (n_even, D_MODEL, even_in), D_MODEL ** -0.5),
        'idx_k_norm': 1.0 + nrm(ks[2], (n_even, IDX_DIM), 0.02),
        'w_in_odd': nrm(ks[3], (n_odd, D_MODEL, odd_in), D_MODEL ** -0.5),
        'w_o': nrm(ks[4], (DEPTH, mix, D_MODEL), mix ** -0.5),
        'rel_bias': nrm(ks[5], (REL_BUCKETS, N_HEADS), 0.2),
        'attn_norm': 1.0 + nrm(ks[6], (DEPTH, D_MODEL), 0.02),
        'ffn_norm': 1.0 + nrm(ks[7], (DEPTH, D_MODEL), 0.02),
        'w_up': nrm(ks[8], (DEPTH, D_MODEL, 2 * D_FF_2), D_MODEL ** -0.5),
        'conv_w': nrm(ks[9], (DEPTH, CONV_WIDTH, 2 * D_FF_2), CONV_WIDTH ** -0.5),
        'conv_b': nrm(ks[10], (DEPTH, 2 * D_FF_2), 0.02),
        'w_down': nrm(ks[11], (DEPTH, D_FF_2, D_MODEL), D_FF_2 ** -0.5),
        'final_norm': 1.0 + nrm(ks[12], (D_MODEL,), 0.02),
    }

def second_block(x, w_in_even, idx_k_norm, w_in_odd, w_o, rel_bias, attn_norm, ffn_norm,
              w_up, conv_w, conv_b, w_down, final_norm):
    B, S, _ = x.shape
    mix = N_HEADS * HEAD_DIM
    sizes_even = [A_HEADS * HEAD_DIM] * 3 + [B_HEADS * HEAD_DIM] * 3 + [IDX_HEADS * IDX_DIM, IDX_DIM, IDX_HEADS]
    sizes_odd = [N_HEADS * HEAD_DIM] * 3
    table_a = rel_bias[:, :A_HEADS].T
    table_b = rel_bias[:, A_HEADS:A_HEADS + B_HEADS].T
    table_c = rel_bias.T
    for layer in range(DEPTH):
        h = rmsnorm(x, attn_norm[layer])
        if layer % 2 == 0:
            j = layer // 2
            qa, ka, va, qb, kb, vb, qi, ki, wi = split_cols(h @ w_in_even[j], sizes_even)
            qa, ka, va = (jnp.swapaxes(a.reshape(B, S, A_HEADS, HEAD_DIM), 1, 2) for a in (qa, ka, va))
            o_a = jnp.swapaxes(moba_attention(qa, ka, va, table_a), 1, 2)
            qb, kb, vb = (a.reshape(B, S, B_HEADS, HEAD_DIM) for a in (qb, kb, vb))
            o_b = dsa_attention(qb, kb, vb,
                                qi.reshape(B, S, IDX_HEADS, IDX_DIM),
                                rmsnorm(ki, idx_k_norm[j]),
                                wi * (IDX_HEADS ** -0.5),
                                table_b)
            mixed = jnp.concatenate([o_a, o_b], axis=2).reshape(B, S, mix)
        else:
            j = layer // 2
            qc, kc, vc = (jnp.swapaxes(a.reshape(B, S, N_HEADS, HEAD_DIM), 1, 2)
                          for a in split_cols(h @ w_in_odd[j], sizes_odd))
            o_c = dilated_mixture(qc, kc, vc, table_c)
            mixed = jnp.swapaxes(o_c, 1, 2).reshape(B, S, mix)
        x = x + mixed @ w_o[layer]
        h = rmsnorm(x, ffn_norm[layer])
        x = x + conv_ffn(h, w_up[layer], conv_w[layer], conv_b[layer], w_down[layer])
    return rmsnorm(x, final_norm)


def setup_inputs(seed=0):
    out = dict(first_inputs(seed))
    for name, value in second_inputs(seed + 1).items():
        if name != "x":
            out[name + "_2"] = value
    return out


def reference(
    x, w_in, hg_lb_param, hg_norm_w, cmp_pos_k, cmp_w1_k, cmp_w2_k, cmp_pos_v, cmp_w1_v,
    cmp_w2_v, rel_bias, w_out, ln1_g, ln1_b, w_ffn_gate, w_ffn_up, w_ffn_down, ln2_g, ln2_b,
    w_in_even_2, idx_k_norm_2, w_in_odd_2, w_o_2, rel_bias_2, attn_norm_2, ffn_norm_2, w_up_2,
    conv_w_2, conv_b_2, w_down_2, final_norm_2,
):
    x = first_block(
        x, w_in, hg_lb_param, hg_norm_w, cmp_pos_k, cmp_w1_k, cmp_w2_k, cmp_pos_v, cmp_w1_v,
        cmp_w2_v, rel_bias, w_out, ln1_g, ln1_b, w_ffn_gate, w_ffn_up, w_ffn_down, ln2_g, ln2_b,
    )
    return second_block(
        x, w_in_even_2, idx_k_norm_2, w_in_odd_2, w_o_2, rel_bias_2, attn_norm_2, ffn_norm_2,
        w_up_2, conv_w_2, conv_b_2, w_down_2, final_norm_2,
    )


_drawn_inputs = setup_inputs


def setup_inputs(seed=0):
    import zlib

    import numpy as np

    out = dict(_drawn_inputs(seed))
    spreads = {}
    factors = {'hg_norm_w': 5.1,
     'cmp_pos_k': 33.812,
     'cmp_pos_v': 7.783,
     'rel_bias': 3.712,
     'idx_k_norm_2': 3.413,
     'ffn_norm_2': 2.725,
     'conv_b_2': 2.748,
     'final_norm_2': 8.002}
    for name, (base, spread) in spreads.items():
        noise = np.random.default_rng([zlib.crc32(name.encode()), seed]).standard_normal(out[name].shape)
        drawn = base * np.exp(spread * noise) if base else spread * noise
        out[name] = jnp.asarray(drawn.astype(out[name].dtype))
    for name, factor in factors.items():
        out[name] = (out[name] * factor).astype(out[name].dtype)
    return out
```

```python
from contextlib import ExitStack

import numpy as np
import concourse.bass as bass
from concourse import mybir

ALU = mybir.AluOpType
ACT = mybir.ActivationFunctionType
AX_X = mybir.AxisListType.X
F32 = mybir.dt.float32
U32 = mybir.dt.uint32

P = 128
S = 256
NT = S // P
D = 1024
KT = D // P
DFF = 2816
FT = DFF // P
LAYERS = 4
TILE = 2048
SLOTS = 7
RING = 4
ALPHA = 4.0 ** 0.25
HG_HEADS = 4
HEADS = 16
DH = 64
NC = 15
NCP = 16
CMP_KT = 16
NEG = -1e30
TAKEN = -2e30
TOPK = 64
ARENA = 14336
BUCKETS = 32
REV = S + P - 1
HALVES = [0, 128, 64, 32, 16, 8, 4, 2, 1]
TRI = S + P


def projections(l):
    if l < 2:
        return ["hf0", "hf1", "hq0", "hq1", "hi0", "hi1", "kcvc", "nq0", "nq1", "w1k", "w1v", "kskw", "vsvw",
                "hg0", "hg1"]
    if l == 2:
        return ([f"qi{j}" for j in range(4)] + [f"q{j}" for j in range(4)] + [f"k{j}" for j in range(4)]
                + [f"v{j}" for j in range(4)])
    return [f"q{j}" for j in range(4)] + [f"k{j}" for j in range(4)] + [f"v{j}" for j in range(4)]


def ffn_order():
    order = []
    for r in range(FT // 2):
        order += [("up", 2 * r), ("up", 2 * r + 1)]
        if r >= 1:
            order.append(("down", r - 1))
    order.append(("down", FT // 2 - 1))
    return order


def stream_order():
    order = []
    for l in range(LAYERS):
        order += [(l, name) for name in projections(l)]
        order += [(l, f"out{r}") for r in range(4)]
        order += [(l, f"{kind}{j}") for kind, j in ffn_order()]
    return order


def attention_steps():
    for i in range(HEADS + 2):
        yield (i if i < HEADS else None, i - 1 if 0 <= i - 1 < HEADS else None, i - 2 if i >= 2 else None)


def bank_order():
    uses = [("cmpbias",), ("biasrow",)] + [("bias", c) for c in range(12)]
    for l in range(LAYERS):
        if l == 2:
            uses += [(4, "xT", tt, q) for tt in range(NT) for q in range(2)]
        def attention():
            out = []
            for s, t, _ in attention_steps():
                out += [(l, "S", s)] if s is not None else []
                out += [(l, "T", t)] if t is not None else []
            return out
        if l < 2:
            names = projections(l)
            for n in names[:names.index("w1k")]:
                uses.append((l, n))
            uses += [(l, "hid"), (l, "kcv"), (l, "kskw"), (l, "vsvw"), (l, "gt"), (l, "cs", 0), (l, "cs", 1), (l, "hg0"), (l, "hg1"),
                     (l, "ho", 0), (l, "ho", 1), (l, "cT"), (l, "hoT", 0), (l, "hoT", 1)]
            uses += attention()
            uses += [(l, "co", 0), (l, "co", 1), (l, "oT", 1, 0), (l, "oT", 1, 1)]
        elif l == 2:
            uses += [(l, "kw")] + [(l, f"qi{j}") for j in range(4)] + [(l, "kiT")]
            for j in range(12):
                uses += [(l, projections(l)[4 + j])]
                uses += [(l, "I", i) for i in ((2 * j, 2 * j + 1) if j < 8 else ())]
            uses += attention() + [(l, "oT", a, tt) for a in range(2) for tt in range(NT)]
        else:
            uses += [(l, n) for n in projections(l)]
            uses += attention() + [(l, "oT", a, tt) for a in range(2) for tt in range(NT)]
        mid, end = norm_after(l)
        uses += [(mid, "xT", tt, q) for tt in range(NT) for q in range(2)]
        uses += [(l, "up", j) for k, j in ffn_order() if k == "up"]
        if end not in (3, 8):
            uses += [(end, "xT", tt, q) for tt in range(NT) for q in range(2)]
    return uses


def norm_after(l):
    return {0: (0, 1), 1: (2, 3), 2: (5, 6), 3: (7, 8)}[l]


def norm_rank(n):
    return n - (n > 3)


def build(nc, a):
    stream = stream_order()
    tile_no = {key: i for i, key in enumerate(stream)}
    bank_no = {key: i for i, key in enumerate(bank_order())}
    assert len(bank_no) == len(bank_order()) and len(tile_no) == len(stream)

    with ExitStack() as ctx:
        def sb(name, shape, dt=F32):
            return ctx.enter_context(nc.sbuf_tensor(name, shape, dt))

        def sem(name):
            return ctx.enter_context(nc.semaphore(name))

        bank = ctx.enter_context(nc.psum_tensor("bank", [P, 8, 512], F32))

        ring = sb("ring", [P, SLOTS, TILE])
        x = sb("x", [P, NT, D])
        res = sb("res", [P, NT, D])
        xT = sb("xT", [P, KT, S])
        oT = sb("oT", [P, KT, S])
        gains = sb("gains", [P, 2, D])
        bias_t = sb("bias_t", [P, 24, S])
        neglog = sb("neglog", [P, NT, P])
        lbuf = sb("lbuf", [P, 2, TRI])
        ebuf = sb("ebuf", [P, 2, TRI])
        pT = sb("pT", [P, 2, TRI])
        ident = sb("ident", [P, P])
        hg_mask = sb("hg_mask", [P, len(HALVES), P], U32)
        cmp_bias = sb("cmp_bias", [P, NT, 8, NC])
        cmp_off = sb("cmp_off", [P, NT, NC])
        cmp_on = sb("cmp_on", [P, NT, NC])
        head_blocks = sb("head_blocks", [P, 8])
        lb = sb("lb", [P, 2, HG_HEADS])
        lb_log = sb("lb_log", [P, 2, HG_HEADS])
        lb_tmp = sb("lb_tmp", [P, 4, HG_HEADS])
        gnorm = sb("gnorm", [P, 2, P])
        pos = sb("pos", [P, 2, 2, CMP_KT])
        w2 = sb("w2", [P, 2, 192])
        w_gate = sb("w_gate", [P, 2, KT, 24])
        w_idx = sb("w_idx", [P, KT, 80])
        idx_norm = sb("idx_norm", [P, DH])
        ln_col = sb("ln_col", [P, 3, 2, KT])
        rms_col = sb("rms_col", [P, 4, KT])
        conv_col = sb("conv_col", [P, 2, 2 * FT, 4])
        causal = sb("causal", [P, TRI])
        mxn = sb("mxn", [P, 2, NT, 8])
        esum = sb("esum", [P, 2, NT, 8])
        wgt = sb("wgt", [P, 2, NT, 8])
        stat = sb("stat", [P, 16])
        nstat = sb("nstat", [P, NT, 20])
        small = sb("small", [P, NT, 128])
        gates = sb("gates", [P, NT, 24])
        cmx = sb("cmx", [P, 3, NT * 8])
        ones = sb("ones", [P, S])
        eps_ln = sb("eps_ln", [P, 1])
        eps_rms = sb("eps_rms", [P, 1])
        arena = sb("arena", [P, ARENA])

        used = [0]

        def take(n):
            used[0] += n
            assert used[0] <= ARENA, used
            return arena[:, used[0] - n:used[0]]

        big = [take(D) for _ in range(9)]
        f_t, q_t, k_t, b_t, dec0, dec1, lev0, lev1, s_hg = big
        dec, lev = [dec0, dec1], [lev0, lev1]
        s_cross = take(512)
        v_hg = take(D).rearrange("p (t c) -> p t c", t=NT)
        g_hg = take(D).rearrange("p (t c) -> p t c", t=NT)
        nq = take(D).rearrange("p (j t) -> p j t", j=4)
        ks2 = take(512).rearrange("p (g t) -> p g t", g=2)
        kw2 = take(512).rearrange("p (g t) -> p g t", g=2)
        v_sw = take(512).rearrange("p (t c) -> p t c", t=NT)
        blk = [oT[:, 4 * i:4 * i + 4, :].rearrange("p j t -> p (j t)")[:, 0:CMP_KT * 30].rearrange(
            "p (k g n) -> p k g n", k=CMP_KT, g=2) for i in range(2)]
        o_hg = [dec[0][:, 0:512], dec[0][:, 512:1024]]
        o_sq = [dec[1][:, 0:512], dec[1][:, 512:1024]]
        hid = sb("hid", [P, 30])
        hid_v = sb("hid_v", [P, 8, NCP])
        kc2 = sb("kc2", [P, 2, NC])
        vc8 = oT[:, 4:6, :].rearrange("p j t -> p (j t)").rearrange("p (h d) -> p h d", d=DH)
        cl = res[:, 0, 0:NT * 8 * NC].rearrange("p (t h n) -> p t h n", t=NT, h=8)
        ce = res[:, 1, 0:NT * 8 * NC].rearrange("p (t h n) -> p t h n", t=NT, h=8)
        cp = sb("cp", [P, NT, 8, NCP])
        cpT = oT[:, 6, :].rearrange("p (t c) -> p t c", t=NT)
        used[0] = 0
        hT = take(FT * S).rearrange("p (j t) -> p j t", j=FT)
        gate_a = [take(S) for _ in range(2)]
        cval = [take(S) for _ in range(2)]
        cgate = [take(S) for _ in range(2)]
        used[0] = 0
        q2 = take(8 * S).rearrange("p (j t) -> p j t", j=8)
        k2 = take(8 * S).rearrange("p (j t) -> p j t", j=8)
        v2 = take(2 * D).rearrange("p (t c) -> p t c", t=NT)
        qi = take(8 * S).rearrange("p (j t) -> p j t", j=8)
        kiT = take(S)
        score = take(TRI)
        relu = [take(TRI) for _ in range(2)]
        unsel = take(TRI)
        bias_s = [take(TRI) for _ in range(2)]
        used[0] = 0
        bias_rev = take(24 * S).rearrange("p (h s) -> p h s", h=24)
        one_hot = take(REV)
        one_hot_c = take(2 * S)
        rel = take(24)
        off_row = take(REV)
        bias_row = take(REV)
        flip = take(P)
        scratch = nc.dram_tensor("bias_rows", (24, REV), F32, kind="Internal").ap()

        tile_loaded = [sem(f"tile_loaded{i}") for i in range(SLOTS)]
        rows_used = sem("rows_used")
        bank_full = sem("bank_full")
        bank_drained = [sem(f"bank_drained{i}") for i in range(RING)]
        consts_in = sem("consts_in")
        start_in = sem("start_in")
        x_in = sem("x_in")
        rows_out = sem("rows_out")
        rev_in = sem("rev_in")
        zeroed = sem("zeroed")
        lb_ready = sem("lb_ready")
        act_step = sem("act_step")
        dve_step = sem("dve_step")
        pool_step = sem("pool_step")
        bias_row_ready = sem("bias_row_ready")
        softplus_done = sem("softplus_done")
        logsig_done = sem("logsig_done")
        gap_done = sem("gap_done")
        softplus2_done = sem("softplus2_done")
        kdiff_done = sem("kdiff_done")
        k_done = sem("k_done")
        cumsum_done = sem("cumsum_done")
        diff_done = sem("diff_done")
        decay_done = sem("decay_done")
        level_done = sem("level_done")
        product_done = sem("product_done")
        picked = sem("picked")
        hid_done = sem("hid_done")
        cmp_logit = sem("cmp_logit")
        cmp_exp = sem("cmp_exp")
        cmp_prob = sem("cmp_prob")
        gate_exp = sem("gate_exp")
        g_scaled = sem("g_scaled")
        sq_done = sem("sq_done")
        ssq_done = sem("ssq_done")
        hg_rstd = sem("hg_rstd")
        hg_out = sem("hg_out")
        logit_done = sem("logit_done")
        exp_done = sem("exp_done")
        pv_done = sem("pv_done")
        mix_done = sem("mix_done")
        acc_full = sem("acc_full")
        acc_drained = sem("acc_drained")
        sum_done = sem("sum_done")
        square_done = sem("square_done")
        rstd_done = sem("rstd_done")
        normed = sem("normed")
        stream_done = sem("stream_done")
        gains_in = sem("gains_in")
        gains_used = sem("gains_used")
        act_gate = sem("act_gate")
        conv_in = sem("conv_in")
        conv_done = sem("conv_done")
        silu_done = sem("silu_done")
        h_done = sem("h_done")
        ki_sq = sem("ki_sq")
        ki_rstd = sem("ki_rstd")
        ki_normed = sem("ki_normed")
        relu_done = sem("relu_done")
        relu_used = sem("relu_used")
        unsel_done = sem("unsel_done")
        bias_sel = sem("bias_sel")
        bias_log = sem("bias_log")
        final_done = sem("final_done")
        out_sem = sem("stored")

        def bank_of(key):
            return bank[:, bank_no[key] % RING, :]

        def wait_full(eng, key):
            eng.wait_ge(bank_full, bank_no[key] + 1)

        def wait_drained(eng, key):
            eng.wait_ge(bank_drained[bank_no[key] % RING], bank_no[key] // RING + 1)

        def drained(key):
            return bank_drained[bank_no[key] % RING], 1

        def steps(eng, s):
            n = [0]

            def step(ins):
                n[0] += 1
                ins.then_inc(s, 1)
                eng.wait_ge(s, n[0])
            return step

        def bc_mid(ap, n):
            return ap.unsqueeze(1).to_broadcast([ap.shape[0], n, ap.shape[1]])

        def bc_last(ap, n):
            return ap.unsqueeze(2).to_broadcast([ap.shape[0], ap.shape[1], n])

        def heads4(ap):
            return ap.rearrange("p (h t) -> p h t", h=HG_HEADS)

        def attn_io(l, i):
            half, h = i // 8, i % 8
            if l < 2:
                g, lo = h // 4, DH * (h % 2)
                kk = (ks2, kw2)[half]
                return (half, h, nq[lo:lo + DH, h // 2, :], kk[lo:lo + DH, g, :],
                        lambda st: v_sw[:, st, half * P + g * DH:half * P + (g + 1) * DH], h, False)
            lo = DH * (i % 2)
            return (half, h, q2[lo:lo + DH, i // 2, :], k2[lo:lo + DH, i // 2, :],
                    lambda st: v2[:, st, i * DH:(i + 1) * DH], 8 + i, l == 2 and half == 1)

        LEVELS_AFTER = {"kcvc": [0, 1], "nq0": [2], "nq1": [3], "kskw": [4], "vsvw": [5], "gt": [6], "hg0": [7],
                        "hg1": [8]}
        PREP_AFTER = {"hi1": [1, 2], "kcvc": [3], "nq0": [4], "nq1": [5], "kskw": [6], "vsvw": [7], "gt": [8]}
        NLEV = len(HALVES)

        def level_banks(v):
            return bank[:, 4 + 2 * (v % 2):6 + 2 * (v % 2), :].rearrange("p b c -> p (b c)")

        def blocks(ap, half):
            return ap.rearrange("p (n w) -> p n w", w=2 * half)

        block = ctx.enter_context(nc.Block())

        @block.sync
        def _(sp):
            sp.dma_start(one_hot_c[0:BUCKETS, :], a["one_hot_c"]).then_inc(start_in, 16)
            sp.dma_start(one_hot[0:BUCKETS, :], a["one_hot"]).then_inc(start_in, 16)
            sp.dma_start(rel[0:BUCKETS, :], a["rel"]).then_inc(start_in, 16)
            sp.dma_start(off_row[0:24, :], a["off_row"]).then_inc(start_in, 16)
            sp.dma_start(ident[:, :], a["ident"]).then_inc(start_in, 16)
            sp.dma_start(flip[:, :], a["flip"]).then_inc(start_in, 16)
            sp.dma_start(cmp_off[:, :, :], a["cmp_off"]).then_inc(start_in, 16)
            sp.dma_start(xT[:, :, :], a["xT"]).then_inc(x_in, 16)

            def tile_used(key):
                l, name = key
                kind, number = name.rstrip("0123456789"), name.lstrip("abcdefghijklmnopqrstuvwxyz")
                if kind in ("out", "down"):
                    last = {"out": 3, "down": FT // 2 - 1}[kind]
                    if int(number) == last:
                        sp.wait_ge(acc_full, (2 * l + (kind == "down") + 1) * NT)
                    else:
                        sp.wait_ge(rows_used, l * (3 + FT // 2 - 1) + int(number) + 1 + 3 * (kind == "down"))
                elif kind == "up":
                    wait_full(sp, (l, "up", int(number)))
                else:
                    wait_full(sp, (l, "hid") if kind == "w" or name in ("w1k", "w1v") else key)

            def load(i):
                if i >= SLOTS:
                    tile_used(stream[i - SLOTS])
                sp.dma_start(ring[:, i % SLOTS, :], a["stream"][i]).then_inc(tile_loaded[i % SLOTS], 16)

            for i in range(4):
                load(i)
            sp.wait_ge(bias_row_ready, 1)
            sp.dma_start(scratch, bias_row[0:24, :]).then_inc(rows_out, 16)
            sp.wait_ge(rows_out, 16)
            sp.dma_start(bias_rev, bass.AP(scratch.tensor, 0, [[1, P], [REV, 24], [1, S]])).then_inc(rev_in, 16)
            sp.dma_start(x[:, :, :], a["x"]).then_inc(consts_in, 16)
            for dst, name in ((hg_mask[:, :, :], "hg_mask"), (cmp_on[:, :, :], "cmp_on"),
                              (head_blocks[:, :], "head_blocks"), (lb[:, :, :], "lb"), (pos[:, :, :, :], "pos"),
                              (w2[:, :, :], "w2"), (w_gate[:, :, :, :], "w_gate"), (w_idx[:, :, :], "w_idx"),
                              (ln_col[:, :, :, :], "ln_col"), (rms_col[:, :, :], "rms_col"),
                              (conv_col[:, :, :, :], "conv_col"), (causal[:, :], "causal"),
                              (neglog[:, :, :], "neglog"), (gnorm[:, :, :], "gnorm"), (idx_norm[:, :], "idx_norm")):
                sp.dma_start(dst, a[name]).then_inc(consts_in, 16)
            for i in range(4, len(stream)):
                load(i)
            sp.wait_ge(final_done, NT)
            sp.dma_start(a["out"], res[:, :, :]).then_inc(out_sem, 16)
            sp.wait_ge(out_sem, 16)

        CONSTS = 16 * 16

        @block.tensor
        def _(pe):
            def open_bank(key):
                n = bank_no[key]
                if n >= RING:
                    pe.wait_ge(bank_drained[n % RING], n // RING)
                return bank_of(key)

            def close_bank(ins):
                ins.then_inc(bank_full, 1)

            def weights(key):
                i = tile_no[key]
                pe.wait_ge(tile_loaded[i % SLOTS], 16 * (i // SLOTS + 1))
                return ring[:, i % SLOTS, :]

            def channel_tile(key, use=None):
                b = open_bank(use or key)
                w = weights(key).rearrange("p (k c) -> p k c", k=KT)
                for c in range(2):
                    for k in range(KT):
                        mm = pe.matmul(b[:, c * S:(c + 1) * S], w[:, k, c * P:(c + 1) * P], xT[:, k, :],
                                       start=(k == 0), stop=(k == KT - 1))
                close_bank(mm)

            def token_tile(key):
                b = open_bank(key)
                w = weights(key).rearrange("p (k c) -> p k c", k=KT)
                for tt in range(NT):
                    for k in range(KT):
                        mm = pe.matmul(b[:, tt * S:(tt + 1) * S], xT[:, k, tt * P:(tt + 1) * P], w[:, k, :],
                                       start=(k == 0), stop=(k == KT - 1))
                close_bank(mm)

            def small_tile(key, w):
                b = open_bank(key)
                n = w.shape[2]
                for tt in range(NT):
                    for k in range(KT):
                        mm = pe.matmul(b[:, tt * n:(tt + 1) * n], xT[:, k, tt * P:(tt + 1) * P], w[:, k, :],
                                       start=(k == 0), stop=(k == KT - 1))
                close_bank(mm)

            def token_major(name):
                return name[:2] in ("hi", "hg", "vs") or name[0] == "v"

            def project(l, name):
                (token_tile if token_major(name) else channel_tile)((l, name))

            def x_transposes(n):
                for tt in range(NT):
                    pe.wait_ge(normed, norm_rank(n) * NT + tt + 1)
                    for q in range(2):
                        b = open_bank((n, "xT", tt, q))
                        for i in range(4):
                            c = (4 * q + i) * P
                            mm = pe.transpose(b[:, i * P:(i + 1) * P], res[:, tt, c:c + P], ident[:, :])
                        close_bank(mm)

            def xT_ready(n):
                for tt in range(NT):
                    for q in range(2):
                        wait_drained(pe, (n, "xT", tt, q))

            def level(l, v):
                half = HALVES[v]
                if l * NLEV + v >= 2:
                    pe.wait_ge(picked, l * NLEV + v - 1)
                if v == 0:
                    if l == 1:
                        pe.wait_ge(acc_drained, 2 * NT)
                    pe.wait_ge(k_done, l + 1)
                    wait_drained(pe, (l, "hq1"))
                    lhs, rhs = k_t, q_t
                else:
                    pe.wait_ge(level_done, l * (NLEV - 1) + v)
                    lhs = rhs = lev[v % 2]
                out = level_banks(v)
                for h in range(HG_HEADS):
                    if half == P:
                        mm = pe.matmul(out[:, h * P:(h + 1) * P], lhs[:, h * S:h * S + P],
                                       rhs[:, h * S + P:(h + 1) * S], start=True, stop=True)
                        continue
                    for st in range(NT):
                        c = h * S + st * P
                        mm = pe.matmul(out[:, c:c + P], lhs[:, c:c + P], rhs[:, c:c + P], start=True, stop=True)
                mm.then_inc(product_done, 1)

            def attention(l):
                for s, t, v in attention_steps():
                    if s is not None:
                        half, h, q, k, _, _, _ = attn_io(l, s)
                        b = open_bank((l, "S", s))
                        pe.matmul(b[:, 0:S], q[:, P:S], k, start=True, stop=True)
                        close_bank(pe.matmul(b[:, S:TRI], q[:, 0:P], k[:, 0:P], start=True, stop=True))
                    if t is not None:
                        b = open_bank((l, "T", t))
                        e = ebuf[:, t % 2, :]
                        pe.wait_ge(exp_done, l * HEADS + t + 1)
                        pe.transpose(b[:, 0:P], e[:, S:TRI], ident[:, :])
                        pe.transpose(b[:, P:2 * P], e[:, 0:P], ident[:, :])
                        close_bank(pe.transpose(b[:, 2 * P:3 * P], e[:, P:2 * P], ident[:, :]))
                    if v is not None:
                        half, h, _, _, val, _, _ = attn_io(l, v)
                        wait_drained(pe, (l, "T", v))
                        if v == 0:
                            if l < 2:
                                pe.wait_ge(picked, (l + 1) * NLEV)
                            else:
                                pe.wait_ge(acc_drained, 2 * l * NT)
                        pt = pT[:, v % 2, :]
                        o0 = bank[:, 4 + 2 * half, h * DH:(h + 1) * DH]
                        o1 = bank[:, 5 + 2 * half, h * DH:(h + 1) * DH]
                        pe.matmul(o0, pt[:, 0:P], val(0), start=True, stop=True)
                        pe.matmul(o1, pt[:, P:2 * P], val(0), start=True, stop=False)
                        pe.matmul(o1, pt[:, 2 * P:3 * P], val(1), start=False, stop=True).then_inc(pv_done, 1)

            def transposes_out(l, half, tt, src):
                b = open_bank((l, "oT", half, tt))
                for i in range(4):
                    mm = pe.transpose(b[:, i * P:(i + 1) * P], src[:, i * P:(i + 1) * P], ident[:, :])
                close_bank(mm)

            def add_rows(key, lhs, first, last):
                w = weights(key).rearrange("p (k c) -> p k c", k=2)
                for tt in range(NT):
                    for kk in range(2):
                        for hf in range(2):
                            mm = pe.matmul(bank[:, 4 + 2 * tt + hf, :], lhs[:, kk, tt * P:(tt + 1) * P],
                                           w[:, kk, hf * 512:(hf + 1) * 512], start=(first and kk == 0),
                                           stop=(last and kk == 1))
                    if last:
                        mm.then_inc(acc_full, 1)
                if not last:
                    mm.then_inc(rows_used, 1)

            def output_projection(l):
                for half in range(2):
                    for tt in range(NT):
                        if (l, "oT", half, tt) in bank_no:
                            wait_drained(pe, (l, "oT", half, tt))
                        else:
                            wait_drained(pe, (l, "hoT", tt))
                pe.wait_ge(mix_done, (2 * l + 2) * NT)
                for r in range(4):
                    add_rows((l, f"out{r}"), oT[:, 2 * r:2 * r + 2, :], r == 0, r == 3)

            def feed_forward(l):
                xT_ready(norm_after(l)[0])
                for kind, j in ffn_order():
                    if kind == "up":
                        channel_tile((l, f"up{j}"), use=(l, "up", j))
                    else:
                        for i in (2 * j, 2 * j + 1):
                            if l < 2:
                                wait_drained(pe, (l, "up", i))
                            else:
                                pe.wait_ge(h_done, (l - 2) * FT + i + 1)
                        if j == 0:
                            pe.wait_ge(acc_drained, (2 * l + 1) * NT)
                        add_rows((l, f"down{j}"), hT[:, 2 * j:2 * j + 2, :], j == 0, j == FT // 2 - 1)

            pe.wait_ge(start_in, 7 * 16)
            b = open_bank(("cmpbias",))
            for tt in range(NT):
                for n in range(NC):
                    at = S - 1 + tt * P - 16 * n - 31
                    mm = pe.matmul(b[:, (tt * NC + n) * 8:(tt * NC + n + 1) * 8], one_hot_c[0:BUCKETS, at:at + P],
                                   rel[0:BUCKETS, 0:8], start=True, stop=True)
            close_bank(mm)
            b = open_bank(("biasrow",))
            close_bank(pe.matmul(b[0:24, 0:REV], rel[0:BUCKETS, 0:24], one_hot[0:BUCKETS, :], start=True, stop=True))
            pe.wait_ge(rev_in, 16)
            for c in range(12):
                b = open_bank(("bias", c))
                close_bank(pe.matmul(b, flip[:, :], bias_rev[:, 2 * c:2 * c + 2, :].rearrange("p h s -> p (h s)"),
                                     start=True, stop=True))

            for l in range(LAYERS):
                if l == 0:
                    pe.wait_ge(x_in, 16)
                    pe.wait_ge(consts_in, CONSTS)
                    pe.wait_ge(bank_drained[0], 1)
                elif l == 2:
                    x_transposes(4)
                    xT_ready(4)
                elif l == 1:
                    xT_ready(1)
                else:
                    xT_ready(6)
                if l < 2:
                    for name in ("hf0", "hf1", "hq0", "hq1", "hi0", "hi1", "kcvc"):
                        project(l, name)
                    for v in LEVELS_AFTER["kcvc"]:
                        level(l, v)
                    for name in ("nq0", "nq1"):
                        project(l, name)
                        for v in LEVELS_AFTER[name]:
                            level(l, v)
                    b = open_bank((l, "hid"))
                    wait_drained(pe, (l, "kcvc"))
                    for i, name in enumerate(("w1k", "w1v")):
                        w = weights((l, name)).rearrange("p (k c) -> p k c", k=CMP_KT)
                        for k in range(CMP_KT):
                            mm = pe.matmul(b[:, 32 * i:32 * i + 30], w[:, k, :],
                                           blk[i][:, k, :, :].rearrange("p g n -> p (g n)"),
                                           start=(k == 0), stop=(k == CMP_KT - 1))
                    close_bank(mm)
                    b = open_bank((l, "kcv"))
                    wait_drained(pe, (l, "hid"))
                    pe.matmul(b[:, 0:30], w2[:, l, 0:P], hid[:, :], start=True, stop=True)
                    close_bank(pe.matmul(b[:, DH:2 * DH], hid_v[:, :, :].rearrange("p h n -> p (h n)"),
                                         w2[:, l, P:P + DH], start=True, stop=True))
                    for name in ("kskw", "vsvw"):
                        project(l, name)
                        for v in LEVELS_AFTER[name]:
                            level(l, v)
                    small_tile((l, "gt"), w_gate[:, l, :, :])
                    for v in LEVELS_AFTER["gt"]:
                        level(l, v)
                    wait_drained(pe, (l, "kcv"))
                    wait_drained(pe, (l, "nq1"))
                    for odd in range(2):
                        b = open_bank((l, "cs", odd))
                        lo = DH * odd
                        for tt in range(NT):
                            for j in range(4):
                                c = (tt * 4 + j) * NCP
                                mm = pe.matmul(b[:, c:c + NC], nq[lo:lo + DH, j, tt * P:(tt + 1) * P],
                                               kc2[lo:lo + DH, j // 2, :], start=True, stop=True)
                        close_bank(mm)
                    for name in ("hg0", "hg1"):
                        project(l, name)
                        for v in LEVELS_AFTER[name]:
                            level(l, v)
                    for tt in range(NT):
                        b = open_bank((l, "ho", tt))
                        pe.wait_ge(picked, (l + 1) * NLEV)
                        wait_drained(pe, (l, "hi1"))
                        for h in range(HG_HEADS):
                            o = b[:, h * P:(h + 1) * P]
                            if tt == 1:
                                pe.matmul(o, s_cross[:, h * P:(h + 1) * P], v_hg[:, 0, h * P:(h + 1) * P],
                                          start=True, stop=False)
                            mm = pe.matmul(o, s_hg[:, h * S + tt * P:h * S + (tt + 1) * P],
                                           v_hg[:, tt, h * P:(h + 1) * P], start=(tt == 0), stop=True)
                        close_bank(mm)
                    b = open_bank((l, "cT"))
                    pe.wait_ge(cmp_prob, l + 1)
                    for tt in range(NT):
                        mm = pe.transpose(b[:, tt * P:(tt + 1) * P], cp[:, tt, :, :].rearrange("p h n -> p (h n)"),
                                          ident[:, :])
                    close_bank(mm)
                    for tt in range(NT):
                        b = open_bank((l, "hoT", tt))
                        pe.wait_ge(hg_out, l * NT + tt + 1)
                        for i in range(HG_HEADS):
                            mm = pe.transpose(b[:, i * P:(i + 1) * P], o_hg[tt][:, i * P:(i + 1) * P], ident[:, :])
                        close_bank(mm)
                    wait_drained(pe, (l, "vsvw"))
                    wait_drained(pe, (l, "kskw"))
                    attention(l)
                    for tt in range(NT):
                        b = open_bank((l, "co", tt))
                        wait_drained(pe, (l, "cT"))
                        close_bank(pe.matmul(b[:, :], cpT[:, tt, :], vc8[:, :, :].rearrange("p h d -> p (h d)"),
                                             start=True, stop=True))
                    for tt in range(NT):
                        pe.wait_ge(mix_done, 2 * l * NT + NT + tt + 1)
                        transposes_out(l, 1, tt, res[:, tt, 0:512])
                else:
                    if l == 2:
                        small_tile((l, "kw"), w_idx[:, :, :])
                        for j in range(4):
                            project(l, f"qi{j}")
                        b = open_bank((l, "kiT"))
                        pe.wait_ge(ki_normed, NT)
                        for tt in range(NT):
                            mm = pe.transpose(b[:, tt * P:(tt + 1) * P], small[:, tt, :], ident[:, :])
                        close_bank(mm)
                    for j, name in enumerate(projections(l)[-12:]):
                        project(l, name)
                        if l == 2 and j < 8:
                            for i in (2 * j, 2 * j + 1):
                                b = open_bank((l, "I", i))
                                lo = DH * (i % 2)
                                wait_drained(pe, (l, "kiT"))
                                wait_drained(pe, (l, f"qi{i // 4}"))
                                pe.matmul(b[:, 0:S], qi[lo:lo + DH, i // 2, P:S], kiT[lo:lo + DH, :],
                                          start=True, stop=True)
                                close_bank(pe.matmul(b[:, S:TRI], qi[lo:lo + DH, i // 2, 0:P],
                                                     kiT[lo:lo + DH, 0:P], start=True, stop=True))
                    for name in projections(l)[-12:]:
                        wait_drained(pe, (l, name))
                    attention(l)
                    for half in range(2):
                        for tt in range(NT):
                            pe.wait_ge(mix_done, (2 * l + half) * NT + tt + 1)
                            transposes_out(l, half, tt, res[:, tt, half * 512:(half + 1) * 512])
                output_projection(l)
                x_transposes(norm_after(l)[0])
                feed_forward(l)
                if norm_after(l)[1] not in (3, 8):
                    x_transposes(norm_after(l)[1])

        @block.scalar
        def _(act):
            step = steps(act, act_step)

            def copy_out(key, dst, src=None, scale=1.0):
                wait_full(act, key)
                act.activation(dst, bank_of(key) if src is None else src, ACT.Copy,
                               scale=scale).then_inc(*drained(key))

            def two(ap):
                return ap.rearrange("p (c t) -> p c t", c=2)

            def level_decay(l, v):
                n = l * (NLEV - 1) + v
                half = HALVES[v]
                act.wait_ge(diff_done, n)
                d = blocks(dec[v % 2], half)
                act.activation(d[:, :, half:], d[:, :, half:], ACT.Exp)
                act.activation(d[:, :, :half], d[:, :, :half], ACT.Exp, scale=-1.0).then_inc(decay_done, 1)

            def prep(l, name):
                for v in PREP_AFTER.get(name, ()):
                    level_decay(l, v)

            def attention(l):
                for i in range(HEADS):
                    half, h = i // 8, i % 8
                    act.wait_ge(logit_done, l * HEADS + i + 1)
                    if i >= 2:
                        wait_full(act, (l, "T", i - 2))
                    act.activation(ebuf[:, i % 2, 0:S], lbuf[:, i % 2, 0:S], ACT.Exp, scale=-1.0,
                                   bias=mxn[:, half, 1, h:h + 1], accum_out=esum[:, half, 1, h:h + 1])
                    act.activation(ebuf[:, i % 2, S:TRI], lbuf[:, i % 2, S:TRI], ACT.Exp, scale=-1.0,
                                   bias=mxn[:, half, 0, h:h + 1],
                                   accum_out=esum[:, half, 0, h:h + 1]).then_inc(exp_done, 1)

            def rstd(n):
                for tt in range(NT):
                    st = nstat[:, tt, :]
                    if n < 4:
                        act.wait_ge(sum_done, n * NT + tt + 1)
                        step(act.activation(st[:, 14:15], st[:, 13:14], ACT.Ln, bias=eps_ln[:, 0:1]))
                    else:
                        if n == 4:
                            act.wait_ge(stream_done, 3 * NT + tt + 1)
                        else:
                            act.wait_ge(acc_drained, (n - 1) * NT + tt + 1)
                        step(act.activation(res[:, tt, :], x[:, tt, :], ACT.Square, accum_out=st[:, 13:14]))
                        step(act.activation(st[:, 14:15], st[:, 13:14], ACT.Ln, scale=1.0 / D, bias=eps_rms[:, 0:1]))
                    act.activation(st[:, 15:16], st[:, 14:15], ACT.Exp, scale=-0.5).then_inc(rstd_done, 1)

            def xT_out(n):
                for tt in range(NT):
                    key = (n, "xT", tt, 0)
                    wait_full(act, key)
                    for i in range(4):
                        dst, src = xT[:, i, tt * P:(tt + 1) * P], bank_of(key)[:, i * P:(i + 1) * P]
                        if n < 4:
                            ins = act.activation(dst, src, ACT.Identity, scale=ln_col[:, n, 0, i:i + 1],
                                                 bias=ln_col[:, n, 1, i:i + 1])
                        else:
                            ins = act.activation(dst, src, ACT.Copy, scale=rms_col[:, n - 4, i:i + 1])
                    ins.then_inc(*drained(key))

            def feed_forward(l):
                for j in range(FT):
                    key = (l, "up", j)
                    wait_full(act, key)
                    b = bank_of(key)
                    if j >= 2 and l < 2:
                        wait_drained(act, (l, "up", j - 2))
                    elif j >= 2:
                        act.wait_ge(h_done, (l - 2) * FT + j - 1)
                    if l < 2:
                        act.activation(gate_a[j % 2], b[:, 0:S], ACT.Silu).then_inc(act_gate, 1)
                    else:
                        m = l - 2
                        act.activation(cval[j % 2], b[:, 0:S], ACT.Identity, scale=conv_col[:, m, j, 2:3],
                                       bias=conv_col[:, m, j, 3:4])
                        act.activation(cgate[j % 2], b[:, S:2 * S], ACT.Identity, scale=conv_col[:, m, FT + j, 2:3],
                                       bias=conv_col[:, m, FT + j, 3:4]).then_inc(conv_in, 1)
                        act.wait_ge(conv_done, m * FT + j + 1)
                        act.activation(gate_a[j % 2], cgate[j % 2], ACT.Silu).then_inc(silu_done, 1)

            act.wait_ge(zeroed, 5)
            act.wait_ge(lb_ready, 1)
            step(act.activation(lb_tmp[:, 1, :], lb_tmp[:, 0, :], ACT.Abs))
            step(act.activation(lb_tmp[:, 2, :], lb_tmp[:, 1, :], ACT.Exp, scale=-1.0))
            act.activation(lb_tmp[:, 3, :], lb_tmp[:, 2, :], ACT.Ln, bias=1.0).then_inc(lb_ready, 1)
            for c in range(12):
                copy_out(("bias", c), bias_t[:, 2 * c:2 * c + 2, :].rearrange("p h s -> p (h s)"))

            for l in range(LAYERS):
                if l < 2:
                    for i in range(2):
                        copy_out((l, f"hf{i}"), f_t[:, i * 512:(i + 1) * 512])
                    wait_drained(act, (l, "hf0"))
                    wait_drained(act, (l, "hf1"))
                    step(act.activation(dec[0], f_t, ACT.Abs))
                    step(act.activation(dec[0], dec[0], ACT.Exp, scale=-1.0))
                    act.activation(dec[0], dec[0], ACT.Ln, bias=1.0).then_inc(softplus_done, 1)
                    if l == 1:
                        act.wait_ge(gap_done, 1)
                        step(act.activation(dec[0], dec[0], ACT.Abs))
                        step(act.activation(dec[0], dec[0], ACT.Exp, scale=-1.0))
                        act.activation(dec[0], dec[0], ACT.Ln, bias=1.0).then_inc(softplus2_done, 1)
                    act.wait_ge(kdiff_done, l + 1)
                    act.activation(k_t, k_t, ACT.Exp).then_inc(k_done, 1)
                    for i in range(2):
                        copy_out((l, f"hq{i}"), q_t[:, i * 512:(i + 1) * 512])
                    for i in range(2):
                        copy_out((l, f"hi{i}"), v_hg[:, :, i * S:(i + 1) * S], two(bank_of((l, f"hi{i}"))))
                    prep(l, "hi1")
                    prep(l, "kcvc")
                    for i in range(2):
                        copy_out((l, f"nq{i}"), nq[:, 2 * i:2 * i + 2, :], two(bank_of((l, f"nq{i}"))),
                                 scale=-(DH ** -0.5))
                        prep(l, f"nq{i}")
                    key = (l, "hid")
                    wait_full(act, key)
                    act.activation(hid[:, :], bank_of(key)[:, 0:30], ACT.Gelu_apprx_tanh)
                    for g in range(2):
                        src = bank_of(key)[:, 32 + g * NC:32 + (g + 1) * NC]
                        ins = act.activation(hid_v[:, 4 * g:4 * g + 4, 0:NC], bc_mid(src, 4), ACT.Gelu_apprx_tanh)
                    ins.then_inc(*drained(key))
                    key = (l, "kskw")
                    wait_full(act, key)
                    for i, dst in enumerate((ks2, kw2)):
                        for g in range(2):
                            for lo in (0, DH):
                                ins = act.activation(dst[lo:lo + DH, g, :],
                                                     bank_of(key)[g * DH:(g + 1) * DH, i * S:(i + 1) * S], ACT.Copy)
                    ins.then_inc(*drained(key))
                    prep(l, "kskw")
                    copy_out((l, "vsvw"), v_sw[:, :, :], two(bank_of((l, "vsvw"))))
                    prep(l, "vsvw")
                    key = (l, "gt")
                    wait_full(act, key)
                    act.activation(gates[:, :, :].rearrange("p t c -> p (t c)"), bank_of(key)[:, 0:48], ACT.Exp,
                                   scale=-1.0).then_inc(*drained(key))
                    prep(l, "gt")
                    act.wait_ge(cmp_logit, l + 1)
                    act.activation(ce[:, :, :, :], cl[:, :, :, :], ACT.Exp, scale=-1.0).then_inc(cmp_exp, 1)
                    for i in range(2):
                        key = (l, f"hg{i}")
                        wait_full(act, key)
                        act.activation(g_hg[:, :, i * S:(i + 1) * S], two(bank_of(key)),
                                       ACT.Silu).then_inc(*drained(key))
                    for tt in range(NT):
                        copy_out((l, "ho", tt), o_hg[tt])
                    act.wait_ge(ssq_done, l + 1)
                    step(act.activation(stat[:, 8:16], stat[:, 0:8], ACT.Ln, scale=1.0 / P, bias=eps_rms[:, 0:1]))
                    act.activation(stat[:, 8:16], stat[:, 8:16], ACT.Exp, scale=-0.5).then_inc(hg_rstd, 1)
                    for tt in range(NT):
                        copy_out((l, "hoT", tt), oT[:, 0:4, tt * P:(tt + 1) * P],
                                 bank_of((l, "hoT", tt)).rearrange("p (i t) -> p i t", i=4))
                    attention(l)
                    for tt in range(NT):
                        copy_out((l, "oT", 1, tt), oT[:, 4:8, tt * P:(tt + 1) * P],
                                 bank_of((l, "oT", 1, tt)).rearrange("p (i t) -> p i t", i=4))
                else:
                    if l == 2:
                        rstd(4)
                        xT_out(4)
                        key = (l, "kw")
                        wait_full(act, key)
                        for tt in range(NT):
                            ins = act.activation(small[:, tt, 0:80], bank_of(key)[:, tt * 80:(tt + 1) * 80], ACT.Copy)
                        ins.then_inc(*drained(key))
                        wait_drained(act, key)
                        for tt in range(NT):
                            step(act.activation(relu[0][:, 0:DH], small[:, tt, 0:DH], ACT.Square,
                                                accum_out=stat[:, tt:tt + 1]))
                        step(act.activation(stat[:, 2:4], stat[:, 0:2], ACT.Ln, scale=1.0 / DH, bias=eps_rms[:, 0:1]))
                        act.activation(stat[:, 4:6], stat[:, 2:4], ACT.Exp, scale=-0.5).then_inc(ki_rstd, 1)
                        for j in range(4):
                            copy_out((l, f"qi{j}"), qi[:, 2 * j:2 * j + 2, :], two(bank_of((l, f"qi{j}"))))
                        copy_out((l, "kiT"), kiT, bank_of((l, "kiT"))[:, 0:S])
                    for j, name in enumerate(projections(l)[-12:]):
                        src = two(bank_of((l, name)))
                        if name[0] == "q":
                            copy_out((l, name), q2[:, 2 * j:2 * j + 2, :], src, scale=-(DH ** -0.5))
                        elif name[0] == "k":
                            copy_out((l, name), k2[:, 2 * j - 8:2 * j - 6, :], src)
                        else:
                            copy_out((l, name), v2[:, :, (j - 8) * S:(j - 7) * S], src)
                        if l == 2 and j < 8:
                            for i in (2 * j, 2 * j + 1):
                                key = (l, "I", i)
                                wait_full(act, key)
                                if i >= 2:
                                    act.wait_ge(relu_used, i - 1)
                                act.activation(relu[i % 2], bank_of(key)[:, 0:TRI], ACT.Relu,
                                               scale=DH ** -0.5).then_inc(*drained(key))
                    attention(l)
                    for half in range(2):
                        for tt in range(NT):
                            key = (l, "oT", half, tt)
                            copy_out(key, oT[:, 4 * half:4 * half + 4, tt * P:(tt + 1) * P],
                                     bank_of(key).rearrange("p (i t) -> p i t", i=4))
                mid, end = norm_after(l)
                rstd(mid)
                xT_out(mid)
                feed_forward(l)
                rstd(end)
                if end not in (3, 8):
                    xT_out(end)

        @block.vector
        def _(dve):
            step = steps(dve, dve_step)

            def level_product(l, v):
                n = l * (NLEV - 1) + v
                half = HALVES[v]
                dve.wait_ge(decay_done, n)
                if n > 2:
                    dve.wait_ge(product_done, l * NLEV + v - 1 if v > 2 else l * NLEV)
                d, o = blocks(dec[v % 2], half), blocks(lev[v % 2], half)
                dve.tensor_tensor(o[:, :, :half], d[:, :, :half], blocks(k_t, half)[:, :, :half], ALU.mult)
                dve.tensor_tensor(o[:, :, half:], d[:, :, half:], blocks(q_t, half)[:, :, half:],
                                  ALU.mult).then_inc(level_done, 1)

            def pick(l, v):
                dve.wait_ge(product_done, l * NLEV + v + 1)
                if v > 0:
                    dve.wait_ge(picked, l * NLEV + v)
                src = level_banks(v)
                if HALVES[v] == P:
                    dve.tensor_copy(s_cross, src[:, 0:512]).then_inc(picked, 1)
                else:
                    dve.copy_predicated(s_hg.rearrange("p (n t) -> p n t", t=P), bc_mid(hg_mask[:, v, :], 8),
                                        src.rearrange("p (n t) -> p n t", t=P)).then_inc(picked, 1)

            def after(l, name):
                for v in LEVELS_AFTER.get(name, ()):
                    pick(l, v)
                for v in PREP_AFTER.get(name, ()):
                    level_product(l, v)

            def attention(l):
                for s, t, _ in attention_steps():
                    if s is not None:
                        half, h, _, _, _, bh, indexed = attn_io(l, s)
                        key = (l, "S", s)
                        wait_full(dve, key)
                        if s >= 2:
                            dve.wait_ge(exp_done, l * HEADS + s - 1)
                        b, o = bank_of(key), lbuf[:, s % 2, :]
                        if l == 3 and s == 0:
                            dve.wait_ge(bias_log, 1)
                        if indexed:
                            dve.wait_ge(bias_sel, h + 1)
                            b1, b0 = bias_s[h % 2][:, 0:S], bias_s[h % 2][:, S:TRI]
                        else:
                            b1, b0 = bias_t[:, bh, :], bias_t[:, bh, P:S]
                        dve.tensor_tensor_reduce(o[:, 0:S], b[:, 0:S], b1, 1.0, 3e38, ALU.add, ALU.min,
                                                 mxn[:, half, 1, h:h + 1])
                        step(dve.tensor_tensor_reduce(o[:, S:TRI], b[:, S:TRI], b0, 1.0, 3e38, ALU.add, ALU.min,
                                                      mxn[:, half, 0, h:h + 1]))
                        dve.nop().then_inc(logit_done, 1)
                        dve.nop().then_inc(*drained(key))
                    if t is not None:
                        key = (l, "T", t)
                        wait_full(dve, key)
                        if t >= 2:
                            dve.wait_ge(pv_done, l * HEADS + t - 1)
                        dve.tensor_copy(pT[:, t % 2, :], bank_of(key)[:, 0:TRI]).then_inc(*drained(key))

            def res_tile(tt, half):
                return res[:, tt, half * 512:(half + 1) * 512].rearrange("p (h d) -> p h d", d=DH)

            def norm(n, l=None, second=False):
                for tt in range(NT):
                    st = nstat[:, tt, :]
                    if n != 4:
                        dve.wait_ge(acc_full, (2 * l + second) * NT + tt + 1)
                        acc = bank[:, 4 + 2 * tt:6 + 2 * tt, :].rearrange("p b c -> p (b c)")
                    if n < 4:
                        if n > 0:
                            dve.wait_ge(stream_done, (n - 1) * NT + tt + 1)
                        dve.scalar_tensor_tensor(res[:, tt, :], x[:, tt, :], ALPHA, acc, ALU.mult,
                                                 ALU.add).then_inc(acc_drained, 1)
                        dve.wait_ge(acc_drained, n * NT + tt + 1)
                        for i in range(2):
                            ins = dve.bn_stats(st[:, 6 * i:6 * i + 6], res[:, tt, i * 512:(i + 1) * 512])
                        step(ins)
                        dve.bn_aggr(st[:, 12:14], st[:, 0:12]).then_inc(sum_done, 1)
                    elif n > 4:
                        dve.tensor_tensor(x[:, tt, :], x[:, tt, :], acc, ALU.add).then_inc(acc_drained, 1)
                for tt in range(NT):
                    st = nstat[:, tt, :]
                    dve.wait_ge(rstd_done, n * NT + tt + 1)
                    if n < 4:
                        ins = dve.tensor_scalar(res[:, tt, :], res[:, tt, :], st[:, 12:13], st[:, 15:16],
                                                ALU.subtract, ALU.mult)
                        if n < 3:
                            ins.then_inc(normed, 1)
                        else:
                            step(ins)
                            dve.wait_ge(gains_in, 2 * 16 * (n + 1))
                            step(dve.tensor_tensor(x[:, tt, :], res[:, tt, :], gains[:, 0, :], ALU.mult))
                            dve.tensor_tensor(x[:, tt, :], x[:, tt, :], gains[:, 1, :], ALU.add).then_inc(stream_done, 1)
                    elif n < 8:
                        dve.tensor_scalar(res[:, tt, :], x[:, tt, :], st[:, 15:16], None,
                                          ALU.mult).then_inc(normed, 1)
                    else:
                        dve.wait_ge(gains_in, 16 * 9)
                        dve.scalar_tensor_tensor(res[:, tt, :], x[:, tt, :], st[:, 15:16], gains[:, 0, :], ALU.mult,
                                                 ALU.mult).then_inc(final_done, 1)

            def xT_out(n):
                for tt in range(NT):
                    key = (n, "xT", tt, 1)
                    wait_full(dve, key)
                    for i in range(4):
                        dst, src = xT[:, 4 + i, tt * P:(tt + 1) * P], bank_of(key)[:, i * P:(i + 1) * P]
                        if n < 4:
                            ins = dve.tensor_scalar(dst, src, ln_col[:, n, 0, 4 + i:5 + i], ln_col[:, n, 1, 4 + i:5 + i],
                                                    ALU.mult, ALU.add)
                        else:
                            ins = dve.tensor_scalar(dst, src, rms_col[:, n - 4, 4 + i:5 + i], None, ALU.mult)
                    ins.then_inc(*drained(key))

            def feed_forward(l):
                for j in range(FT):
                    key = (l, "up", j)
                    b = bank_of(key)
                    if l < 2:
                        dve.wait_ge(act_gate, l * FT + j + 1)
                        dve.tensor_tensor(hT[:, j, :], gate_a[j % 2], b[:, S:2 * S],
                                          ALU.mult).then_inc(*drained(key))
                    else:
                        m = l - 2
                        dve.wait_ge(conv_in, m * FT + j + 1)
                        for tap in (1, 0):
                            lag = 2 - tap
                            for i, c in enumerate((cval[j % 2], cgate[j % 2])):
                                ins = dve.scalar_tensor_tensor(
                                    c[:, lag:], b[:, i * S:(i + 1) * S - lag],
                                    conv_col[:, m, i * FT + j, tap:tap + 1], c[:, lag:], ALU.mult, ALU.add)
                            if tap == 1:
                                step(ins)
                        ins.then_inc(conv_done, 1)
                        dve.wait_ge(conv_done, m * FT + j + 1)
                        dve.nop().then_inc(*drained(key))
                        dve.wait_ge(silu_done, m * FT + j + 1)
                        dve.tensor_tensor(hT[:, j, :], gate_a[j % 2], cval[j % 2], ALU.mult).then_inc(h_done, 1)

            key = ("cmpbias",)
            wait_full(dve, key)
            dve.wait_ge(start_in, 7 * 16)
            for tt in range(NT):
                src = bank_of(key)[:, tt * NC * 8:(tt + 1) * NC * 8].rearrange("p (n h) -> p h n", h=8)
                ins = dve.tensor_tensor(cmp_bias[:, tt, :, :], src, bc_mid(cmp_off[:, tt, :], 8), ALU.add)
            ins.then_inc(*drained(key))
            key = ("biasrow",)
            wait_full(dve, key)
            step(dve.tensor_tensor(bias_row[0:24, :], bank_of(key)[0:24, 0:REV], off_row[0:24, :], ALU.add))
            dve.nop().then_inc(bias_row_ready, 1)
            dve.nop().then_inc(*drained(key))
            dve.wait_ge(consts_in, CONSTS)
            dve.tensor_tensor(lb_tmp[:, 0, :], lb[:, 1, :], lb[:, 0, :], ALU.subtract).then_inc(lb_ready, 1)
            dve.wait_ge(lb_ready, 2)
            step(dve.scalar_tensor_tensor(lb_log[:, 0, :], lb_tmp[:, 0, :], 0.0, lb_tmp[:, 3, :], ALU.min,
                                          ALU.subtract))
            step(dve.tensor_tensor(lb_log[:, 1, :], lb_log[:, 0, :], lb_tmp[:, 0, :], ALU.subtract))

            for l in range(LAYERS):
                if l < 2:
                    dve.wait_ge(softplus_done, l + 1)
                    step(dve.scalar_tensor_tensor(b_t, f_t, 0.0, dec[0], ALU.min, ALU.subtract))
                    if l == 1:
                        step(dve.tensor_tensor(heads4(b_t), heads4(b_t), bc_last(lb_log[:, 1, :], S), ALU.add))
                        dve.tensor_tensor(heads4(dec[0]), heads4(b_t), bc_last(lb_log[:, 0, :], S),
                                          ALU.subtract).then_inc(gap_done, 1)
                    dve.tensor_tensor(k_t, b_t, f_t, ALU.subtract).then_inc(kdiff_done, 1)
                    if l == 1:
                        dve.wait_ge(kdiff_done, l + 1)
                        dve.wait_ge(softplus2_done, 1)
                        step(dve.tensor_tensor(heads4(b_t), heads4(b_t), bc_last(lb_log[:, 0, :], S), ALU.max))
                        step(dve.tensor_tensor(b_t, b_t, dec[0], ALU.add))
                    else:
                        dve.wait_ge(kdiff_done, l + 1)
                    dve.wait_ge(zeroed, 5)
                    for h in range(HG_HEADS):
                        ins = dve.tensor_tensor_scan(f_t[:, h * S:(h + 1) * S], ones[:, :], b_t[:, h * S:(h + 1) * S],
                                                     0.0, ALU.mult, ALU.add)
                    ins.then_inc(cumsum_done, 1)
                    dve.wait_ge(k_done, l + 1)
                    wait_drained(dve, (l, "hq0"))
                    wait_drained(dve, (l, "hq1"))
                    after(l, "hi1")
                    key = (l, "kcvc")
                    wait_full(dve, key)
                    for i in range(2):
                        for g in range(2):
                            for par in range(2):
                                at = i * S + par
                                full = bank_of(key)
                                base = full[g * DH:(g + 1) * DH, at:at + 1]
                                src = bass.AP(base.tensor, base.offset,
                                              [list(base.ap[0]), [2, CMP_KT], [16, NC]])
                                lo = par * DH
                                ins = dve.tensor_tensor(blk[i][lo:lo + DH, :, g, :], src,
                                                        bc_last(pos[lo:lo + DH, l, i, :], NC), ALU.add)
                    ins.then_inc(*drained(key))
                    after(l, "kcvc")
                    after(l, "nq0")
                    after(l, "nq1")
                    key = (l, "kcv")
                    wait_full(dve, key)
                    dve.tensor_copy(kc2[:, :, :].rearrange("p g n -> p (g n)"), bank_of(key)[:, 0:30])
                    dve.tensor_tensor(vc8[:, :, :], bc_mid(bank_of(key)[:, DH:2 * DH], 8),
                                      bc_last(head_blocks[:, :], DH), ALU.mult).then_inc(*drained(key))
                    after(l, "kskw")
                    after(l, "vsvw")
                    wait_drained(dve, (l, "gt"))
                    gf = gates[:, :, :].rearrange("p t c -> p (t c)")
                    step(dve.tensor_scalar(gf, gf, 1.0, None, ALU.add))
                    step(dve.reciprocal(gf, gf))
                    after(l, "gt")
                    for odd in range(2):
                        key = (l, "cs", odd)
                        wait_full(dve, key)
                        src = bank_of(key)[:, 0:P].rearrange("p (t j n) -> p t j n", t=NT, j=4)[:, :, :, 0:NC]
                        for tt in range(NT):
                            ins = dve.tensor_tensor(cl[:, tt, odd::2, :], src[:, tt, :, :],
                                                    cmp_bias[:, tt, odd::2, :], ALU.add)
                        ins.then_inc(*drained(key))
                    wait_drained(dve, key)
                    c3 = cl[:, :, :, :].rearrange("p t h n -> p (t h) n")
                    e3 = ce[:, :, :, :].rearrange("p t h n -> p (t h) n")
                    step(dve.tensor_reduce(cmx[:, 0, :], c3, AX_X, ALU.min))
                    dve.tensor_tensor(c3, c3, bc_last(cmx[:, 0, :], NC), ALU.subtract).then_inc(cmp_logit, 1)
                    dve.wait_ge(cmp_exp, l + 1)
                    step(dve.tensor_reduce(cmx[:, 1, :], e3, AX_X, ALU.add))
                    step(dve.reciprocal(cmx[:, 1, :], cmx[:, 1, :]))
                    for tt in range(NT):
                        ins = dve.tensor_tensor(cmx[:, 2, 8 * tt:8 * tt + 8], cmx[:, 1, 8 * tt:8 * tt + 8],
                                                gates[:, tt, 0:8], ALU.mult)
                    step(ins)
                    step(dve.tensor_tensor(e3, e3, bc_last(cmx[:, 2, :], NC), ALU.mult))
                    for tt in range(NT):
                        ins = dve.tensor_tensor(cp[:, tt, :, 0:NC], ce[:, tt, :, :], bc_mid(cmp_on[:, tt, :], 8),
                                                ALU.mult)
                    ins.then_inc(cmp_prob, 1)
                    after(l, "hg0")
                    after(l, "hg1")
                    for tt in range(NT):
                        dve.wait_ge(sq_done, l * NT + tt + 1)
                        ins = dve.tensor_reduce(stat[:, 4 * tt:4 * tt + 4],
                                                o_sq[tt].rearrange("p (h v) -> p h v", h=HG_HEADS), AX_X, ALU.add)
                    ins.then_inc(ssq_done, 1)
                    key = (l, "cT")
                    wait_full(dve, key)
                    dve.tensor_copy(cpT[:, :, :].rearrange("p t c -> p (t c)"),
                                    bank_of(key)[:, 0:2 * P]).then_inc(*drained(key))
                    dve.wait_ge(hg_rstd, l + 1)
                    dve.wait_ge(g_scaled, l + 1)
                    for tt in range(NT):
                        o3 = o_hg[tt].rearrange("p (h v) -> p h v", h=HG_HEADS)
                        step(dve.tensor_tensor(o3, o3, bc_last(stat[:, 8 + 4 * tt:12 + 4 * tt], P), ALU.mult))
                        dve.tensor_tensor(o_hg[tt], o_hg[tt], g_hg[:, tt, :], ALU.mult).then_inc(hg_out, 1)
                    attention(l)
                    dve.wait_ge(exp_done, (l + 1) * HEADS)
                    sums = esum[:, :, :, :].rearrange("p a t h -> p (a t h)")
                    wf = wgt[:, :, :, :].rearrange("p a t h -> p (a t h)")
                    step(dve.reciprocal(wf, sums))
                    for half in range(2):
                        ins = dve.tensor_tensor(wgt[:, half, :, :], wgt[:, half, :, :],
                                                gates[:, :, 8 + 8 * half:16 + 8 * half], ALU.mult)
                    step(ins)
                    dve.wait_ge(pv_done, (l + 1) * HEADS)
                    for tt in range(NT):
                        for half in range(2):
                            ps = bank[:, 4 + 2 * half + tt, :].rearrange("p (h d) -> p h d", d=DH)
                            ins = dve.tensor_tensor(res_tile(tt, half), ps, bc_last(wgt[:, half, tt, :], DH), ALU.mult)
                            ins.then_inc(mix_done, 1) if half == 0 else step(ins)
                        dve.wait_ge(mix_done, 2 * l * NT + tt + 1)
                    for tt in range(NT):
                        step(dve.tensor_tensor(res[:, tt, 0:512], res[:, tt, 0:512], res[:, tt, 512:1024], ALU.add))
                        key = (l, "co", tt)
                        wait_full(dve, key)
                        step(dve.tensor_tensor(res[:, tt, 0:512], res[:, tt, 0:512], bank_of(key), ALU.add))
                        dve.nop().then_inc(*drained(key))
                        dve.nop().then_inc(mix_done, 1)
                else:
                    if l == 2:
                        norm(4)
                        xT_out(4)
                        dve.wait_ge(ki_rstd, 1)
                        for tt in range(NT):
                            step(dve.tensor_scalar(gates[:, tt, 0:16], small[:, tt, DH:80], 16.0 ** -0.5, None, ALU.mult))
                            step(dve.scalar_tensor_tensor(small[:, tt, 0:DH], small[:, tt, 0:DH],
                                                          stat[:, 4 + tt:5 + tt], idx_norm[:, :], ALU.mult, ALU.mult))
                            dve.tensor_copy(small[:, tt, DH:2 * DH], small[:, tt, 0:DH]).then_inc(ki_normed, 1)
                        step(dve.tensor_copy(score, causal[:, :]))
                        for i in range(16):
                            wait_drained(dve, (l, "I", i))
                            if i > 0:
                                dve.wait_ge(relu_used, i)
                            r = relu[i % 2]
                            dve.scalar_tensor_tensor(score[:, 0:S], r[:, 0:S], gates[:, 1, i:i + 1], score[:, 0:S],
                                                     ALU.mult, ALU.add)
                            dve.scalar_tensor_tensor(score[:, S:TRI], r[:, S:TRI], gates[:, 0, i:i + 1],
                                                     score[:, S:TRI], ALU.mult, ALU.add).then_inc(relu_used, 1)
                        dve.wait_ge(relu_used, 16)
                        for part in (score[:, 0:S], score[:, S:TRI]):
                            for _ in range(TOPK // 8):
                                step(dve.max(stat[:, 8:16], part))
                                step(dve.match_replace(part, stat[:, 8:16], part, TAKEN))
                        dve.tensor_scalar(unsel, score, 1.5 * NEG, -NEG, ALU.is_gt, ALU.mult).then_inc(unsel_done, 1)
                    attention(l)
                    dve.wait_ge(exp_done, (l + 1) * HEADS)
                    step(dve.reciprocal(wgt[:, :, :, :].rearrange("p a t h -> p (a t h)"),
                                        esum[:, :, :, :].rearrange("p a t h -> p (a t h)")))
                    dve.wait_ge(pv_done, (l + 1) * HEADS)
                    for half in range(2):
                        for tt in range(NT):
                            ps = bank[:, 4 + 2 * half + tt, :].rearrange("p (h d) -> p h d", d=DH)
                            dve.tensor_tensor(res_tile(tt, half), ps, bc_last(wgt[:, half, tt, :], DH),
                                              ALU.mult).then_inc(mix_done, 1)
                mid, end = norm_after(l)
                norm(mid, l)
                xT_out(mid)
                feed_forward(l)
                norm(end, l, second=True)
                if end not in (3, 8):
                    xT_out(end)

        @block.gpsimd
        def _(pool):
            step = steps(pool, pool_step)
            pool.memset(s_hg, 0.0).then_inc(zeroed, 1)
            pool.memset(hid_v[:, :, :], 0.0).then_inc(zeroed, 1)
            pool.memset(cp[:, :, :, :], 0.0).then_inc(zeroed, 1)
            pool.memset(ones[:, :], 1.0).then_inc(zeroed, 1)
            pool.memset(eps_ln[:, :], 1e-5)
            pool.memset(eps_rms[:, :], 1e-6).then_inc(zeroed, 1)

            def load_gains(g, b):
                pool.dma_start(gains[:, 0, :], g.partition_broadcast(P)).then_inc(gains_in, 16)
                if b is not None:
                    pool.dma_start(gains[:, 1, :], b.partition_broadcast(P)).then_inc(gains_in, 16)

            def rescale(n):
                pool.wait_ge(gains_in, 2 * 16 * (n + 1))
                for tt in range(NT):
                    pool.wait_ge(normed, norm_rank(n) * NT + tt + 1)
                    step(pool.tensor_tensor(x[:, tt, :], res[:, tt, :], gains[:, 0, :], ALU.mult))
                    pool.tensor_tensor(x[:, tt, :], x[:, tt, :], gains[:, 1, :], ALU.add).then_inc(stream_done, 1)
                pool.wait_ge(stream_done, (n + 1) * NT)

            load_gains(a["ln1_g"][0], a["ln1_b"][0])
            for l in range(2):
                pool.wait_ge(cumsum_done, l + 1)
                for v in range(1, NLEV):
                    n = l * (NLEV - 1) + v
                    half = HALVES[v]
                    if v > 2:
                        pool.wait_ge(level_done, n - 2)
                    src = blocks(f_t, half)
                    mid = src[:, :, half - 1:half].to_broadcast([P, D // (2 * half), 2 * half])
                    pool.tensor_tensor(blocks(dec[v % 2], half), src, mid, ALU.subtract).then_inc(diff_done, 1)
                for i in range(2):
                    wait_drained(pool, (l, f"hg{i}"))
                for tt in range(NT):
                    g3 = g_hg[:, tt, :].rearrange("p (h v) -> p h v", h=HG_HEADS)
                    ins = pool.tensor_tensor(g3, g3, bc_mid(gnorm[:, l, :], HG_HEADS), ALU.mult)
                ins.then_inc(g_scaled, 1)
                for tt in range(NT):
                    wait_drained(pool, (l, "ho", tt))
                    pool.tensor_tensor(o_sq[tt], o_hg[tt], o_hg[tt], ALU.mult).then_inc(sq_done, 1)
                rescale(2 * l)
                load_gains(a["ln2_g"][l], a["ln2_b"][l])
                if l == 0:
                    rescale(1)
                    load_gains(a["ln1_g"][1], a["ln1_b"][1])
            pool.wait_ge(unsel_done, 1)
            for h in range(8):
                if h >= 2:
                    pool.wait_ge(logit_done, 2 * HEADS + 8 + h - 1)
                o = bias_s[h % 2]
                pool.tensor_tensor(o[:, 0:S], bias_t[:, 16 + h, :], unsel[:, 0:S], ALU.add)
                pool.tensor_tensor(o[:, S:TRI], bias_t[:, 16 + h, P:S], unsel[:, S:TRI],
                                   ALU.add).then_inc(bias_sel, 1)
            pool.wait_ge(logit_done, 3 * HEADS)
            pool.wait_ge(consts_in, CONSTS)
            for h in range(16):
                ins = pool.tensor_tensor(bias_t[:, 8 + h, :], bias_t[:, 8 + h, :],
                                         neglog[:, :, :].rearrange("p t s -> p (t s)"), ALU.add)
            ins.then_inc(bias_log, 1)
            pool.wait_ge(stream_done, 4 * NT)
            load_gains(a["final_g"], None)


def bucket(dist):
    n = np.maximum(dist, 0)
    exact = BUCKETS // 2
    nf = np.maximum(n, 1).astype(np.float32)
    large = exact + (np.log(nf / np.float32(exact)) / np.float32(np.log(128 / exact))
                     * np.float32(BUCKETS - exact)).astype(np.int32)
    return np.where(n < exact, n, np.minimum(large, BUCKETS - 1))


def constants():
    f = np.float32
    p = np.arange(P)
    rev = S - 1 - np.arange(REV)
    one_hot = -((bucket(rev)[None, :] == np.arange(BUCKETS)[:, None]) & (rev >= 0)).astype(f)
    dc = np.arange(2 * S) - (S - 1)
    one_hot_c = -((bucket(dc)[None, :] == np.arange(BUCKETS)[:, None]) & (dc >= 0)).astype(f)
    off_row = np.broadcast_to(np.where(rev >= 0, 0.0, -NEG).astype(f), (24, REV)).copy()
    masks = np.zeros((P, len(HALVES), P), np.uint32)
    for v, half in enumerate(HALVES):
        if half == 0:
            masks[:, v, :] = np.eye(P, dtype=np.uint32)
        elif half < P:
            same = (p[:, None] // (2 * half)) == (p[None, :] // (2 * half))
            masks[:, v, :] = same & (p[:, None] % (2 * half) < half) & (p[None, :] % (2 * half) >= half)
    t = np.arange(S).reshape(NT, P).T
    done = (np.arange(NC) * 16 + 31)[None, None, :] <= t[:, :, None]
    s = np.arange(S)
    causal = np.concatenate([np.where(s[None, :] <= P + p[:, None], 0.0, NEG),
                             np.where(s[None, :P] <= p[:, None], 0.0, NEG)], axis=1)
    dist = P + p[:, None] - s[None, :]
    count = ((dist >= 0) & (dist <= P)).astype(int) + ((dist >= 0) & (dist % 4 == 0)) + ((dist >= 0) & (dist % 16 == 0))
    log_count = np.where(count > 0, -np.log(np.maximum(count, 1)), -NEG)
    return {
        "one_hot": one_hot, "one_hot_c": one_hot_c, "off_row": off_row, "ident": np.eye(P, dtype=f),
        "flip": np.eye(P, dtype=f)[::-1].copy(), "hg_mask": masks,
        "cmp_off": np.where(done, 0.0, -NEG).astype(f), "cmp_on": done.astype(f),
        "head_blocks": (p[:, None] // NCP == np.arange(8)[None, :]).astype(f),
        "causal": causal.astype(f), "neglog": log_count.astype(f).reshape(P, NT, P),
    }


def col_tile(w):
    return w.reshape(KT, P, S).transpose(1, 0, 2).reshape(P, TILE)


def row_tile(w):
    return w.reshape(2, P, D).transpose(1, 0, 2).reshape(P, TILE)


def layout(i):
    cols = {}
    for l in range(2):
        w = i["w_in"][l]
        at = dict(zip(("hq", "hf", "hi", "hg", "nq", "kc", "vc", "ks", "vs", "kw", "vw", "gt"),
                      (0, 512, 1024, 1536, 2048, 2560, 2688, 2816, 2944, 3072, 3200, 3328)))
        for n in ("hq", "hf", "hi", "hg", "nq"):
            for j in range(2):
                cols[(l, f"{n}{j}")] = col_tile(w[:, at[n] + S * j:at[n] + S * (j + 1)])
        for n in ("kcvc", "kskw", "vsvw"):
            cols[(l, n)] = col_tile(np.concatenate([w[:, at[n[:2]]:at[n[:2]] + P], w[:, at[n[2:]]:at[n[2:]] + P]], 1))
        for n, src in (("w1k", "cmp_w1_k"), ("w1v", "cmp_w1_v")):
            cols[(l, n)] = i[src][l].reshape(CMP_KT, P, P).transpose(1, 0, 2).reshape(P, TILE)
        for j in range(FT):
            c = slice(j * P, (j + 1) * P)
            cols[(l, f"up{j}")] = col_tile(np.concatenate([i["w_ffn_gate"][l][:, c], i["w_ffn_up"][l][:, c]], 1))
        for r in range(4):
            cols[(l, f"out{r}")] = row_tile(i["w_out"][l][r * S:(r + 1) * S])
        for r in range(FT // 2):
            cols[(l, f"down{r}")] = row_tile(i["w_ffn_down"][l][r * S:(r + 1) * S])
    e, o = i["w_in_even_2"][0], i["w_in_odd_2"][0]
    for l, w, starts in ((2, e, {"q": (0, 1536), "k": (512, 2048), "v": (1024, 2560)}),
                         (3, o, {"q": (0, 512), "k": (1024, 1536), "v": (2048, 2560)})):
        for n, (a, b) in starts.items():
            for j in range(4):
                c = (a, b)[j // 2] + S * (j % 2)
                cols[(l, f"{n}{j}")] = col_tile(w[:, c:c + S])
        for j in range(FT):
            v = i["w_up_2"][l - 2]
            cols[(l, f"up{j}")] = col_tile(np.concatenate([v[:, j * P:(j + 1) * P],
                                                           v[:, DFF + j * P:DFF + (j + 1) * P]], 1))
        for r in range(4):
            cols[(l, f"out{r}")] = row_tile(i["w_o_2"][l - 2][r * S:(r + 1) * S])
        for r in range(FT // 2):
            cols[(l, f"down{r}")] = row_tile(i["w_down_2"][l - 2][r * S:(r + 1) * S])
    for j in range(4):
        cols[(2, f"qi{j}")] = col_tile(e[:, 3072 + S * j:3072 + S * (j + 1)])

    def by_channel(v):
        return np.ascontiguousarray(np.moveaxis(v.reshape(v.shape[:-1] + (KT, P)), -1, 0))

    x = i["x"][0]
    taps = np.concatenate([i["conv_w_2"], i["conv_b_2"][:, None, :]], 1)
    w2k, w2v = i["cmp_w2_k"], i["cmp_w2_v"]
    p2 = np.stack([i["cmp_pos_k"], i["cmp_pos_v"]], 1)
    d = {
        "stream": np.stack([cols[k] for k in stream_order()]),
        "xT": x.T.reshape(KT, P, S).transpose(1, 0, 2), "x": x.reshape(NT, P, D).transpose(1, 0, 2),
        "rel": np.concatenate([i["rel_bias"], i["rel_bias_2"]], 1),
        "lb": i["hg_lb_param"].reshape(2, HG_HEADS, P).transpose(2, 0, 1),
        "gnorm": np.broadcast_to(i["hg_norm_w"][None], (P, 2, P)),
        "idx_norm": np.broadcast_to(i["idx_k_norm_2"], (P, DH)),
        "pos": p2.reshape(2, 2, CMP_KT, 2, DH).transpose(3, 4, 0, 1, 2).reshape(P, 2, 2, CMP_KT),
        "w2": np.concatenate([w2k, w2k, w2v], 2).transpose(1, 0, 2),
        "w_gate": i["w_in"][:, :, 3328:3352].reshape(2, KT, P, 24).transpose(2, 0, 1, 3),
        "w_idx": e[:, 4096:4176].reshape(KT, P, 80).transpose(1, 0, 2),
        "ln_col": by_channel(np.stack([np.stack([i["ln1_g"][0], i["ln1_b"][0]]), np.stack([i["ln2_g"][0], i["ln2_b"][0]]),
                                       np.stack([i["ln1_g"][1], i["ln1_b"][1]])])),
        "rms_col": by_channel(np.stack([i["attn_norm_2"][0], i["ffn_norm_2"][0], i["attn_norm_2"][1],
                                        i["ffn_norm_2"][1]])),
        "conv_col": taps.reshape(2, 4, 2 * FT, P).transpose(3, 0, 2, 1),
        "ln1_g": i["ln1_g"], "ln1_b": i["ln1_b"], "ln2_g": i["ln2_g"], "ln2_b": i["ln2_b"],
        "final_g": i["final_norm_2"],
    }
    d.update(constants())
    return {k: np.ascontiguousarray(v) for k, v in d.items()}


def kernel(**inputs):
    import concourse.bacc as bacc
    from concourse.bass_utils import run_bass_kernel_spmd

    arrays = layout({k: np.asarray(v) for k, v in inputs.items()})
    nc = bacc.Bacc("TRN2", target_bir_lowering=False, num_devices=1)
    args = {k: nc.dram_tensor(f"in_{k}", v.shape, mybir.dt.from_np(v.dtype), kind="ExternalInput").ap()
            for k, v in arrays.items()}
    args["out"] = nc.dram_tensor("out", (P, NT, D), F32, kind="ExternalOutput").ap()
    build(nc, args)
    r = run_bass_kernel_spmd(nc, [{f"in_{k}": v for k, v in arrays.items()}], core_ids=[0])
    return r.results[0]["out"].transpose(1, 0, 2).reshape(1, S, D)
```

```python
from contextlib import ExitStack

import numpy as np
import concourse.bass as bass
from concourse import mybir

ALU = mybir.AluOpType
ACT = mybir.ActivationFunctionType
AX_X = mybir.AxisListType.X
F32 = mybir.dt.float32
F32R = mybir.dt.float32r
U8 = mybir.dt.uint8

P = 128
S = 256
NT = S // P
D = 1024
KT = D // P
DFF = 2816
FT = DFF // P
LAYERS = 4
TILE = 2048
SLOTS = 3
PARTS = 3
HSLOTS = 6
RING = 4
ALPHA = 4.0 ** 0.25
HG_HEADS = 4
HEADS = 16
DH = 64
NC = 15
NCP = 16
CMP_KT = 16
NEG = -1e30
TAKEN = -2e30
TOPK = 64
ARENA = 12288
BUCKETS = 32
REV = S + P - 1
HALVES = [0, 128, 64, 32, 16, 8, 4, 2, 1]
TRI = S + P


def projections(l):
    if l < 2:
        return ["hf0", "hf1", "hq0", "hq1", "hi0", "hi1", "kcvc", "nq0", "nq1", "w1k", "w1v", "kskw", "vsvw",
                "hg0", "hg1"]
    if l == 2:
        return ([f"qi{j}" for j in range(4)] + [f"q{j}" for j in range(4)] + [f"k{j}" for j in range(4)]
                + [f"v{j}" for j in range(4)])
    return [f"q{j}" for j in range(4)] + [f"k{j}" for j in range(4)] + [f"v{j}" for j in range(4)]


def ffn_order():
    order = []
    for r in range(FT // 2):
        order += [("up", 2 * r), ("up", 2 * r + 1)]
        if r >= 1:
            order.append(("down", r - 1))
    order.append(("down", FT // 2 - 1))
    return order


def stream_order():
    order = []
    for l in range(LAYERS):
        order += [(l, name) for name in projections(l)]
        order += [(l, f"out{r}") for r in range(4)]
        order += [(l, f"{kind}{j}") for kind, j in ffn_order()]
    return order


def attention_steps():
    for i in range(HEADS + 2):
        yield (i if i < HEADS else None, i - 1 if 0 <= i - 1 < HEADS else None, i - 2 if i >= 2 else None)


def bank_order():
    uses = [("cmpbias",), ("biasrow",)] + [("bias", c) for c in range(12)]
    for l in range(LAYERS):
        if l == 2:
            uses += [(4, "xT", tt, q) for tt in range(NT) for q in range(2)]
        def attention():
            out = []
            for s, t, _ in attention_steps():
                out += [(l, "S", s)] if s is not None else []
                out += [(l, "T", t)] if t is not None else []
            return out
        if l < 2:
            names = projections(l)
            for n in names[:names.index("w1k")]:
                uses.append((l, n))
            uses += [(l, "hid"), (l, "kcv"), (l, "kskw"), (l, "vsvw"), (l, "gt"), (l, "cs", 0), (l, "cs", 1), (l, "hg0"), (l, "hg1"),
                     (l, "ho", 0), (l, "ho", 1), (l, "cT"), (l, "hoT", 0), (l, "hoT", 1),
                     (l, "co", 0), (l, "co", 1)]
            uses += attention()
            uses += [(l, "oT", 1, 0), (l, "oT", 1, 1)]
        elif l == 2:
            uses += [(l, "kw")] + [(l, f"qi{j}") for j in range(4)] + [(l, "kiT")]
            for j in range(12):
                uses += [(l, projections(l)[4 + j])]
                uses += [(l, "I", i) for i in ((2 * j, 2 * j + 1) if j < 8 else ())]
            uses += attention() + [(l, "oT", a, tt) for a in range(2) for tt in range(NT)]
        else:
            uses += [(l, n) for n in projections(l)]
            uses += attention() + [(l, "oT", a, tt) for a in range(2) for tt in range(NT)]
        mid, end = norm_after(l)
        uses += [(mid, "xT", tt, q) for tt in range(NT) for q in range(2)]
        uses += [(l, "up", j) for k, j in ffn_order() if k == "up"]
        if end not in (3, 8):
            uses += [(end, "xT", tt, q) for tt in range(NT) for q in range(2)]
    return uses


def norm_after(l):
    return {0: (0, 1), 1: (2, 3), 2: (5, 6), 3: (7, 8)}[l]


def unsplit(key):
    return key[1] in ("w1k", "w1v")


def turned(key):
    return key[1:2] in (("xT",), ("oT",), ("hoT",))


def build(nc, a):
    stream = stream_order()
    tile_no = {key: i for i, key in enumerate(stream)}
    bank_no = {key: i for i, key in enumerate(bank_order())}
    split_tiles = [key for key in stream if not unsplit(key)]
    split_no = {key: i for i, key in enumerate(split_tiles)}
    turned_no = {key: i for i, key in enumerate(k for k in bank_order() if turned(k))}
    assert len(bank_no) == len(bank_order()) and len(tile_no) == len(stream)

    with ExitStack() as ctx:
        def sb(name, shape, dt=F32):
            return ctx.enter_context(nc.sbuf_tensor(name, shape, dt))

        def sem(name):
            return ctx.enter_context(nc.semaphore(name))

        bank = ctx.enter_context(nc.psum_tensor("bank", [P, 8, 512], F32))

        raw = sb("raw", [P, SLOTS, TILE])
        w_hi = sb("w_hi", [P, PARTS, TILE], F32R)
        w_lo = sb("w_lo", [P, PARTS, TILE], F32R)
        x = sb("x", [P, NT, D])
        res = sb("res", [P, NT, D])
        a_hi = sb("a_hi", [P, KT, S], F32R)
        a_lo = sb("a_lo", [P, KT, S], F32R)
        gains = sb("gains", [P, 2, D])
        bias_t = sb("bias_t", [P, 24, S])
        neglog = sb("neglog", [P, NT, P])
        lbuf = sb("lbuf", [P, 2, TRI])
        pT = sb("pT", [P, 2, TRI])
        ident = sb("ident", [P, P])
        hg_mask = sb("hg_mask", [P, len(HALVES), P], U8)
        cmp_bias = sb("cmp_bias", [P, NT, 8, NC])
        cmp_off = sb("cmp_off", [P, NT, NC])
        cmp_on = sb("cmp_on", [P, NT, NC])
        head_blocks = sb("head_blocks", [P, 8])
        lb = sb("lb", [P, 2, HG_HEADS])
        lb_log = sb("lb_log", [P, 2, HG_HEADS])
        lb_tmp = sb("lb_tmp", [P, 4, HG_HEADS])
        gnorm = sb("gnorm", [P, 2, P])
        pos = sb("pos", [P, 2, 2, CMP_KT])
        w2 = sb("w2", [P, 2, 192])
        w_gate = sb("w_gate", [P, 2, KT, 24])
        idx_norm = sb("idx_norm", [P, DH])
        conv_col = sb("conv_col", [P, 2, 2 * FT, 4])
        causal = sb("causal", [P, TRI])
        mxn = sb("mxn", [P, 2, NT, 8])
        esum = sb("esum", [P, 2, NT, 8])
        wgt = sb("wgt", [P, 2, NT, 8])
        stat = sb("stat", [P, 16])
        nstat = sb("nstat", [P, NT, 20])
        small = sb("small", [P, NT, 128])
        gates = sb("gates", [P, NT, 24])
        cmx = sb("cmx", [P, 3, NT * 8])
        ones = sb("ones", [P, S])
        eps_ln = sb("eps_ln", [P, 1])
        eps_rms = sb("eps_rms", [P, 1])
        hid = sb("hid", [P, 30])
        hid_v = sb("hid_v", [P, 8, NCP])
        kc2 = sb("kc2", [P, 2, NC])
        cp = sb("cp", [P, NT, 8, NCP])
        with nc.sbuf_tensor("arena", [P, ARENA], F32) as arena:
            pass
        h_hi = sb("h_hi", [P, HSLOTS, S], F32R)
        h_lo = sb("h_lo", [P, HSLOTS, S], F32R)

        used = [0]

        def take(n):
            used[0] += n
            assert used[0] <= ARENA, used
            return arena[:, used[0] - n:used[0]]

        f_t, q_t, k_t, dec0, dec1, lev0, lev1 = [take(D) for _ in range(7)]
        dec, lev = [dec0, dec1], [lev0, lev1]
        b_t = dec1
        s_cross = take(512)
        v_hg = take(D).rearrange("p (t c) -> p t c", t=NT)
        g_hg = f_t.rearrange("p (t c) -> p t c", t=NT)
        nq = take(D).rearrange("p (j t) -> p j t", j=4)
        ks2 = take(512).rearrange("p (g t) -> p g t", g=2)
        kw2 = take(512).rearrange("p (g t) -> p g t", g=2)
        v_sw = take(512).rearrange("p (t c) -> p t c", t=NT)
        s_hg = take(D)
        blk = [b[:, :, :].rearrange("p j t -> p (j t)")[:, 0:CMP_KT * 30].rearrange(
            "p (k g n) -> p k g n", k=CMP_KT, g=2) for b in (lbuf, pT)]
        o_hg = [dec[0][:, 0:512], dec[0][:, 512:1024]]
        o_sq = [dec[1][:, 0:512], dec[1][:, 512:1024]]
        vc8 = res[:, 0, 512:1024].rearrange("p (h d) -> p h d", d=DH)
        cl = res[:, 0, 0:NT * 8 * NC].rearrange("p (t h n) -> p t h n", t=NT, h=8)
        ce = res[:, 1, 0:NT * 8 * NC].rearrange("p (t h n) -> p t h n", t=NT, h=8)
        cpT = res[:, 1, 512:512 + 2 * P].rearrange("p (t c) -> p t c", t=NT)
        used[0] = 0
        take(2 * HSLOTS * S)
        h_full = [take(S) for _ in range(2)]
        gate_a = [take(S) for _ in range(2)]
        cval = [take(S) for _ in range(2)]
        cgate = [take(S) for _ in range(2)]
        used[0] = 0
        q2 = take(8 * S).rearrange("p (j t) -> p j t", j=8)
        k2 = take(8 * S).rearrange("p (j t) -> p j t", j=8)
        v2 = take(2 * D).rearrange("p (t c) -> p t c", t=NT)
        qi = take(8 * S).rearrange("p (j t) -> p j t", j=8)
        kiT = take(S)
        score = take(TRI)
        relu = [take(TRI) for _ in range(2)]
        unsel = take(TRI)
        bias_s = [take(TRI) for _ in range(2)]
        w_idx = take(KT * 80).rearrange("p (k c) -> p k c", k=KT)
        used[0] = 0
        bias_rev = take(24 * S).rearrange("p (h s) -> p h s", h=24)
        one_hot = take(REV)
        one_hot_c = take(2 * S)
        rel = take(24)
        off_row = take(REV)
        bias_row = take(REV)
        mask_in = res[:, :, :].rearrange("p t c -> p (t c)")[:, 0:len(HALVES) * P].rearrange(
            "p (v s) -> p v s", v=len(HALVES))
        flip = take(P)
        xT0 = take(KT * S).rearrange("p (k t) -> p k t", k=KT)
        scratch = nc.dram_tensor("bias_rows", (24, REV), F32, kind="Internal").ap()

        tile_loaded = [sem(f"tile_loaded{i}") for i in range(SLOTS)]
        rows_used = sem("rows_used")
        w_hi_done = sem("w_hi_done")
        w_lo_done = sem("w_lo_done")
        a_hi_done = sem("a_hi_done")
        a_lo_done = sem("a_lo_done")
        w_idx_in = sem("w_idx_in")
        bank_full = sem("bank_full")
        bank_drained = [sem(f"bank_drained{i}") for i in range(RING)]
        consts_in = sem("consts_in")
        start_in = sem("start_in")
        x_in = sem("x_in")
        rows_out = sem("rows_out")
        rev_in = sem("rev_in")
        zeroed = sem("zeroed")
        lb_ready = sem("lb_ready")
        act_step = sem("act_step")
        dve_step = sem("dve_step")
        pool_step = sem("pool_step")
        bias_row_ready = sem("bias_row_ready")
        softplus_done = sem("softplus_done")
        logsig_done = sem("logsig_done")
        gap_done = sem("gap_done")
        softplus2_done = sem("softplus2_done")
        kdiff_done = sem("kdiff_done")
        k_done = sem("k_done")
        cumsum_done = sem("cumsum_done")
        diff_done = sem("diff_done")
        decay_done = sem("decay_done")
        level_done = sem("level_done")
        product_done = sem("product_done")
        picked = sem("picked")
        hid_done = sem("hid_done")
        cmp_logit = sem("cmp_logit")
        cmp_exp = sem("cmp_exp")
        cmp_prob = sem("cmp_prob")
        gate_exp = sem("gate_exp")
        g_scaled = sem("g_scaled")
        sq_done = sem("sq_done")
        ssq_done = sem("ssq_done")
        hg_rstd = sem("hg_rstd")
        hg_out = sem("hg_out")
        logit_done = sem("logit_done")
        exp_done = sem("exp_done")
        pv_done = sem("pv_done")
        mix_done = sem("mix_done")
        acc_full = sem("acc_full")
        acc_drained = sem("acc_drained")
        sum_done = sem("sum_done")
        square_done = sem("square_done")
        rstd_done = sem("rstd_done")
        normed = sem("normed")
        gains_in = sem("gains_in")
        gains_used = sem("gains_used")
        act_gate = sem("act_gate")
        conv_in = sem("conv_in")
        conv_done = sem("conv_done")
        silu_done = sem("silu_done")
        h_done = sem("h_done")
        ki_sq = sem("ki_sq")
        ki_rstd = sem("ki_rstd")
        ki_normed = sem("ki_normed")
        relu_done = sem("relu_done")
        relu_used = sem("relu_used")
        unsel_done = sem("unsel_done")
        bias_sel = sem("bias_sel")
        bias_log = sem("bias_log")
        out_sem = sem("stored")

        def bank_of(key):
            return bank[:, bank_no[key] % RING, :]

        def wait_full(eng, key):
            eng.wait_ge(bank_full, bank_no[key] + 1)

        def wait_drained(eng, key):
            eng.wait_ge(bank_drained[bank_no[key] % RING], bank_no[key] // RING + 1)

        def drained(key):
            return bank_drained[bank_no[key] % RING], 1

        def steps(eng, s):
            n = [0]

            def step(ins):
                n[0] += 1
                ins.then_inc(s, 1)
                eng.wait_ge(s, n[0])
            return step

        def wait_used(eng, key):
            l, name = key
            kind = name.rstrip("0123456789")
            number = int(name[len(kind):] or 0)
            if kind in ("out", "down"):
                if number == {"out": 3, "down": FT // 2 - 1}[kind]:
                    eng.wait_ge(acc_full, (2 * l + (kind == "down") + 1) * NT)
                else:
                    eng.wait_ge(rows_used, l * (3 + FT // 2 - 1) + number + 1 + 3 * (kind == "down"))
            elif kind == "up":
                wait_full(eng, (l, "up", number))
            else:
                wait_full(eng, (l, "hid") if unsplit(key) else key)

        def half_tile(i):
            return slice(i * (TILE // 2), (i + 1) * (TILE // 2))

        def split_high(act, i):
            key = split_tiles[i]
            t = tile_no[key]
            act.wait_ge(tile_loaded[t % SLOTS], 16 * (t // SLOTS + 1))
            if i >= PARTS:
                wait_used(act, split_tiles[i - PARTS])
            for h in range(2):
                act.activation(w_hi[:, i % PARTS, half_tile(h)], raw[:, t % SLOTS, half_tile(h)],
                               ACT.Copy).then_inc(w_hi_done, 1)

        def split_low(dve, i):
            t = tile_no[split_tiles[i]]
            for h in range(2):
                dve.wait_ge(w_hi_done, 2 * i + h + 1)
                dve.tensor_tensor(w_lo[:, i % PARTS, half_tile(h)], raw[:, t % SLOTS, half_tile(h)],
                                  w_hi[:, i % PARTS, half_tile(h)].bitcast(F32), ALU.subtract).then_inc(w_lo_done, 1)

        def split_behind(eng, key, split):
            i = split_no[key] + PARTS
            if i < len(split_tiles):
                split(eng, i)

        def turned_high(act, key, part):
            wait_full(act, key)
            act.activation(part, bank_of(key).rearrange("p (i t) -> p i t", i=4), ACT.Copy).then_inc(a_hi_done, 1)

        def turned_low(dve, key, part, high):
            dve.wait_ge(a_hi_done, turned_no[key] + 2)
            dve.tensor_tensor(part, bank_of(key).rearrange("p (i t) -> p i t", i=4), high.bitcast(F32),
                              ALU.subtract).then_inc(*drained(key))

        def bc_mid(ap, n):
            return ap.unsqueeze(1).to_broadcast([ap.shape[0], n, ap.shape[1]])

        def bc_last(ap, n):
            return ap.unsqueeze(2).to_broadcast([ap.shape[0], ap.shape[1], n])

        def heads4(ap):
            return ap.rearrange("p (h t) -> p h t", h=HG_HEADS)

        def attn_io(l, i):
            half, h = i // 8, i % 8
            if l < 2:
                g, lo = h // 4, DH * (h % 2)
                kk = (ks2, kw2)[half]
                return (half, h, nq[lo:lo + DH, h // 2, :], kk[lo:lo + DH, g, :],
                        lambda st: v_sw[:, st, half * P + g * DH:half * P + (g + 1) * DH], h, False)
            lo = DH * (i % 2)
            return (half, h, q2[lo:lo + DH, i // 2, :], k2[lo:lo + DH, i // 2, :],
                    lambda st: v2[:, st, i * DH:(i + 1) * DH], 8 + i, l == 2 and half == 1)

        LEVELS_AFTER = {"kcvc": [0, 1], "nq0": [2], "nq1": [3], "kskw": [4], "vsvw": [5], "gt": [6], "hg0": [7],
                        "hg1": [8]}
        PREP_AFTER = {"hi1": [1, 2], "kcvc": [3], "nq0": [4], "nq1": [5], "kskw": [6], "vsvw": [7], "gt": [8]}
        NLEV = len(HALVES)

        def level_banks(v):
            return bank[:, 4 + 2 * (v % 2):6 + 2 * (v % 2), :].rearrange("p b c -> p (b c)")

        def blocks(ap, half):
            return ap.rearrange("p (n w) -> p n w", w=2 * half)

        block = ctx.enter_context(nc.Block())

        @block.sync
        def _(sp):
            sp.dma_start(one_hot_c[0:BUCKETS, :], a["one_hot_c"]).then_inc(start_in, 16)
            sp.dma_start(one_hot[0:BUCKETS, :], a["one_hot"]).then_inc(start_in, 16)
            sp.dma_start(rel[0:BUCKETS, :], a["rel"]).then_inc(start_in, 16)
            sp.dma_start(off_row[0:24, :], a["off_row"]).then_inc(start_in, 16)
            sp.dma_start(ident[:, :], a["ident"]).then_inc(start_in, 16)
            sp.dma_start(flip[:, :], a["flip"]).then_inc(start_in, 16)
            sp.dma_start(cmp_off[:, :, :], a["cmp_off"]).then_inc(start_in, 16)
            sp.dma_start(xT0, a["xT"]).then_inc(x_in, 16)

            def load(i):
                if i >= SLOTS:
                    old = stream[i - SLOTS]
                    if unsplit(old):
                        wait_used(sp, old)
                    else:
                        sp.wait_ge(w_lo_done, 2 * (split_no[old] + 1))
                sp.dma_start(raw[:, i % SLOTS, :], a["stream"][i]).then_inc(tile_loaded[i % SLOTS], 16)

            for i in range(SLOTS):
                load(i)
            sp.wait_ge(bias_row_ready, 1)
            sp.dma_start(scratch, bias_row[0:24, :]).then_inc(rows_out, 16)
            sp.wait_ge(rows_out, 16)
            sp.dma_start(bias_rev, bass.AP(scratch.tensor, 0, [[1, P], [REV, 24], [1, S]])).then_inc(rev_in, 16)
            sp.dma_start(x[:, :, :], a["x"]).then_inc(consts_in, 16)
            for dst, name in ((mask_in, "hg_mask"), (cmp_on[:, :, :], "cmp_on"),
                              (head_blocks[:, :], "head_blocks"), (lb[:, :, :], "lb"), (pos[:, :, :, :], "pos"),
                              (w2[:, :, :], "w2"), (w_gate[:, :, :, :], "w_gate"),
                              (conv_col[:, :, :, :], "conv_col"), (causal[:, :], "causal"),
                              (neglog[:, :, :], "neglog"), (gnorm[:, :, :], "gnorm"), (idx_norm[:, :], "idx_norm")):
                sp.dma_start(dst, a[name]).then_inc(consts_in, 16)
            for i in range(SLOTS, len(stream)):
                load(i)
            sp.wait_ge(normed, 9 * NT)
            sp.dma_start(a["out"], res[:, :, :]).then_inc(out_sem, 16)
            sp.wait_ge(out_sem, 16)

        CONSTS = 13 * 16

        @block.tensor
        def _(pe):
            def open_bank(key):
                n = bank_no[key]
                if n >= RING:
                    pe.wait_ge(bank_drained[n % RING], n // RING)
                return bank_of(key)

            def close_bank(ins):
                ins.then_inc(bank_full, 1)

            def weights(key):
                i = split_no[key]
                pe.wait_ge(w_lo_done, 2 * (i + 1))
                return w_hi[:, i % PARTS, :], w_lo[:, i % PARTS, :]

            def products(out, left, right, first=True, last=True):
                (lh, ll), (rh, rl) = left, right
                pe.matmul(out, lh, rh, start=first, stop=False)
                pe.matmul(out, lh, rl, start=False, stop=False)
                return pe.matmul(out, ll, rh, start=False, stop=last)

            def channel_tile(key, use=None):
                b = open_bank(use or key)
                w = [part.rearrange("p (k c) -> p k c", k=KT) for part in weights(key)]
                for c in range(2):
                    for k in range(KT):
                        mm = products(b[:, c * S:(c + 1) * S], [part[:, k, c * P:(c + 1) * P] for part in w],
                                      (a_hi[:, k, :], a_lo[:, k, :]), k == 0, k == KT - 1)
                close_bank(mm)

            def token_tile(key):
                b = open_bank(key)
                w = [part.rearrange("p (k c) -> p k c", k=KT) for part in weights(key)]
                for tt in range(NT):
                    t = slice(tt * P, (tt + 1) * P)
                    for k in range(KT):
                        mm = products(b[:, tt * S:(tt + 1) * S], (a_hi[:, k, t], a_lo[:, k, t]),
                                      [part[:, k, :] for part in w], k == 0, k == KT - 1)
                close_bank(mm)

            def small_tile(key, w):
                b = open_bank(key)
                n = w.shape[2]
                for tt in range(NT):
                    for k in range(KT):
                        for part in (a_hi, a_lo):
                            mm = pe.matmul(b[:, tt * n:(tt + 1) * n], part[:, k, tt * P:(tt + 1) * P].bitcast(F32),
                                           w[:, k, :], start=(k == 0 and part is a_hi),
                                           stop=(k == KT - 1 and part is a_lo))
                close_bank(mm)

            def token_major(name):
                return name[:2] in ("hi", "hg", "vs") or name[0] == "v"

            def project(l, name):
                (token_tile if token_major(name) else channel_tile)((l, name))

            def x_transposes(n):
                for tt in range(NT):
                    pe.wait_ge(normed, n * NT + tt + 1)
                    for q in range(2):
                        b = open_bank((n, "xT", tt, q))
                        for i in range(4):
                            c = (4 * q + i) * P
                            mm = pe.transpose(b[:, i * P:(i + 1) * P], (x if n < 3 else res)[:, tt, c:c + P],
                                              ident[:, :])
                        close_bank(mm)

            def xT_ready(n):
                for tt in range(NT):
                    for q in range(2):
                        wait_drained(pe, (n, "xT", tt, q))

            def level(l, v):
                half = HALVES[v]
                if l * NLEV + v >= 2:
                    pe.wait_ge(picked, l * NLEV + v - 1)
                if v == 0:
                    if l == 1:
                        pe.wait_ge(acc_drained, 2 * NT)
                    pe.wait_ge(k_done, l + 1)
                    wait_drained(pe, (l, "hq1"))
                    lhs, rhs = k_t, q_t
                else:
                    pe.wait_ge(level_done, l * (NLEV - 1) + v)
                    lhs = rhs = lev[v % 2]
                out = level_banks(v)
                for h in range(HG_HEADS):
                    if half == P:
                        mm = pe.matmul(out[:, h * P:(h + 1) * P], lhs[:, h * S:h * S + P],
                                       rhs[:, h * S + P:(h + 1) * S], start=True, stop=True)
                        continue
                    for st in range(NT):
                        c = h * S + st * P
                        mm = pe.matmul(out[:, c:c + P], lhs[:, c:c + P], rhs[:, c:c + P], start=True, stop=True)
                mm.then_inc(product_done, 1)

            def attention(l):
                for s, t, v in attention_steps():
                    if s is not None:
                        half, h, q, k, _, _, _ = attn_io(l, s)
                        b = open_bank((l, "S", s))
                        pe.matmul(b[:, 0:S], q[:, P:S], k, start=True, stop=True)
                        close_bank(pe.matmul(b[:, S:TRI], q[:, 0:P], k[:, 0:P], start=True, stop=True))
                    if t is not None:
                        b = open_bank((l, "T", t))
                        e = lbuf[:, t % 2, :]
                        pe.wait_ge(exp_done, l * HEADS + t + 1)
                        pe.transpose(b[:, 0:P], e[:, S:TRI], ident[:, :])
                        pe.transpose(b[:, P:2 * P], e[:, 0:P], ident[:, :])
                        close_bank(pe.transpose(b[:, 2 * P:3 * P], e[:, P:2 * P], ident[:, :]))
                    if v is not None:
                        half, h, _, _, val, _, _ = attn_io(l, v)
                        wait_drained(pe, (l, "T", v))
                        if v == 0:
                            if l < 2:
                                pe.wait_ge(picked, (l + 1) * NLEV)
                            else:
                                pe.wait_ge(acc_drained, 2 * l * NT)
                        pt = pT[:, v % 2, :]
                        o0 = bank[:, 4 + 2 * half, h * DH:(h + 1) * DH]
                        o1 = bank[:, 5 + 2 * half, h * DH:(h + 1) * DH]
                        pe.matmul(o0, pt[:, 0:P], val(0), start=True, stop=True)
                        pe.matmul(o1, pt[:, P:2 * P], val(0), start=True, stop=False)
                        pe.matmul(o1, pt[:, 2 * P:3 * P], val(1), start=False, stop=True).then_inc(pv_done, 1)

            def transposes_out(l, half, tt, src):
                b = open_bank((l, "oT", half, tt))
                for i in range(4):
                    mm = pe.transpose(b[:, i * P:(i + 1) * P], src[:, i * P:(i + 1) * P], ident[:, :])
                close_bank(mm)

            def add_rows(key, left, first, last):
                w = [part.rearrange("p (k c) -> p k c", k=2) for part in weights(key)]
                for tt in range(NT):
                    for kk in range(2):
                        for hf in range(2):
                            mm = products(bank[:, 4 + 2 * tt + hf, :],
                                          [part[:, kk, tt * P:(tt + 1) * P] for part in left],
                                          [part[:, kk, hf * 512:(hf + 1) * 512] for part in w],
                                          first and kk == 0, last and kk == 1)
                    if last:
                        mm.then_inc(acc_full, 1)
                if not last:
                    mm.then_inc(rows_used, 1)

            def output_projection(l):
                for half in range(2):
                    for tt in range(NT):
                        if (l, "oT", half, tt) in bank_no:
                            wait_drained(pe, (l, "oT", half, tt))
                        else:
                            wait_drained(pe, (l, "hoT", tt))
                pe.wait_ge(mix_done, (2 * l + 2) * NT)
                for r in range(4):
                    add_rows((l, f"out{r}"), [part[:, 2 * r:2 * r + 2, :] for part in (a_hi, a_lo)], r == 0, r == 3)

            def feed_forward(l):
                xT_ready(norm_after(l)[0])
                for kind, j in ffn_order():
                    if kind == "up":
                        channel_tile((l, f"up{j}"), use=(l, "up", j))
                    else:
                        pe.wait_ge(h_done, l * FT + 2 * j + 2)
                        if j == 0:
                            pe.wait_ge(acc_drained, (2 * l + 1) * NT)
                        i = 2 * j % HSLOTS
                        add_rows((l, f"down{j}"), (h_hi[:, i:i + 2, :], h_lo[:, i:i + 2, :]), j == 0, j == FT // 2 - 1)

            pe.wait_ge(start_in, 7 * 16)
            b = open_bank(("cmpbias",))
            for tt in range(NT):
                for n in range(NC):
                    at = S - 1 + tt * P - 16 * n - 31
                    mm = pe.matmul(b[:, (tt * NC + n) * 8:(tt * NC + n + 1) * 8], one_hot_c[0:BUCKETS, at:at + P],
                                   rel[0:BUCKETS, 0:8], start=True, stop=True)
            close_bank(mm)
            b = open_bank(("biasrow",))
            close_bank(pe.matmul(b[0:24, 0:REV], rel[0:BUCKETS, 0:24], one_hot[0:BUCKETS, :], start=True, stop=True))
            pe.wait_ge(rev_in, 16)
            for c in range(12):
                b = open_bank(("bias", c))
                close_bank(pe.matmul(b, flip[:, :], bias_rev[:, 2 * c:2 * c + 2, :].rearrange("p h s -> p (h s)"),
                                     start=True, stop=True))

            for l in range(LAYERS):
                if l == 0:
                    pe.wait_ge(a_lo_done, 1)
                    pe.wait_ge(consts_in, CONSTS)
                elif l == 2:
                    x_transposes(4)
                    xT_ready(4)
                elif l == 1:
                    xT_ready(1)
                else:
                    xT_ready(6)
                if l < 2:
                    for name in ("hf0", "hf1", "hq0", "hq1", "hi0", "hi1", "kcvc"):
                        project(l, name)
                    for v in LEVELS_AFTER["kcvc"]:
                        level(l, v)
                    for name in ("nq0", "nq1"):
                        project(l, name)
                        for v in LEVELS_AFTER[name]:
                            level(l, v)
                    b = open_bank((l, "hid"))
                    wait_drained(pe, (l, "kcvc"))
                    for i, name in enumerate(("w1k", "w1v")):
                        t = tile_no[(l, name)]
                        pe.wait_ge(tile_loaded[t % SLOTS], 16 * (t // SLOTS + 1))
                        w = raw[:, t % SLOTS, :].rearrange("p (k c) -> p k c", k=CMP_KT)
                        for k in range(CMP_KT):
                            mm = pe.matmul(b[:, 32 * i:32 * i + 30], w[:, k, :],
                                           blk[i][:, k, :, :].rearrange("p g n -> p (g n)"),
                                           start=(k == 0), stop=(k == CMP_KT - 1))
                    close_bank(mm)
                    b = open_bank((l, "kcv"))
                    wait_drained(pe, (l, "hid"))
                    pe.matmul(b[:, 0:30], w2[:, l, 0:P], hid[:, :], start=True, stop=True)
                    close_bank(pe.matmul(b[:, DH:2 * DH], hid_v[:, :, :].rearrange("p h n -> p (h n)"),
                                         w2[:, l, P:P + DH], start=True, stop=True))
                    for name in ("kskw", "vsvw"):
                        project(l, name)
                        for v in LEVELS_AFTER[name]:
                            level(l, v)
                    small_tile((l, "gt"), w_gate[:, l, :, :])
                    for v in LEVELS_AFTER["gt"]:
                        level(l, v)
                    wait_drained(pe, (l, "kcv"))
                    wait_drained(pe, (l, "nq1"))
                    for odd in range(2):
                        b = open_bank((l, "cs", odd))
                        lo = DH * odd
                        for tt in range(NT):
                            for j in range(4):
                                c = (tt * 4 + j) * NCP
                                mm = pe.matmul(b[:, c:c + NC], nq[lo:lo + DH, j, tt * P:(tt + 1) * P],
                                               kc2[lo:lo + DH, j // 2, :], start=True, stop=True)
                        close_bank(mm)
                    for name in ("hg0", "hg1"):
                        project(l, name)
                        for v in LEVELS_AFTER[name]:
                            level(l, v)
                    for tt in range(NT):
                        b = open_bank((l, "ho", tt))
                        pe.wait_ge(picked, (l + 1) * NLEV)
                        wait_drained(pe, (l, "hi1"))
                        for h in range(HG_HEADS):
                            o = b[:, h * P:(h + 1) * P]
                            if tt == 1:
                                pe.matmul(o, s_cross[:, h * P:(h + 1) * P], v_hg[:, 0, h * P:(h + 1) * P],
                                          start=True, stop=False)
                            mm = pe.matmul(o, s_hg[:, h * S + tt * P:h * S + (tt + 1) * P],
                                           v_hg[:, tt, h * P:(h + 1) * P], start=(tt == 0), stop=True)
                        close_bank(mm)
                    b = open_bank((l, "cT"))
                    pe.wait_ge(cmp_prob, l + 1)
                    for tt in range(NT):
                        mm = pe.transpose(b[:, tt * P:(tt + 1) * P], cp[:, tt, :, :].rearrange("p h n -> p (h n)"),
                                          ident[:, :])
                    close_bank(mm)
                    for tt in range(NT):
                        b = open_bank((l, "hoT", tt))
                        pe.wait_ge(hg_out, l * NT + tt + 1)
                        for i in range(HG_HEADS):
                            mm = pe.transpose(b[:, i * P:(i + 1) * P], o_hg[tt][:, i * P:(i + 1) * P], ident[:, :])
                        close_bank(mm)
                    for tt in range(NT):
                        b = open_bank((l, "co", tt))
                        wait_drained(pe, (l, "cT"))
                        close_bank(pe.matmul(b[:, :], cpT[:, tt, :], vc8[:, :, :].rearrange("p h d -> p (h d)"),
                                             start=True, stop=True))
                    wait_drained(pe, (l, "vsvw"))
                    wait_drained(pe, (l, "kskw"))
                    attention(l)
                    for tt in range(NT):
                        pe.wait_ge(mix_done, 2 * l * NT + NT + tt + 1)
                        transposes_out(l, 1, tt, res[:, tt, 0:512])
                else:
                    if l == 2:
                        pe.wait_ge(w_idx_in, 16)
                        small_tile((l, "kw"), w_idx)
                        for j in range(4):
                            project(l, f"qi{j}")
                        b = open_bank((l, "kiT"))
                        pe.wait_ge(ki_normed, NT)
                        for tt in range(NT):
                            mm = pe.transpose(b[:, tt * P:(tt + 1) * P], small[:, tt, :], ident[:, :])
                        close_bank(mm)
                    for j, name in enumerate(projections(l)[-12:]):
                        project(l, name)
                        if l == 2 and j < 8:
                            for i in (2 * j, 2 * j + 1):
                                b = open_bank((l, "I", i))
                                lo = DH * (i % 2)
                                wait_drained(pe, (l, "kiT"))
                                wait_drained(pe, (l, f"qi{i // 4}"))
                                pe.matmul(b[:, 0:S], qi[lo:lo + DH, i // 2, P:S], kiT[lo:lo + DH, :],
                                          start=True, stop=True)
                                close_bank(pe.matmul(b[:, S:TRI], qi[lo:lo + DH, i // 2, 0:P],
                                                     kiT[lo:lo + DH, 0:P], start=True, stop=True))
                    for name in projections(l)[-12:]:
                        wait_drained(pe, (l, name))
                    attention(l)
                    for half in range(2):
                        for tt in range(NT):
                            pe.wait_ge(mix_done, (2 * l + half) * NT + tt + 1)
                            transposes_out(l, half, tt, res[:, tt, half * 512:(half + 1) * 512])
                output_projection(l)
                x_transposes(norm_after(l)[0])
                feed_forward(l)
                if norm_after(l)[1] not in (3, 8):
                    x_transposes(norm_after(l)[1])

        @block.scalar
        def _(act):
            step = steps(act, act_step)

            def copy_out(key, dst, src=None, scale=1.0):
                wait_full(act, key)
                act.activation(dst, bank_of(key) if src is None else src, ACT.Copy,
                               scale=scale).then_inc(*drained(key))

            def two(ap):
                return ap.rearrange("p (c t) -> p c t", c=2)

            def level_decay(l, v):
                n = l * (NLEV - 1) + v
                half = HALVES[v]
                act.wait_ge(diff_done, n)
                d = blocks(dec[v % 2], half)
                act.activation(d[:, :, half:], d[:, :, half:], ACT.Exp)
                act.activation(d[:, :, :half], d[:, :, :half], ACT.Exp, scale=-1.0).then_inc(decay_done, 1)

            def prep(l, name):
                for v in PREP_AFTER.get(name, ()):
                    level_decay(l, v)

            def attention(l):
                for i in range(HEADS):
                    half, h = i // 8, i % 8
                    act.wait_ge(logit_done, l * HEADS + i + 1)
                    if i >= 2:
                        wait_full(act, (l, "T", i - 2))
                    act.activation(lbuf[:, i % 2, 0:S], lbuf[:, i % 2, 0:S], ACT.Exp, scale=-1.0,
                                   bias=mxn[:, half, 1, h:h + 1], accum_out=esum[:, half, 1, h:h + 1])
                    act.activation(lbuf[:, i % 2, S:TRI], lbuf[:, i % 2, S:TRI], ACT.Exp, scale=-1.0,
                                   bias=mxn[:, half, 0, h:h + 1],
                                   accum_out=esum[:, half, 0, h:h + 1]).then_inc(exp_done, 1)

            def rstd(n):
                for tt in range(NT):
                    st = nstat[:, tt, :]
                    if n < 4:
                        act.wait_ge(sum_done, n * NT + tt + 1)
                        step(act.activation(st[:, 14:15], st[:, 13:14], ACT.Ln, bias=eps_ln[:, 0:1]))
                    else:
                        if n == 4:
                            act.wait_ge(normed, 3 * NT + tt + 1)
                        else:
                            act.wait_ge(acc_drained, (n - 1) * NT + tt + 1)
                        step(act.activation(res[:, tt, :], x[:, tt, :], ACT.Square, accum_out=st[:, 13:14]))
                        step(act.activation(st[:, 14:15], st[:, 13:14], ACT.Ln, scale=1.0 / D, bias=eps_rms[:, 0:1]))
                    act.activation(st[:, 15:16], st[:, 14:15], ACT.Exp, scale=-0.5).then_inc(rstd_done, 1)

            def xT_out(n):
                for tt in range(NT):
                    for q in range(2):
                        turned_high(act, (n, "xT", tt, q), a_hi[:, 4 * q:4 * q + 4, tt * P:(tt + 1) * P])

            def feed_forward(l):
                for kind, j in ffn_order():
                    if kind == "up":
                        up(l, j)
                    split_behind(act, (l, f"{kind}{j}"), split_high)

            def up(l, j):
                if True:
                    key = (l, "up", j)
                    wait_full(act, key)
                    b = bank_of(key)
                    if j >= 2:
                        act.wait_ge(h_done, l * FT + j - 1)
                    if l < 2:
                        act.activation(gate_a[j % 2], b[:, 0:S], ACT.Silu).then_inc(act_gate, 1)
                    else:
                        m = l - 2
                        act.activation(cval[j % 2], b[:, 0:S], ACT.Identity, scale=conv_col[:, m, j, 2:3],
                                       bias=conv_col[:, m, j, 3:4])
                        act.activation(cgate[j % 2], b[:, S:2 * S], ACT.Identity, scale=conv_col[:, m, FT + j, 2:3],
                                       bias=conv_col[:, m, FT + j, 3:4]).then_inc(conv_in, 1)
                        act.wait_ge(conv_done, m * FT + j + 1)
                        act.activation(gate_a[j % 2], cgate[j % 2], ACT.Silu).then_inc(silu_done, 1)

            act.wait_ge(x_in, 16)
            act.activation(a_hi[:, :, :], xT0, ACT.Copy).then_inc(a_hi_done, 1)
            for i in range(PARTS):
                split_high(act, i)
            act.wait_ge(zeroed, 5)
            act.wait_ge(lb_ready, 1)
            step(act.activation(lb_tmp[:, 1, :], lb_tmp[:, 0, :], ACT.Abs))
            step(act.activation(lb_tmp[:, 2, :], lb_tmp[:, 1, :], ACT.Exp, scale=-1.0))
            act.activation(lb_tmp[:, 3, :], lb_tmp[:, 2, :], ACT.Ln, bias=1.0).then_inc(lb_ready, 1)
            for c in range(12):
                copy_out(("bias", c), bias_t[:, 2 * c:2 * c + 2, :].rearrange("p h s -> p (h s)"))

            for l in range(LAYERS):
                if l < 2:
                    for i in range(2):
                        copy_out((l, f"hf{i}"), f_t[:, i * 512:(i + 1) * 512])
                        split_behind(act, (l, f"hf{i}"), split_high)
                    wait_drained(act, (l, "hf0"))
                    wait_drained(act, (l, "hf1"))
                    step(act.activation(dec[0], f_t, ACT.Abs))
                    step(act.activation(dec[0], dec[0], ACT.Exp, scale=-1.0))
                    act.activation(dec[0], dec[0], ACT.Ln, bias=1.0).then_inc(softplus_done, 1)
                    if l == 1:
                        act.wait_ge(gap_done, 1)
                        step(act.activation(dec[0], dec[0], ACT.Abs))
                        step(act.activation(dec[0], dec[0], ACT.Exp, scale=-1.0))
                        act.activation(dec[0], dec[0], ACT.Ln, bias=1.0).then_inc(softplus2_done, 1)
                    act.wait_ge(kdiff_done, l + 1)
                    act.activation(k_t, k_t, ACT.Exp).then_inc(k_done, 1)
                    for i in range(2):
                        copy_out((l, f"hq{i}"), q_t[:, i * 512:(i + 1) * 512])
                        split_behind(act, (l, f"hq{i}"), split_high)
                    for i in range(2):
                        copy_out((l, f"hi{i}"), v_hg[:, :, i * S:(i + 1) * S], two(bank_of((l, f"hi{i}"))))
                        split_behind(act, (l, f"hi{i}"), split_high)
                    prep(l, "hi1")
                    split_behind(act, (l, "kcvc"), split_high)
                    prep(l, "kcvc")
                    for i in range(2):
                        copy_out((l, f"nq{i}"), nq[:, 2 * i:2 * i + 2, :], two(bank_of((l, f"nq{i}"))),
                                 scale=-(DH ** -0.5))
                        split_behind(act, (l, f"nq{i}"), split_high)
                        prep(l, f"nq{i}")
                    key = (l, "hid")
                    wait_full(act, key)
                    act.activation(hid[:, :], bank_of(key)[:, 0:30], ACT.Gelu_apprx_tanh)
                    for g in range(2):
                        src = bank_of(key)[:, 32 + g * NC:32 + (g + 1) * NC]
                        ins = act.activation(hid_v[:, 4 * g:4 * g + 4, 0:NC], bc_mid(src, 4), ACT.Gelu_apprx_tanh)
                    ins.then_inc(*drained(key))
                    key = (l, "kskw")
                    wait_full(act, key)
                    for i, dst in enumerate((ks2, kw2)):
                        for g in range(2):
                            for lo in (0, DH):
                                ins = act.activation(dst[lo:lo + DH, g, :],
                                                     bank_of(key)[g * DH:(g + 1) * DH, i * S:(i + 1) * S], ACT.Copy)
                    ins.then_inc(*drained(key))
                    split_behind(act, key, split_high)
                    prep(l, "kskw")
                    copy_out((l, "vsvw"), v_sw[:, :, :], two(bank_of((l, "vsvw"))))
                    split_behind(act, (l, "vsvw"), split_high)
                    prep(l, "vsvw")
                    key = (l, "gt")
                    wait_full(act, key)
                    act.activation(gates[:, :, :].rearrange("p t c -> p (t c)"), bank_of(key)[:, 0:48], ACT.Exp,
                                   scale=-1.0).then_inc(*drained(key))
                    prep(l, "gt")
                    act.wait_ge(cmp_logit, l + 1)
                    act.activation(ce[:, :, :, :], cl[:, :, :, :], ACT.Exp, scale=-1.0).then_inc(cmp_exp, 1)
                    for i in range(2):
                        key = (l, f"hg{i}")
                        wait_full(act, key)
                        act.activation(g_hg[:, :, i * S:(i + 1) * S], two(bank_of(key)),
                                       ACT.Silu).then_inc(*drained(key))
                        split_behind(act, key, split_high)
                    for tt in range(NT):
                        copy_out((l, "ho", tt), o_hg[tt])
                    act.wait_ge(ssq_done, l + 1)
                    step(act.activation(stat[:, 8:16], stat[:, 0:8], ACT.Ln, scale=1.0 / P, bias=eps_rms[:, 0:1]))
                    act.activation(stat[:, 8:16], stat[:, 8:16], ACT.Exp, scale=-0.5).then_inc(hg_rstd, 1)
                    for tt in range(NT):
                        turned_high(act, (l, "hoT", tt), a_hi[:, 0:4, tt * P:(tt + 1) * P])
                    attention(l)
                    for tt in range(NT):
                        turned_high(act, (l, "oT", 1, tt), a_hi[:, 4:8, tt * P:(tt + 1) * P])
                else:
                    if l == 2:
                        rstd(4)
                        xT_out(4)
                        key = (l, "kw")
                        wait_full(act, key)
                        for tt in range(NT):
                            ins = act.activation(small[:, tt, 0:80], bank_of(key)[:, tt * 80:(tt + 1) * 80], ACT.Copy)
                        ins.then_inc(*drained(key))
                        wait_drained(act, key)
                        for tt in range(NT):
                            step(act.activation(relu[0][:, 0:DH], small[:, tt, 0:DH], ACT.Square,
                                                accum_out=stat[:, tt:tt + 1]))
                        step(act.activation(stat[:, 2:4], stat[:, 0:2], ACT.Ln, scale=1.0 / DH, bias=eps_rms[:, 0:1]))
                        act.activation(stat[:, 4:6], stat[:, 2:4], ACT.Exp, scale=-0.5).then_inc(ki_rstd, 1)
                        for j in range(4):
                            copy_out((l, f"qi{j}"), qi[:, 2 * j:2 * j + 2, :], two(bank_of((l, f"qi{j}"))))
                            split_behind(act, (l, f"qi{j}"), split_high)
                        copy_out((l, "kiT"), kiT, bank_of((l, "kiT"))[:, 0:S])
                    for j, name in enumerate(projections(l)[-12:]):
                        src = two(bank_of((l, name)))
                        if name[0] == "q":
                            copy_out((l, name), q2[:, 2 * j:2 * j + 2, :], src, scale=-(DH ** -0.5))
                        elif name[0] == "k":
                            copy_out((l, name), k2[:, 2 * j - 8:2 * j - 6, :], src)
                        else:
                            copy_out((l, name), v2[:, :, (j - 8) * S:(j - 7) * S], src)
                        split_behind(act, (l, name), split_high)
                        if l == 2 and j < 8:
                            for i in (2 * j, 2 * j + 1):
                                key = (l, "I", i)
                                wait_full(act, key)
                                if i >= 2:
                                    act.wait_ge(relu_used, i - 1)
                                act.activation(relu[i % 2], bank_of(key)[:, 0:TRI], ACT.Relu,
                                               scale=DH ** -0.5).then_inc(*drained(key))
                    attention(l)
                    for half in range(2):
                        for tt in range(NT):
                            turned_high(act, (l, "oT", half, tt), a_hi[:, 4 * half:4 * half + 4, tt * P:(tt + 1) * P])
                for r in range(4):
                    split_behind(act, (l, f"out{r}"), split_high)
                mid, end = norm_after(l)
                rstd(mid)
                xT_out(mid)
                feed_forward(l)
                rstd(end)
                if end not in (3, 8):
                    xT_out(end)

        @block.vector
        def _(dve):
            step = steps(dve, dve_step)

            def level_product(l, v):
                n = l * (NLEV - 1) + v
                half = HALVES[v]
                dve.wait_ge(decay_done, n)
                if n > 2:
                    dve.wait_ge(product_done, l * NLEV + v - 1 if v > 2 else l * NLEV)
                d, o = blocks(dec[v % 2], half), blocks(lev[v % 2], half)
                dve.tensor_tensor(o[:, :, :half], d[:, :, :half], blocks(k_t, half)[:, :, :half], ALU.mult)
                dve.tensor_tensor(o[:, :, half:], d[:, :, half:], blocks(q_t, half)[:, :, half:],
                                  ALU.mult).then_inc(level_done, 1)

            def pick(l, v):
                dve.wait_ge(product_done, l * NLEV + v + 1)
                if v > 0:
                    dve.wait_ge(picked, l * NLEV + v)
                src = level_banks(v)
                if HALVES[v] == P:
                    dve.tensor_copy(s_cross, src[:, 0:512]).then_inc(picked, 1)
                else:
                    dve.copy_predicated(s_hg.rearrange("p (n t) -> p n t", t=P), bc_mid(hg_mask[:, v, :], 8),
                                        src.rearrange("p (n t) -> p n t", t=P)).then_inc(picked, 1)

            def after(l, name):
                for v in LEVELS_AFTER.get(name, ()):
                    pick(l, v)
                for v in PREP_AFTER.get(name, ()):
                    level_product(l, v)

            def attention(l):
                for s, t, _ in attention_steps():
                    if s is not None:
                        half, h, _, _, _, bh, indexed = attn_io(l, s)
                        key = (l, "S", s)
                        wait_full(dve, key)
                        if s >= 2:
                            dve.wait_ge(exp_done, l * HEADS + s - 1)
                        b, o = bank_of(key), lbuf[:, s % 2, :]
                        if l == 3 and s == 0:
                            dve.wait_ge(bias_log, 1)
                        if indexed:
                            dve.wait_ge(bias_sel, h + 1)
                            b1, b0 = bias_s[h % 2][:, 0:S], bias_s[h % 2][:, S:TRI]
                        else:
                            b1, b0 = bias_t[:, bh, :], bias_t[:, bh, P:S]
                        dve.tensor_tensor_reduce(o[:, 0:S], b[:, 0:S], b1, 1.0, 3e38, ALU.add, ALU.min,
                                                 mxn[:, half, 1, h:h + 1])
                        step(dve.tensor_tensor_reduce(o[:, S:TRI], b[:, S:TRI], b0, 1.0, 3e38, ALU.add, ALU.min,
                                                      mxn[:, half, 0, h:h + 1]))
                        dve.nop().then_inc(logit_done, 1)
                        dve.nop().then_inc(*drained(key))
                    if t is not None:
                        key = (l, "T", t)
                        wait_full(dve, key)
                        if t >= 2:
                            dve.wait_ge(pv_done, l * HEADS + t - 1)
                        dve.tensor_copy(pT[:, t % 2, :], bank_of(key)[:, 0:TRI]).then_inc(*drained(key))

            def res_tile(tt, half):
                return res[:, tt, half * 512:(half + 1) * 512].rearrange("p (h d) -> p h d", d=DH)

            def norm(n, l=None, second=False):
                for tt in range(NT):
                    st = nstat[:, tt, :]
                    if n != 4:
                        dve.wait_ge(acc_full, (2 * l + second) * NT + tt + 1)
                        acc = bank[:, 4 + 2 * tt:6 + 2 * tt, :].rearrange("p b c -> p (b c)")
                    if n < 4:
                        if n > 0:
                            dve.wait_ge(normed, (n - 1) * NT + tt + 1)
                        dve.scalar_tensor_tensor(res[:, tt, :], x[:, tt, :], ALPHA, acc, ALU.mult,
                                                 ALU.add).then_inc(acc_drained, 1)
                        dve.wait_ge(acc_drained, n * NT + tt + 1)
                        for i in range(2):
                            ins = dve.bn_stats(st[:, 6 * i:6 * i + 6], res[:, tt, i * 512:(i + 1) * 512])
                        step(ins)
                        dve.bn_aggr(st[:, 12:14], st[:, 0:12]).then_inc(sum_done, 1)
                    elif n > 4:
                        dve.tensor_tensor(x[:, tt, :], x[:, tt, :], acc, ALU.add).then_inc(acc_drained, 1)
                for tt in range(NT):
                    st = nstat[:, tt, :]
                    dve.wait_ge(rstd_done, n * NT + tt + 1)
                    if n < 4:
                        dve.wait_ge(gains_in, 2 * 16 * (n + 1))
                        step(dve.scalar_tensor_tensor(res[:, tt, :], res[:, tt, :], st[:, 12:13], gains[:, 0, :],
                                                      ALU.subtract, ALU.mult))
                        dve.scalar_tensor_tensor(x[:, tt, :], res[:, tt, :], st[:, 15:16], gains[:, 1, :], ALU.mult,
                                                 ALU.add).then_inc(normed, 1)
                    else:
                        dve.wait_ge(gains_in, 16 * (8 + n - 3))
                        dve.scalar_tensor_tensor(res[:, tt, :], x[:, tt, :], st[:, 15:16], gains[:, 0, :], ALU.mult,
                                                 ALU.mult).then_inc(normed, 1)

            def xT_out(n):
                for tt in range(NT):
                    for q in range(2):
                        part = (slice(None), slice(4 * q, 4 * q + 4), slice(tt * P, (tt + 1) * P))
                        turned_low(dve, (n, "xT", tt, q), a_lo[part], a_hi[part])

            def feed_forward(l):
                for kind, j in ffn_order():
                    if kind == "up":
                        up(l, j)
                    split_behind(dve, (l, f"{kind}{j}"), split_low)

            def up(l, j):
                key = (l, "up", j)
                b = bank_of(key)
                full = h_full[j % 2]
                if l < 2:
                    dve.wait_ge(act_gate, l * FT + j + 1)
                    dve.tensor_tensor(full, gate_a[j % 2], b[:, S:2 * S], ALU.mult).then_inc(*drained(key))
                    wait_drained(dve, key)
                else:
                    m = l - 2
                    dve.wait_ge(conv_in, m * FT + j + 1)
                    for tap in (1, 0):
                        lag = 2 - tap
                        for i, c in enumerate((cval[j % 2], cgate[j % 2])):
                            ins = dve.scalar_tensor_tensor(
                                c[:, lag:], b[:, i * S:(i + 1) * S - lag],
                                conv_col[:, m, i * FT + j, tap:tap + 1], c[:, lag:], ALU.mult, ALU.add)
                        if tap == 1:
                            step(ins)
                    ins.then_inc(conv_done, 1)
                    dve.wait_ge(conv_done, m * FT + j + 1)
                    dve.nop().then_inc(*drained(key))
                    dve.wait_ge(silu_done, m * FT + j + 1)
                    step(dve.tensor_tensor(full, gate_a[j % 2], cval[j % 2], ALU.mult))
                if j >= HSLOTS:
                    wait_used(dve, (l, f"down{(j - HSLOTS) // 2}"))
                step(dve.tensor_scalar(h_hi[:, j % HSLOTS, :], full, 1.0, None, ALU.mult))
                dve.tensor_tensor(h_lo[:, j % HSLOTS, :], full, h_hi[:, j % HSLOTS, :].bitcast(F32),
                                  ALU.subtract).then_inc(h_done, 1)

            dve.wait_ge(a_hi_done, 1)
            dve.tensor_tensor(a_lo[:, :, :], xT0, a_hi[:, :, :].bitcast(F32), ALU.subtract).then_inc(a_lo_done, 1)
            for i in range(PARTS):
                split_low(dve, i)
            key = ("cmpbias",)
            wait_full(dve, key)
            dve.wait_ge(start_in, 7 * 16)
            for tt in range(NT):
                src = bank_of(key)[:, tt * NC * 8:(tt + 1) * NC * 8].rearrange("p (n h) -> p h n", h=8)
                ins = dve.tensor_tensor(cmp_bias[:, tt, :, :], src, bc_mid(cmp_off[:, tt, :], 8), ALU.add)
            ins.then_inc(*drained(key))
            key = ("biasrow",)
            wait_full(dve, key)
            step(dve.tensor_tensor(bias_row[0:24, :], bank_of(key)[0:24, 0:REV], off_row[0:24, :], ALU.add))
            dve.nop().then_inc(bias_row_ready, 1)
            dve.nop().then_inc(*drained(key))
            dve.wait_ge(consts_in, CONSTS)
            step(dve.tensor_copy(hg_mask[:, :, :], mask_in))
            dve.tensor_tensor(lb_tmp[:, 0, :], lb[:, 1, :], lb[:, 0, :], ALU.subtract).then_inc(lb_ready, 1)
            dve.wait_ge(lb_ready, 2)
            step(dve.scalar_tensor_tensor(lb_log[:, 0, :], lb_tmp[:, 0, :], 0.0, lb_tmp[:, 3, :], ALU.min,
                                          ALU.subtract))
            step(dve.tensor_tensor(lb_log[:, 1, :], lb_log[:, 0, :], lb_tmp[:, 0, :], ALU.subtract))

            for l in range(LAYERS):
                if l < 2:
                    for i in range(2):
                        split_behind(dve, (l, f"hf{i}"), split_low)
                    dve.wait_ge(softplus_done, l + 1)
                    step(dve.scalar_tensor_tensor(b_t, f_t, 0.0, dec[0], ALU.min, ALU.subtract))
                    if l == 1:
                        step(dve.tensor_tensor(heads4(b_t), heads4(b_t), bc_last(lb_log[:, 1, :], S), ALU.add))
                        dve.tensor_tensor(heads4(dec[0]), heads4(b_t), bc_last(lb_log[:, 0, :], S),
                                          ALU.subtract).then_inc(gap_done, 1)
                    dve.tensor_tensor(k_t, b_t, f_t, ALU.subtract).then_inc(kdiff_done, 1)
                    if l == 1:
                        dve.wait_ge(kdiff_done, l + 1)
                        dve.wait_ge(softplus2_done, 1)
                        step(dve.tensor_tensor(heads4(b_t), heads4(b_t), bc_last(lb_log[:, 0, :], S), ALU.max))
                        step(dve.tensor_tensor(b_t, b_t, dec[0], ALU.add))
                    else:
                        dve.wait_ge(kdiff_done, l + 1)
                    dve.wait_ge(zeroed, 5)
                    for h in range(HG_HEADS):
                        ins = dve.tensor_tensor_scan(f_t[:, h * S:(h + 1) * S], ones[:, :], b_t[:, h * S:(h + 1) * S],
                                                     0.0, ALU.mult, ALU.add)
                    ins.then_inc(cumsum_done, 1)
                    dve.wait_ge(k_done, l + 1)
                    wait_drained(dve, (l, "hq0"))
                    wait_drained(dve, (l, "hq1"))
                    for name in ("hq0", "hq1", "hi0", "hi1"):
                        split_behind(dve, (l, name), split_low)
                    after(l, "hi1")
                    key = (l, "kcvc")
                    wait_full(dve, key)
                    for i in range(2):
                        for g in range(2):
                            for par in range(2):
                                at = i * S + par
                                full = bank_of(key)
                                base = full[g * DH:(g + 1) * DH, at:at + 1]
                                src = bass.AP(base.tensor, base.offset,
                                              [list(base.ap[0]), [2, CMP_KT], [16, NC]])
                                lo = par * DH
                                ins = dve.tensor_tensor(blk[i][lo:lo + DH, :, g, :], src,
                                                        bc_last(pos[lo:lo + DH, l, i, :], NC), ALU.add)
                    ins.then_inc(*drained(key))
                    for name in ("kcvc", "nq0", "nq1"):
                        split_behind(dve, (l, name), split_low)
                        after(l, name)
                    key = (l, "kcv")
                    wait_full(dve, key)
                    dve.tensor_copy(kc2[:, :, :].rearrange("p g n -> p (g n)"), bank_of(key)[:, 0:30])
                    dve.tensor_tensor(vc8[:, :, :], bc_mid(bank_of(key)[:, DH:2 * DH], 8),
                                      bc_last(head_blocks[:, :], DH), ALU.mult).then_inc(*drained(key))
                    for name in ("kskw", "vsvw"):
                        split_behind(dve, (l, name), split_low)
                        after(l, name)
                    wait_drained(dve, (l, "gt"))
                    gf = gates[:, :, :].rearrange("p t c -> p (t c)")
                    step(dve.tensor_scalar(gf, gf, 1.0, None, ALU.add))
                    step(dve.reciprocal(gf, gf))
                    after(l, "gt")
                    for odd in range(2):
                        key = (l, "cs", odd)
                        wait_full(dve, key)
                        src = bank_of(key)[:, 0:P].rearrange("p (t j n) -> p t j n", t=NT, j=4)[:, :, :, 0:NC]
                        for tt in range(NT):
                            ins = dve.tensor_tensor(cl[:, tt, odd::2, :], src[:, tt, :, :],
                                                    cmp_bias[:, tt, odd::2, :], ALU.add)
                        ins.then_inc(*drained(key))
                    wait_drained(dve, key)
                    c3 = cl[:, :, :, :].rearrange("p t h n -> p (t h) n")
                    e3 = ce[:, :, :, :].rearrange("p t h n -> p (t h) n")
                    step(dve.tensor_reduce(cmx[:, 0, :], c3, AX_X, ALU.min))
                    dve.tensor_tensor(c3, c3, bc_last(cmx[:, 0, :], NC), ALU.subtract).then_inc(cmp_logit, 1)
                    dve.wait_ge(cmp_exp, l + 1)
                    step(dve.tensor_reduce(cmx[:, 1, :], e3, AX_X, ALU.add))
                    step(dve.reciprocal(cmx[:, 1, :], cmx[:, 1, :]))
                    for tt in range(NT):
                        ins = dve.tensor_tensor(cmx[:, 2, 8 * tt:8 * tt + 8], cmx[:, 1, 8 * tt:8 * tt + 8],
                                                gates[:, tt, 0:8], ALU.mult)
                    step(ins)
                    step(dve.tensor_tensor(e3, e3, bc_last(cmx[:, 2, :], NC), ALU.mult))
                    for tt in range(NT):
                        ins = dve.tensor_tensor(cp[:, tt, :, 0:NC], ce[:, tt, :, :], bc_mid(cmp_on[:, tt, :], 8),
                                                ALU.mult)
                    ins.then_inc(cmp_prob, 1)
                    for name in ("hg0", "hg1"):
                        split_behind(dve, (l, name), split_low)
                        after(l, name)
                    for tt in range(NT):
                        dve.wait_ge(sq_done, l * NT + tt + 1)
                        ins = dve.tensor_reduce(stat[:, 4 * tt:4 * tt + 4],
                                                o_sq[tt].rearrange("p (h v) -> p h v", h=HG_HEADS), AX_X, ALU.add)
                    ins.then_inc(ssq_done, 1)
                    key = (l, "cT")
                    wait_full(dve, key)
                    dve.tensor_copy(cpT[:, :, :].rearrange("p t c -> p (t c)"),
                                    bank_of(key)[:, 0:2 * P]).then_inc(*drained(key))
                    dve.wait_ge(hg_rstd, l + 1)
                    dve.wait_ge(g_scaled, l + 1)
                    for tt in range(NT):
                        o3 = o_hg[tt].rearrange("p (h v) -> p h v", h=HG_HEADS)
                        step(dve.tensor_tensor(o3, o3, bc_last(stat[:, 8 + 4 * tt:12 + 4 * tt], P), ALU.mult))
                        dve.tensor_tensor(o_hg[tt], o_hg[tt], g_hg[:, tt, :], ALU.mult).then_inc(hg_out, 1)
                    for tt in range(NT):
                        part = (slice(None), slice(0, 4), slice(tt * P, (tt + 1) * P))
                        turned_low(dve, (l, "hoT", tt), a_lo[part], a_hi[part])
                    for tt in range(NT):
                        key = (l, "co", tt)
                        wait_full(dve, key)
                        dve.tensor_copy(res[:, tt, 0:512], bank_of(key)).then_inc(*drained(key))
                    attention(l)
                    dve.wait_ge(exp_done, (l + 1) * HEADS)
                    sums = esum[:, :, :, :].rearrange("p a t h -> p (a t h)")
                    wf = wgt[:, :, :, :].rearrange("p a t h -> p (a t h)")
                    step(dve.reciprocal(wf, sums))
                    for half in range(2):
                        ins = dve.tensor_tensor(wgt[:, half, :, :], wgt[:, half, :, :],
                                                gates[:, :, 8 + 8 * half:16 + 8 * half], ALU.mult)
                    step(ins)
                    dve.wait_ge(pv_done, (l + 1) * HEADS)
                    for half in range(2):
                        for tt in range(NT):
                            ps = bank[:, 4 + 2 * half + tt, :].rearrange("p (h d) -> p h d", d=DH)
                            step(dve.tensor_tensor(res_tile(tt, 1), ps, bc_last(wgt[:, half, tt, :], DH), ALU.mult))
                            if half == 0:
                                dve.nop().then_inc(mix_done, 1)
                            ins = dve.tensor_tensor(res[:, tt, 0:512], res[:, tt, 0:512], res[:, tt, 512:1024],
                                                    ALU.add)
                            step(ins) if half == 0 else ins.then_inc(mix_done, 1)
                    for tt in range(NT):
                        part = (slice(None), slice(4, 8), slice(tt * P, (tt + 1) * P))
                        turned_low(dve, (l, "oT", 1, tt), a_lo[part], a_hi[part])
                else:
                    if l == 2:
                        norm(4)
                        xT_out(4)
                        pass
                        dve.wait_ge(ki_rstd, 1)
                        for tt in range(NT):
                            step(dve.tensor_scalar(gates[:, tt, 0:16], small[:, tt, DH:80], 16.0 ** -0.5, None, ALU.mult))
                            step(dve.scalar_tensor_tensor(small[:, tt, 0:DH], small[:, tt, 0:DH],
                                                          stat[:, 4 + tt:5 + tt], idx_norm[:, :], ALU.mult, ALU.mult))
                            dve.tensor_copy(small[:, tt, DH:2 * DH], small[:, tt, 0:DH]).then_inc(ki_normed, 1)
                        for j in range(4):
                            split_behind(dve, (l, f"qi{j}"), split_low)
                        step(dve.tensor_copy(score, causal[:, :]))
                        for i in range(16):
                            if i % 2 == 0:
                                split_behind(dve, (l, projections(l)[4 + i // 2]), split_low)
                            wait_drained(dve, (l, "I", i))
                            if i > 0:
                                dve.wait_ge(relu_used, i)
                            r = relu[i % 2]
                            dve.scalar_tensor_tensor(score[:, 0:S], r[:, 0:S], gates[:, 1, i:i + 1], score[:, 0:S],
                                                     ALU.mult, ALU.add)
                            dve.scalar_tensor_tensor(score[:, S:TRI], r[:, S:TRI], gates[:, 0, i:i + 1],
                                                     score[:, S:TRI], ALU.mult, ALU.add).then_inc(relu_used, 1)
                        dve.wait_ge(relu_used, 16)
                        for n, part in enumerate((score[:, 0:S], score[:, S:TRI])):
                            for i in range(TOPK // 8):
                                if i % 4 == 0:
                                    split_behind(dve, (l, projections(l)[12 + 2 * n + i // 4]), split_low)
                                step(dve.max(stat[:, 8:16], part))
                                step(dve.match_replace(part, stat[:, 8:16], part, TAKEN))
                        dve.tensor_scalar(unsel, score, 1.5 * NEG, -NEG, ALU.is_gt, ALU.mult).then_inc(unsel_done, 1)
                    else:
                        for name in projections(l):
                            split_behind(dve, (l, name), split_low)
                    attention(l)
                    dve.wait_ge(exp_done, (l + 1) * HEADS)
                    step(dve.reciprocal(wgt[:, :, :, :].rearrange("p a t h -> p (a t h)"),
                                        esum[:, :, :, :].rearrange("p a t h -> p (a t h)")))
                    dve.wait_ge(pv_done, (l + 1) * HEADS)
                    for half in range(2):
                        for tt in range(NT):
                            ps = bank[:, 4 + 2 * half + tt, :].rearrange("p (h d) -> p h d", d=DH)
                            dve.tensor_tensor(res_tile(tt, half), ps, bc_last(wgt[:, half, tt, :], DH),
                                              ALU.mult).then_inc(mix_done, 1)
                    for half in range(2):
                        for tt in range(NT):
                            part = (slice(None), slice(4 * half, 4 * half + 4), slice(tt * P, (tt + 1) * P))
                            turned_low(dve, (l, "oT", half, tt), a_lo[part], a_hi[part])
                for r in range(4):
                    split_behind(dve, (l, f"out{r}"), split_low)
                mid, end = norm_after(l)
                norm(mid, l)
                xT_out(mid)
                feed_forward(l)
                norm(end, l, second=True)
                if end not in (3, 8):
                    xT_out(end)

        @block.gpsimd
        def _(pool):
            step = steps(pool, pool_step)
            pool.memset(s_hg, 0.0).then_inc(zeroed, 1)
            pool.memset(hid_v[:, :, :], 0.0).then_inc(zeroed, 1)
            pool.memset(cp[:, :, :, :], 0.0).then_inc(zeroed, 1)
            pool.memset(ones[:, :], 1.0).then_inc(zeroed, 1)
            pool.memset(eps_ln[:, :], 1e-5)
            pool.memset(eps_rms[:, :], 1e-6).then_inc(zeroed, 1)

            def load_gains(g, b):
                pool.dma_start(gains[:, 0, :], g.partition_broadcast(P)).then_inc(gains_in, 16)
                if b is not None:
                    pool.dma_start(gains[:, 1, :], b.partition_broadcast(P)).then_inc(gains_in, 16)

            def next_gains(n, g, b=None):
                pool.wait_ge(normed, n * NT)
                load_gains(g, b)

            load_gains(a["ln1_g"][0], a["ln1_b"][0])
            for l in range(2):
                pool.wait_ge(cumsum_done, l + 1)
                for v in range(1, NLEV):
                    n = l * (NLEV - 1) + v
                    half = HALVES[v]
                    if v > 2:
                        pool.wait_ge(level_done, n - 2)
                    src = blocks(f_t, half)
                    mid = src[:, :, half - 1:half].to_broadcast([P, D // (2 * half), 2 * half])
                    pool.tensor_tensor(blocks(dec[v % 2], half), src, mid, ALU.subtract).then_inc(diff_done, 1)
                for i in range(2):
                    wait_drained(pool, (l, f"hg{i}"))
                for tt in range(NT):
                    g3 = g_hg[:, tt, :].rearrange("p (h v) -> p h v", h=HG_HEADS)
                    ins = pool.tensor_tensor(g3, g3, bc_mid(gnorm[:, l, :], HG_HEADS), ALU.mult)
                ins.then_inc(g_scaled, 1)
                for tt in range(NT):
                    wait_drained(pool, (l, "ho", tt))
                    pool.tensor_tensor(o_sq[tt], o_hg[tt], o_hg[tt], ALU.mult).then_inc(sq_done, 1)
                next_gains(2 * l + 1, a["ln2_g"][l], a["ln2_b"][l])
                if l == 0:
                    next_gains(2, a["ln1_g"][1], a["ln1_b"][1])
            next_gains(4, a["rms_g"][0])
            pool.dma_start(w_idx, a["w_idx"]).then_inc(w_idx_in, 16)
            next_gains(5, a["rms_g"][1])
            pool.wait_ge(unsel_done, 1)
            for h in range(8):
                if h >= 2:
                    pool.wait_ge(logit_done, 2 * HEADS + 8 + h - 1)
                o = bias_s[h % 2]
                pool.tensor_tensor(o[:, 0:S], bias_t[:, 16 + h, :], unsel[:, 0:S], ALU.add)
                pool.tensor_tensor(o[:, S:TRI], bias_t[:, 16 + h, P:S], unsel[:, S:TRI],
                                   ALU.add).then_inc(bias_sel, 1)
            next_gains(6, a["rms_g"][2])
            next_gains(7, a["rms_g"][3])
            pool.wait_ge(logit_done, 3 * HEADS)
            pool.wait_ge(consts_in, CONSTS)
            for h in range(16):
                ins = pool.tensor_tensor(bias_t[:, 8 + h, :], bias_t[:, 8 + h, :],
                                         neglog[:, :, :].rearrange("p t s -> p (t s)"), ALU.add)
            ins.then_inc(bias_log, 1)
            next_gains(8, a["final_g"])


def bucket(dist):
    n = np.maximum(dist, 0)
    exact = BUCKETS // 2
    nf = np.maximum(n, 1).astype(np.float32)
    large = exact + (np.log(nf / np.float32(exact)) / np.float32(np.log(128 / exact))
                     * np.float32(BUCKETS - exact)).astype(np.int32)
    return np.where(n < exact, n, np.minimum(large, BUCKETS - 1))


def constants():
    f = np.float32
    p = np.arange(P)
    rev = S - 1 - np.arange(REV)
    one_hot = -((bucket(rev)[None, :] == np.arange(BUCKETS)[:, None]) & (rev >= 0)).astype(f)
    dc = np.arange(2 * S) - (S - 1)
    one_hot_c = -((bucket(dc)[None, :] == np.arange(BUCKETS)[:, None]) & (dc >= 0)).astype(f)
    off_row = np.broadcast_to(np.where(rev >= 0, 0.0, -NEG).astype(f), (24, REV)).copy()
    masks = np.zeros((P, len(HALVES), P), np.float32)
    for v, half in enumerate(HALVES):
        if half == 0:
            masks[:, v, :] = np.eye(P, dtype=np.float32)
        elif half < P:
            same = (p[:, None] // (2 * half)) == (p[None, :] // (2 * half))
            masks[:, v, :] = same & (p[:, None] % (2 * half) < half) & (p[None, :] % (2 * half) >= half)
    t = np.arange(S).reshape(NT, P).T
    done = (np.arange(NC) * 16 + 31)[None, None, :] <= t[:, :, None]
    s = np.arange(S)
    causal = np.concatenate([np.where(s[None, :] <= P + p[:, None], 0.0, NEG),
                             np.where(s[None, :P] <= p[:, None], 0.0, NEG)], axis=1)
    dist = P + p[:, None] - s[None, :]
    count = ((dist >= 0) & (dist <= P)).astype(int) + ((dist >= 0) & (dist % 4 == 0)) + ((dist >= 0) & (dist % 16 == 0))
    log_count = np.where(count > 0, -np.log(np.maximum(count, 1)), -NEG)
    return {
        "one_hot": one_hot, "one_hot_c": one_hot_c, "off_row": off_row, "ident": np.eye(P, dtype=f),
        "flip": np.eye(P, dtype=f)[::-1].copy(), "hg_mask": masks,
        "cmp_off": np.where(done, 0.0, -NEG).astype(f), "cmp_on": done.astype(f),
        "head_blocks": (p[:, None] // NCP == np.arange(8)[None, :]).astype(f),
        "causal": causal.astype(f), "neglog": log_count.astype(f).reshape(P, NT, P),
    }


def col_tile(w):
    return w.reshape(KT, P, S).transpose(1, 0, 2).reshape(P, TILE)


def row_tile(w):
    return w.reshape(2, P, D).transpose(1, 0, 2).reshape(P, TILE)


def layout(i):
    cols = {}
    for l in range(2):
        w = i["w_in"][l]
        at = dict(zip(("hq", "hf", "hi", "hg", "nq", "kc", "vc", "ks", "vs", "kw", "vw", "gt"),
                      (0, 512, 1024, 1536, 2048, 2560, 2688, 2816, 2944, 3072, 3200, 3328)))
        for n in ("hq", "hf", "hi", "hg", "nq"):
            for j in range(2):
                cols[(l, f"{n}{j}")] = col_tile(w[:, at[n] + S * j:at[n] + S * (j + 1)])
        for n in ("kcvc", "kskw", "vsvw"):
            cols[(l, n)] = col_tile(np.concatenate([w[:, at[n[:2]]:at[n[:2]] + P], w[:, at[n[2:]]:at[n[2:]] + P]], 1))
        for n, src in (("w1k", "cmp_w1_k"), ("w1v", "cmp_w1_v")):
            cols[(l, n)] = i[src][l].reshape(CMP_KT, P, P).transpose(1, 0, 2).reshape(P, TILE)
        for j in range(FT):
            c = slice(j * P, (j + 1) * P)
            cols[(l, f"up{j}")] = col_tile(np.concatenate([i["w_ffn_gate"][l][:, c], i["w_ffn_up"][l][:, c]], 1))
        for r in range(4):
            cols[(l, f"out{r}")] = row_tile(i["w_out"][l][r * S:(r + 1) * S])
        for r in range(FT // 2):
            cols[(l, f"down{r}")] = row_tile(i["w_ffn_down"][l][r * S:(r + 1) * S])
    e, o = i["w_in_even_2"][0], i["w_in_odd_2"][0]
    for l, w, starts in ((2, e, {"q": (0, 1536), "k": (512, 2048), "v": (1024, 2560)}),
                         (3, o, {"q": (0, 512), "k": (1024, 1536), "v": (2048, 2560)})):
        for n, (a, b) in starts.items():
            for j in range(4):
                c = (a, b)[j // 2] + S * (j % 2)
                cols[(l, f"{n}{j}")] = col_tile(w[:, c:c + S])
        for j in range(FT):
            v = i["w_up_2"][l - 2]
            cols[(l, f"up{j}")] = col_tile(np.concatenate([v[:, j * P:(j + 1) * P],
                                                           v[:, DFF + j * P:DFF + (j + 1) * P]], 1))
        for r in range(4):
            cols[(l, f"out{r}")] = row_tile(i["w_o_2"][l - 2][r * S:(r + 1) * S])
        for r in range(FT // 2):
            cols[(l, f"down{r}")] = row_tile(i["w_down_2"][l - 2][r * S:(r + 1) * S])
    for j in range(4):
        cols[(2, f"qi{j}")] = col_tile(e[:, 3072 + S * j:3072 + S * (j + 1)])

    x = i["x"][0]
    taps = np.concatenate([i["conv_w_2"], i["conv_b_2"][:, None, :]], 1)
    w2k, w2v = i["cmp_w2_k"], i["cmp_w2_v"]
    p2 = np.stack([i["cmp_pos_k"], i["cmp_pos_v"]], 1)
    d = {
        "stream": np.stack([cols[k] for k in stream_order()]),
        "xT": x.T.reshape(KT, P, S).transpose(1, 0, 2), "x": x.reshape(NT, P, D).transpose(1, 0, 2),
        "rel": np.concatenate([i["rel_bias"], i["rel_bias_2"]], 1),
        "lb": i["hg_lb_param"].reshape(2, HG_HEADS, P).transpose(2, 0, 1),
        "gnorm": np.broadcast_to(i["hg_norm_w"][None], (P, 2, P)),
        "idx_norm": np.broadcast_to(i["idx_k_norm_2"], (P, DH)),
        "pos": p2.reshape(2, 2, CMP_KT, 2, DH).transpose(3, 4, 0, 1, 2).reshape(P, 2, 2, CMP_KT),
        "w2": np.concatenate([w2k, w2k, w2v], 2).transpose(1, 0, 2),
        "w_gate": i["w_in"][:, :, 3328:3352].reshape(2, KT, P, 24).transpose(2, 0, 1, 3),
        "w_idx": e[:, 4096:4176].reshape(KT, P, 80).transpose(1, 0, 2),
        "rms_g": np.stack([i["attn_norm_2"][0], i["ffn_norm_2"][0], i["attn_norm_2"][1], i["ffn_norm_2"][1]]),
        "conv_col": taps.reshape(2, 4, 2 * FT, P).transpose(3, 0, 2, 1),
        "ln1_g": i["ln1_g"], "ln1_b": i["ln1_b"], "ln2_g": i["ln2_g"], "ln2_b": i["ln2_b"],
        "final_g": i["final_norm_2"],
    }
    d.update(constants())
    return {k: np.ascontiguousarray(v) for k, v in d.items()}


def kernel(**inputs):
    import concourse.bacc as bacc
    from concourse.bass_utils import run_bass_kernel_spmd

    arrays = layout({k: np.asarray(v) for k, v in inputs.items()})
    nc = bacc.Bacc("TRN2", target_bir_lowering=False, num_devices=1)
    args = {k: nc.dram_tensor(f"in_{k}", v.shape, mybir.dt.from_np(v.dtype), kind="ExternalInput").ap()
            for k, v in arrays.items()}
    args["out"] = nc.dram_tensor("out", (P, NT, D), F32, kind="ExternalOutput").ap()
    build(nc, args)
    r = run_bass_kernel_spmd(nc, [{f"in_{k}": v for k, v in arrays.items()}], core_ids=[0])
    return r.results[0]["out"].transpose(1, 0, 2).reshape(1, S, D)
```

```python
from contextlib import ExitStack

import numpy as np
import concourse.bass as bass
from concourse import mybir

ALU = mybir.AluOpType
ACT = mybir.ActivationFunctionType
AX_X = mybir.AxisListType.X
F32 = mybir.dt.float32
F32R = mybir.dt.float32r
U8 = mybir.dt.uint8

P = 128
S = 256
NT = S // P
D = 1024
KT = D // P
DFF = 2816
FT = DFF // P
LAYERS = 4
PIECES = 2 * NT
TILE = 2048
SLOTS = 3
PARTS = 3
HSLOTS = 6
HEAD = 2
TAIL = 3
RING = 4
ALPHA = 4.0 ** 0.25
HG_HEADS = 4
HEADS = 16
DH = 64
NC = 15
NCP = 16
CMP_KT = 16
NEG = -1e30
TAKEN = -2e30
TOPK = 64
ARENA = 12288
BUCKETS = 32
BIAS_READS = 6
REV = S + P - 1
CB = 4
CG = (NC + CB - 1) // CB
LBUFS = 3
HALVES = [0, 128, 64, 32, 16, 8, 4, 2, 1]
TRI = S + P


def projections(l):
    if l < 2:
        return ["hi0", "hi1", "hf0", "hf1", "hq0", "hq1", "kcvc", "nq0", "nq1", "w1k", "w1v", "kskw",
                "hg0", "hg1", "vsvw"]
    if l == 2:
        return ["v0", "v1"] + [f"qi{j}" for j in range(4)] + attention_tiles()
    return ["v0", "v1"] + attention_tiles()


def attention_tiles():
    return [f"q{j}" for j in range(4)] + [f"k{j}" for j in range(4)] + ["v2", "v3"]


def ffn_order():
    order = []
    for r in range(FT // 2):
        order += [("up", 2 * r), ("up", 2 * r + 1)]
        if 1 <= r <= FT // 2 - TAIL:
            order.append(("down", r - 1))
    return order + [("down", FT // 2 - 3 + i) for i in range(TAIL)]


def stream_order():
    order = []
    for l in range(LAYERS):
        order += [(l, name) for name in projections(l)]
        order += [(l, f"out{r}") for r in range(4)]
        order += [(l, f"{kind}{j}") for kind, j in ffn_order()]
    return order


def attention_steps():
    for i in range(HEADS + 3):
        yield (i if i < HEADS else None, i - 2 if 0 <= i - 2 < HEADS else None, i - 3 if i >= 3 else None)


def bank_order(closing=False):
    uses = [(0, "hi0"), (0, "hi1"), ("cmpbias",), ("biasrow",)]
    for l in range(LAYERS):
        def attention():
            out = []
            for s, t, _ in attention_steps():
                out += [(l, "S", s)] if s is not None else []
                out += [(l, "T", t)] if t is not None else []
            return out
        if l < 2:
            names = projections(l)
            uses += [(l, n) for n in names[HEAD:names.index("w1k")]]
            uses += [(l, n) for n in ("hid", "kskw", "gt", "kcv", "hg0", "gtT")] + [(l, "cs", 0), (l, "cs", 1)]
            uses += [(l, "hg1"), (l, "vsvw"), (l, "cT"), (l, "ho", 0), (l, "ho", 1), (l, "co", 0), (l, "co", 1)]
            uses += attention() + [(l, "hoT", 0), (l, "hoT", 1), (l, "oT", 1, 0), (l, "oT", 1, 1)]
        elif l == 2:
            uses += [(l, n) for n in ("kw", "qi0", "kwT", "qi1", "qi2", "qi3", "kiT")]
            for j, name in enumerate(attention_tiles()):
                uses += [(l, name)] + [(l, "I", i) for i in index_heads(j)]
            uses += attention() + [(l, "oT", a, tt) for a in range(2) for tt in range(NT)]
        else:
            uses += [(l, n) for n in projections(l)[HEAD:]]
            uses += attention() + [(l, "oT", a, tt) for a in range(2) for tt in range(NT)]
        mid, end = norm_after(l)
        uses += behind_norm(mid, [(l, "head", j) for j in range(HEAD)], closing)
        uses += [(l, "up", j) for j in [HEAD] + list(range(HEAD)) + list(range(HEAD + 1, FT))]
        if l < LAYERS - 1:
            uses += behind_norm(4 if end == 3 else end, [(l + 1, name) for name in projections(l + 1)[:HEAD]],
                                closing)
    return uses


def index_heads(j):
    return range(3 * j, min(3 * j + 3, 16))


def behind_norm(n, heads, closing):
    first, second = [[(n, "xT", tt, q) for q in range(2)] for tt in range(NT)]
    return first + (second + heads if closing else heads + second)


def tail(l, kind):
    last = 3 if kind == "out" else FT // 2 - 1
    return [(l, f"{kind}{j}") for j in range(last - TAIL + 1, last + 1)]


def norm_after(l):
    return {0: (0, 1), 1: (2, 3), 2: (5, 6), 3: (7, 8)}[l]


def unsplit(key):
    return key[1] in ("w1k", "w1v")


POOL_AFTER = ["kcvc", "nq1", "kskw", "hg0"]


def turned(key):
    return key[1:2] in (("xT",), ("oT",), ("hoT",))


def build(nc, a):
    stream = stream_order()
    tile_no = {key: i for i, key in enumerate(stream)}
    full_no = {key: i for i, key in enumerate(bank_order(closing=True))}
    bank_no = {key: i for i, key in enumerate(bank_order())}
    split_tiles = [key for key in stream if not unsplit(key)]
    split_no = {key: i for i, key in enumerate(split_tiles)}
    on_pool = {split_no[tail(l, kind)[i]] + PARTS for l in range(LAYERS) for kind in ("out", "down") for i in (0, 2)}
    on_pool |= {split_no[(l, n)] + PARTS for l in range(2) for n in POOL_AFTER}
    turned_no = {key: i for i, key in enumerate(k for k in bank_order() if turned(k))}
    assert len(bank_no) == len(bank_order()) and len(tile_no) == len(stream)

    with ExitStack() as ctx:
        def sb(name, shape, dt=F32):
            return ctx.enter_context(nc.sbuf_tensor(name, shape, dt))

        def sem(name):
            return ctx.enter_context(nc.semaphore(name))

        bank = ctx.enter_context(nc.psum_tensor("bank", [P, 8, 512], F32))

        raw = sb("raw", [P, SLOTS, TILE])
        w_hi = sb("w_hi", [P, PARTS, TILE], F32R)
        w_lo = sb("w_lo", [P, PARTS, TILE], F32R)
        x = sb("x", [P, NT, D])
        res = sb("res", [P, NT, D])
        a_hi = sb("a_hi", [P, KT, S], F32R)
        a_lo = sb("a_lo", [P, KT, S], F32R)
        gains = sb("gains", [P, 2, D])
        bias_t = sb("bias_t", [P, 24, S])
        lbuf = sb("lbuf", [P, LBUFS, TRI])
        pT = sb("pT", [P, 2, TRI])
        ident = sb("ident", [P, P])
        hg_mask = sb("hg_mask", [P, len(HALVES), P], U8)
        cmp_bias = sb("cmp_bias", [P, NT, 8, NC])
        cmp_off = sb("cmp_off", [P, NT, NC])
        cmp_on = sb("cmp_on", [P, NT, NC])
        head_blocks = sb("head_blocks", [P, 8])
        lb = sb("lb", [P, 2, HG_HEADS])
        lb_log = sb("lb_log", [P, 2, HG_HEADS])
        lb_tmp = sb("lb_tmp", [P, 4, HG_HEADS])
        gnorm = sb("gnorm", [P, 2, P])
        pos = sb("pos", [P, 2, 2, CMP_KT])
        w2 = sb("w2", [P, 2, 192])
        w_gate = [sb(f"w_gate_{part}", [P, 2, KT, 24], F32R) for part in ("hi", "lo")]
        idx_norm = sb("idx_norm", [P, DH])
        conv_col = sb("conv_col", [P, 2, 2 * FT, 4])
        mxn = sb("mxn", [P, 2, NT, 8])
        esum = sb("esum", [P, 2, NT, 8])
        wgt = sb("wgt", [P, 2, NT, 8])
        stat = sb("stat", [P, 16])
        nstat = sb("nstat", [P, NT, 20])
        small = sb("small", [P, NT, 128])
        gates = sb("gates", [P, NT, 24])
        cmx = sb("cmx", [P, 3, NT * 8])
        ones = sb("ones", [P, S])
        eps_ln = sb("eps_ln", [P, 1])
        eps_rms = sb("eps_rms", [P, 1])
        hid = sb("hid", [P, 30])
        hid_v = sb("hid_v", [P, 8, NCP])
        kc2 = sb("kc2", [P, 2, NC])
        cp = sb("cp", [P, NT, 8, NCP])
        with nc.sbuf_tensor("arena", [P, ARENA], F32) as arena:
            pass
        h_hi = sb("h_hi", [P, HSLOTS, S], F32R)
        h_lo = sb("h_lo", [P, HSLOTS, S], F32R)
        sb("between", [P, ARENA - 2 * HSLOTS * S - 2 * KT * 80])
        w_idx = [sb(f"w_idx_{part}", [P, KT, 80], F32R) for part in ("hi", "lo")]

        used = [0]

        def take(n):
            used[0] += n
            assert used[0] <= ARENA, used
            return arena[:, used[0] - n:used[0]]

        f_t, q_t, k_t, dec0, dec1, lev0, lev1 = [take(D) for _ in range(7)]
        dec, lev = [dec0, dec1], [lev0, lev1]
        b_t = dec1
        s_cross = take(512)
        v_hg = take(D).rearrange("p (t c) -> p t c", t=NT)
        g_hg = f_t.rearrange("p (t c) -> p t c", t=NT)
        nq = take(D).rearrange("p (j t) -> p j t", j=4)
        ks2 = take(512).rearrange("p (g t) -> p g t", g=2)
        kw2 = take(512).rearrange("p (g t) -> p g t", g=2)
        v_sw = take(512).rearrange("p (t c) -> p t c", t=NT)
        s_hg = take(D)
        blk = [b[:, :, :].rearrange("p j t -> p (j t)")[:, 0:CMP_KT * 30].rearrange(
            "p (k g n) -> p k g n", k=CMP_KT, g=2) for b in (lbuf, pT)]
        o_hg = [dec[0][:, 0:512], dec[0][:, 512:1024]]
        o_sq = [dec[1][:, 0:512], dec[1][:, 512:1024]]
        vc8 = res[:, 0, 512:1024].rearrange("p (h d) -> p h d", d=DH)
        cl = res[:, 0, 0:NT * 8 * NC].rearrange("p (t h n) -> p t h n", t=NT, h=8)
        ce = res[:, 1, 0:NT * 8 * NC].rearrange("p (t h n) -> p t h n", t=NT, h=8)
        cpT = res[:, 1, 512:512 + 2 * P].rearrange("p (t c) -> p t c", t=NT)
        used[0] = 0
        take(2 * HSLOTS * S)
        h_full = [take(S) for _ in range(2)]
        gate_a = [take(S) for _ in range(2)]
        cval = [take(S) for _ in range(2)]
        cgate = [take(S) for _ in range(2)]
        used[0] += D
        head_rows = [take(2 * S) for _ in range(HEAD)]
        neglog = take(S)
        used[0] = 0
        q2 = take(8 * S).rearrange("p (j t) -> p j t", j=8)
        k2 = take(8 * S).rearrange("p (j t) -> p j t", j=8)
        v2 = take(2 * D).rearrange("p (t c) -> p t c", t=NT)
        qi = take(8 * S).rearrange("p (j t) -> p j t", j=8)
        kiT = take(S)
        score = take(TRI)
        relu = [take(TRI) for _ in range(2)]
        unsel = take(TRI)
        bias_s = [take(TRI) for _ in range(2)]
        w_idx_in = arena[:, 9216:9216 + KT * 80].rearrange("p (k c) -> p k c", k=KT)
        kw_rows = bias_s[0][0:80, 0:S]
        gate_rows = small[0:24, :, :].rearrange("p t c -> p (t c)")
        gain4 = arena[:, 5120:5120 + D]
        used[0] = 0
        mask_in = arena[:, 5 * D:5 * D + len(HALVES) * P].rearrange("p (v s) -> p v s", v=len(HALVES))
        xT0 = res[:, :, :].rearrange("p t c -> p (t c)").rearrange("p (k t) -> p k t", k=KT)
        used[0] = 8 * D + 512
        one_hot = take(REV)
        one_hot_c = take(2 * S)
        rel = take(24)
        rel_c = take(CB * 8)
        off_row = take(REV)
        bias_row = take(REV)
        w_gate_in = take(2 * KT * 24).rearrange("p (l k c) -> p l k c", l=2, k=KT)
        scratch = nc.dram_tensor("bias_rows", (24, REV), F32, kind="Internal").ap()

        tile_loaded = [sem(f"tile_loaded{i}") for i in range(SLOTS)]
        rows_used = sem("rows_used")
        w_hi_done = sem("w_hi_done")
        w_lo_done = sem("w_lo_done")
        w_lo_pool = sem("w_lo_pool")
        a_hi_done = sem("a_hi_done")
        a_lo_done = sem("a_lo_done")
        w_idx_loaded = sem("w_idx_loaded")
        w_idx_split = sem("w_idx_split")
        score_in = sem("score_in")
        neglog_in = sem("neglog_in")
        w_gate_split = sem("w_gate_split")
        bank_full = sem("bank_full")
        bank_drained = [sem(f"bank_drained{i}") for i in range(RING)]
        consts_in = sem("consts_in")
        start_in = sem("start_in")
        x_in = sem("x_in")
        rows_out = sem("rows_out")
        x_rows_in = sem("x_rows_in")
        bias_in = sem("bias_in")
        zeroed = sem("zeroed")
        lb_ready = sem("lb_ready")
        act_step = sem("act_step")
        dve_step = sem("dve_step")
        pool_step = sem("pool_step")
        bias_row_ready = sem("bias_row_ready")
        softplus_done = sem("softplus_done")
        gap_done = sem("gap_done")
        softplus2_done = sem("softplus2_done")
        kdiff_done = sem("kdiff_done")
        k_done = sem("k_done")
        cumsum_done = sem("cumsum_done")
        diff_done = sem("diff_done")
        decay_done = sem("decay_done")
        level_done = sem("level_done")
        product_done = sem("product_done")
        picked = sem("picked")
        cmp_logit = sem("cmp_logit")
        cmp_exp = sem("cmp_exp")
        cmp_prob = sem("cmp_prob")
        g_scaled = sem("g_scaled")
        hg_rstd = sem("hg_rstd")
        logit_done = sem("logit_done")
        exp_done = sem("exp_done")
        pv_done = sem("pv_done")
        mix_done = sem("mix_done")
        acc_full = sem("acc_full")
        acc_drained = sem("acc_drained")
        sum_done = sem("sum_done")
        root_done = sem("root_done")
        normed = sem("normed")
        gains_in = sem("gains_in")
        gain4_in = sem("gain4_in")
        act_gate = sem("act_gate")
        conv_in = sem("conv_in")
        conv_done = sem("conv_done")
        silu_done = sem("silu_done")
        h_done = sem("h_done")
        ki_rstd = sem("ki_rstd")
        ki_normed = sem("ki_normed")
        relu_used = sem("relu_used")
        unsel_done = sem("unsel_done")
        bias_sel = sem("bias_sel")
        bias_log = sem("bias_log")
        out_sem = sem("stored")

        def bank_of(key):
            return bank[:, bank_no[key] % RING, :]

        def wait_full(eng, key):
            eng.wait_ge(bank_full, full_no[key] + 1)

        def wait_drained(eng, key):
            eng.wait_ge(bank_drained[bank_no[key] % RING], bank_no[key] // RING + 1)

        def drained(key):
            return bank_drained[bank_no[key] % RING], 1

        def steps(eng, s):
            n = [0]

            def step(ins):
                n[0] += 1
                ins.then_inc(s, 1)
                eng.wait_ge(s, n[0])
            return step

        def wait_used(eng, key):
            l, name = key
            kind = name.rstrip("0123456789")
            number = int(name[len(kind):] or 0)
            if kind in ("out", "down"):
                if number == {"out": 3, "down": FT // 2 - 1}[kind]:
                    eng.wait_ge(acc_full, (2 * l + (kind == "down") + 1) * PIECES)
                else:
                    eng.wait_ge(rows_used, l * (3 + FT // 2 - 1) + number + 1 + 3 * (kind == "down"))
            elif kind == "up":
                wait_full(eng, (l, "up" if number >= HEAD else "head", number))
            else:
                wait_full(eng, (l, "hid") if unsplit(key) else key)

        def half_tile(i):
            return slice(i * (TILE // 2), (i + 1) * (TILE // 2))

        def piece(tt, hf):
            return 2 * tt + hf + 1

        def half_rows(hf):
            return slice(hf * 512, (hf + 1) * 512)

        def normed_by(n, tt, hf):
            if n in (3, 4):
                return 3 * PIECES + 4 * tt + 2 * (n - 3) + hf + 1
            return n * PIECES + piece(tt, hf)

        def sum_done_at(n, tt):
            return 3 * NT + 2 * tt + n - 2 if n in (3, 4) else n * NT + tt + 1

        def sum_of(n):
            return n if n < 4 else n - 1

        def split_high(act, i):
            key = split_tiles[i]
            t = tile_no[key]
            act.wait_ge(tile_loaded[t % SLOTS], 16 * (t // SLOTS + 1))
            if i >= PARTS:
                wait_used(act, split_tiles[i - PARTS])
            for h in range(2):
                act.activation(w_hi[:, i % PARTS, half_tile(h)], raw[:, t % SLOTS, half_tile(h)],
                               ACT.Copy).then_inc(w_hi_done, 1)

        def wait_split(eng, i):
            mine = i in on_pool
            count = sum((j in on_pool) == mine for j in range(i + 1))
            eng.wait_ge(w_lo_pool if mine else w_lo_done, 2 * count)

        def take_rest(eng, i, done):
            t = tile_no[split_tiles[i]]
            for h in range(2):
                eng.wait_ge(w_hi_done, 2 * i + h + 1)
                eng.tensor_tensor(w_lo[:, i % PARTS, half_tile(h)], raw[:, t % SLOTS, half_tile(h)],
                                  w_hi[:, i % PARTS, half_tile(h)].bitcast(F32), ALU.subtract).then_inc(done, 1)

        def split_low(dve, i):
            if i not in on_pool:
                take_rest(dve, i, w_lo_done)

        def split_low_pool(pool, i):
            take_rest(pool, i, w_lo_pool)

        def split_behind(eng, key, split):
            i = split_no[key] + PARTS
            if i < len(split_tiles):
                split(eng, i)

        def turned_high(act, key, part):
            wait_full(act, key)
            act.activation(part, bank_of(key).rearrange("p (i t) -> p i t", i=4), ACT.Copy).then_inc(a_hi_done, 1)

        def turned_low(dve, key, part, high):
            dve.wait_ge(a_hi_done, turned_no[key] + 2)
            dve.tensor_tensor(part, bank_of(key).rearrange("p (i t) -> p i t", i=4), high.bitcast(F32),
                              ALU.subtract).then_inc(*drained(key))

        def bias_of(h, tt):
            n = P * (tt + 1)
            last = bias_t[:, h, n - 1:n]
            return bass.AP(last.tensor, last.offset, [list(last.ap[0]), [-1, n]])

        def bc_mid(ap, n):
            return ap.unsqueeze(1).to_broadcast([ap.shape[0], n, ap.shape[1]])

        def bc_last(ap, n):
            return ap.unsqueeze(2).to_broadcast([ap.shape[0], ap.shape[1], n])

        def heads4(ap):
            return ap.rearrange("p (h t) -> p h t", h=HG_HEADS)

        def attn_io(l, i):
            half, h = i // 8, i % 8
            if l < 2:
                g, lo = h // 4, DH * (h % 2)
                kk = (ks2, kw2)[half]
                return (half, h, nq[lo:lo + DH, h // 2, :], kk[lo:lo + DH, g, :],
                        lambda st: v_sw[:, st, half * P + g * DH:half * P + (g + 1) * DH], h, False)
            lo = DH * (i % 2)
            return (half, h, q2[lo:lo + DH, i // 2, :], k2[lo:lo + DH, i // 2, :],
                    lambda st: v2[:, st, i * DH:(i + 1) * DH], 8 + i, l == 2 and half == 1)

        LEVELS_AFTER = {"nq0": [0, 1], "nq1": [2], "hid": [3], "kskw": [4], "gt": [5], "hg0": [6], "hg1": [7],
                        "vsvw": [8]}
        DECAYS_AFTER = {"hq1": [1, 2], "nq0": [3], "nq1": [4], "hid": [5], "kskw": [6], "gt": [7, 8]}
        FACTORS_AFTER = {"hq1": [1, 2], "nq0": [3], "nq1": [4], "hid": [5], "kskw": [6], "gt": [7], "hg0": [8]}
        NLEV = len(HALVES)

        def level_banks(v):
            return bank[:, 4 + 2 * (v % 2):6 + 2 * (v % 2), :].rearrange("p b c -> p (b c)")

        def blocks(ap, half):
            return ap.rearrange("p (n w) -> p n w", w=2 * half)

        block = ctx.enter_context(nc.Block())

        @block.sync
        def _(sp):
            def load(i):
                if i >= SLOTS:
                    old = stream[i - SLOTS]
                    if unsplit(old):
                        wait_used(sp, old)
                    else:
                        wait_split(sp, split_no[old])
                sp.dma_start(raw[:, i % SLOTS, :], a["stream"][i]).then_inc(tile_loaded[i % SLOTS], 16)

            sp.dma_start(xT0, a["xT"]).then_inc(x_in, 16)
            for i in range(SLOTS):
                load(i)
            for dst, name in ((one_hot_c, "one_hot_c"), (rel_c, "rel_c"), (one_hot[0:BUCKETS, :], "one_hot"),
                              (rel[0:BUCKETS, :], "rel"), (off_row[0:24, :], "off_row"),
                              (cmp_off[:, :, :], "cmp_off"), (mask_in, "hg_mask"), (lb[:, :, :], "lb"),
                              (w_gate_in, "w_gate")):
                sp.dma_start(dst, a[name]).then_inc(start_in, 16)
            load(SLOTS)
            load(SLOTS + 1)
            for dst, name in ((pos[:, :, :, :], "pos"), (head_blocks[:, :], "head_blocks"), (w2[:, :, :], "w2"),
                              (cmp_on[:, :, :], "cmp_on"), (ident[:, :], "ident"), (gnorm[:, :, :], "gnorm"),
                              (idx_norm[:, :], "idx_norm")):
                sp.dma_start(dst, a[name]).then_inc(consts_in, 16)
            load(SLOTS + 2)
            sp.wait_ge(bias_row_ready, 1)
            sp.dma_start(scratch, bias_row[0:24, :]).then_inc(rows_out, 16)
            load(SLOTS + 3)
            sp.wait_ge(rows_out, 16)
            load(SLOTS + 4)
            for g in range(BIAS_READS):
                heads = slice(g * 24 // BIAS_READS, (g + 1) * 24 // BIAS_READS)
                src = bass.AP(scratch.tensor, heads.start * REV, [[1, P], [REV, 24 // BIAS_READS], [1, S]])
                sp.dma_start(bias_t[:, heads, :], src).then_inc(bias_in, 16)
                load(SLOTS + 5 + g)
            sp.dma_start(x[:, :, :], a["x"]).then_inc(x_rows_in, 16)
            load(SLOTS + 5 + BIAS_READS)
            sp.dma_start(conv_col[:, :, :, :], a["conv_col"]).then_inc(x_rows_in, 16)
            for i in range(SLOTS + 6 + BIAS_READS, len(stream)):
                load(i)
            for tt in range(NT):
                sp.wait_ge(normed, 8 * PIECES + piece(tt, 1))
                sp.dma_start(a["out"][:, tt, :], res[:, tt, :]).then_inc(out_sem, 16)
            sp.wait_ge(out_sem, 16 * NT)

        STARTS = 9 * 16
        CONSTS = 7 * 16

        @block.tensor
        def _(pe):
            def open_bank(key):
                n = bank_no[key]
                if n >= RING:
                    pe.wait_ge(bank_drained[n % RING], n // RING)
                return bank_of(key)

            def close_bank(ins):
                ins.then_inc(bank_full, 1)

            def weights(key):
                i = split_no[key]
                wait_split(pe, i)
                return w_hi[:, i % PARTS, :], w_lo[:, i % PARTS, :]

            def products(out, left, right, first=True, last=True):
                (lh, ll), (rh, rl) = left, right
                pe.matmul(out, lh, rh, start=first, stop=False)
                pe.matmul(out, lh, rl, start=False, stop=False)
                return pe.matmul(out, ll, rh, start=False, stop=last)

            def channel_tile(key, use=None):
                b = open_bank(use or key)
                w = [part.rearrange("p (k c) -> p k c", k=KT) for part in weights(key)]
                for c in range(2):
                    for k in range(KT):
                        mm = products(b[:, c * S:(c + 1) * S], [part[:, k, c * P:(c + 1) * P] for part in w],
                                      (a_hi[:, k, :], a_lo[:, k, :]), k == 0, k == KT - 1)
                close_bank(mm)

            def tokens(b, key, tt, norm=None):
                w = [part.rearrange("p (k c) -> p k c", k=KT) for part in weights(key)]
                t = slice(tt * P, (tt + 1) * P)
                for k in range(KT):
                    if norm is not None and k % 4 == 0:
                        wait_drained(pe, (norm, "xT", tt, k // 4))
                    mm = products(b[:, tt * S:(tt + 1) * S], (a_hi[:, k, t], a_lo[:, k, t]),
                                  [part[:, k, :] for part in w], k == 0, k == KT - 1)
                return mm

            def behind_norm_tiles(n, keys, uses):
                banks = []
                for key, use in zip(keys, uses):
                    banks.append(open_bank(use))
                    tokens(banks[-1], key, 0, norm=n)
                x_transposes(n, 1)
                for key, b in zip(keys, banks):
                    close_bank(tokens(b, key, 1, norm=n))

            def token_tile(key):
                b = open_bank(key)
                tokens(b, key, 0)
                close_bank(tokens(b, key, 1))

            def few_channels(key, w, n):
                b = open_bank(key)
                for k in range(KT):
                    mm = products(b[0:n, 0:S], [part[:, k, :] for part in w], (a_hi[:, k, :], a_lo[:, k, :]),
                                  k == 0, k == KT - 1)
                close_bank(mm)

            def turn_few(key, rows, n):
                b = open_bank(key)
                for tt in range(NT):
                    mm = pe.transpose(b[:, tt * n:(tt + 1) * n], rows[:, tt * P:(tt + 1) * P], ident[0:n, 0:n])
                close_bank(mm)

            def token_major(name):
                return name[:2] in ("hi", "hg", "vs") or name[0] == "v"

            def project(l, name):
                (token_tile if token_major(name) else channel_tile)((l, name))

            def x_transposes(n, tt):
                for q in range(2):
                    b = open_bank((n, "xT", tt, q))
                    pe.wait_ge(normed, normed_by(n, tt, q))
                    for i in range(4):
                        c = (4 * q + i) * P
                        mm = pe.transpose(b[:, i * P:(i + 1) * P], (x if n < 3 else res)[:, tt, c:c + P], ident[:, :])
                    close_bank(mm)

            def level(l, v):
                half = HALVES[v]
                if l * NLEV + v >= 2:
                    pe.wait_ge(picked, l * NLEV + v - 1)
                if v == 0:
                    if l == 1:
                        pe.wait_ge(acc_drained, 2 * PIECES)
                    pe.wait_ge(k_done, l + 1)
                    wait_drained(pe, (l, "hq1"))
                    lhs, rhs = k_t, q_t
                else:
                    pe.wait_ge(level_done, l * (NLEV - 1) + v)
                    lhs = rhs = lev[v % 2]
                out = level_banks(v)
                for h in range(HG_HEADS):
                    if half == P:
                        mm = pe.matmul(out[:, h * P:(h + 1) * P], lhs[:, h * S:h * S + P],
                                       rhs[:, h * S + P:(h + 1) * S], start=True, stop=True)
                        continue
                    for st in range(NT):
                        c = h * S + st * P
                        mm = pe.matmul(out[:, c:c + P], lhs[:, c:c + P], rhs[:, c:c + P], start=True, stop=True)
                mm.then_inc(product_done, 1)

            def attention(l):
                for s, t, v in attention_steps():
                    if s is not None:
                        half, h, q, k, _, _, _ = attn_io(l, s)
                        b = open_bank((l, "S", s))
                        pe.matmul(b[:, 0:S], q[:, P:S], k, start=True, stop=True)
                        close_bank(pe.matmul(b[:, S:TRI], q[:, 0:P], k[:, 0:P], start=True, stop=True))
                    if t is not None:
                        b = open_bank((l, "T", t))
                        e = lbuf[:, t % LBUFS, :]
                        pe.wait_ge(exp_done, l * HEADS + t + 1)
                        pe.transpose(b[:, 0:P], e[:, S:TRI], ident[:, :])
                        pe.transpose(b[:, P:2 * P], e[:, 0:P], ident[:, :])
                        close_bank(pe.transpose(b[:, 2 * P:3 * P], e[:, P:2 * P], ident[:, :]))
                    if v is not None:
                        half, h, _, _, val, _, _ = attn_io(l, v)
                        wait_drained(pe, (l, "T", v))
                        if v == 0:
                            if l < 2:
                                pe.wait_ge(picked, (l + 1) * NLEV)
                            else:
                                pe.wait_ge(acc_drained, 2 * l * PIECES)
                        pt = pT[:, v % 2, :]
                        o0 = bank[:, 4 + 2 * half, h * DH:(h + 1) * DH]
                        o1 = bank[:, 5 + 2 * half, h * DH:(h + 1) * DH]
                        pe.matmul(o0, pt[:, 0:P], val(0), start=True, stop=True)
                        pe.matmul(o1, pt[:, P:2 * P], val(0), start=True, stop=False)
                        pe.matmul(o1, pt[:, 2 * P:3 * P], val(1), start=False, stop=True).then_inc(pv_done, 1)

            def transposes_out(l, half, tt, src):
                b = open_bank((l, "oT", half, tt))
                for i in range(4):
                    mm = pe.transpose(b[:, i * P:(i + 1) * P], src[:, i * P:(i + 1) * P], ident[:, :])
                close_bank(mm)

            def add_rows(key, left, tt, first, last):
                w = [part.rearrange("p (k c) -> p k c", k=2) for part in weights(key)]
                for hf in range(2):
                    for kk in range(2):
                        mm = products(bank[:, 4 + 2 * tt + hf, :],
                                      [part[:, kk, tt * P:(tt + 1) * P] for part in left],
                                      [part[:, kk, hf * 512:(hf + 1) * 512] for part in w],
                                      first and kk == 0, last and kk == 1)
                    if last:
                        mm.then_inc(acc_full, 1)
                if tt == NT - 1 and not last:
                    mm.then_inc(rows_used, 1)

            def add_tail(l, kind, lefts, norm):
                keys = tail(l, kind)
                for tt in range(NT):
                    for i, (key, left) in enumerate(zip(keys, lefts)):
                        if tt == 1 and i == TAIL - 1 and norm not in (4, 8):
                            x_transposes(norm, 0)
                        if kind == "down" and tt == 0:
                            pe.wait_ge(h_done, l * FT + 2 * (FT // 2 - TAIL + i) + 2)
                        add_rows(key, left, tt, False, i == TAIL - 1)
                if norm == 4:
                    x_transposes(norm, 0)

            def output_projection(l):
                for half in range(2):
                    for tt in range(NT):
                        if (l, "oT", half, tt) in bank_no:
                            wait_drained(pe, (l, "oT", half, tt))
                        else:
                            wait_drained(pe, (l, "hoT", tt))
                pe.wait_ge(mix_done, (2 * l + 2) * NT)
                left = [[part[:, 2 * r:2 * r + 2, :] for part in (a_hi, a_lo)] for r in range(4)]
                for tt in range(NT):
                    add_rows((l, "out0"), left[0], tt, True, False)
                add_tail(l, "out", left[1:], norm_after(l)[0])

            def turn_heads(l):
                for j in range(HEAD):
                    b = open_bank((l, "up", j))
                    wait_drained(pe, (l, "head", j))
                    for c in range(2):
                        for tt in range(NT):
                            src = tt * S + c * P
                            mm = pe.transpose(b[:, c * S + tt * P:c * S + (tt + 1) * P],
                                              head_rows[j][:, src:src + P], ident[:, :])
                    close_bank(mm)

            def feed_forward(l):
                for kind, j in ffn_order():
                    if kind == "up":
                        if j >= HEAD:
                            channel_tile((l, f"up{j}"), use=(l, "up", j))
                        if j == HEAD:
                            turn_heads(l)
                    elif j < FT // 2 - TAIL:
                        pe.wait_ge(h_done, l * FT + 2 * j + 2)
                        if j == 0:
                            pe.wait_ge(acc_drained, (2 * l + 1) * PIECES)
                        for tt in range(NT):
                            add_rows((l, f"down{j}"), hidden(j), tt, j == 0, False)
                end = norm_after(l)[1]
                add_tail(l, "down", [hidden(j) for j in range(FT // 2 - TAIL, FT // 2)], 4 if end == 3 else end)

            def hidden(j):
                i = 2 * j % HSLOTS
                return h_hi[:, i:i + 2, :], h_lo[:, i:i + 2, :]

            for l in range(LAYERS):
                if l == 0:
                    pe.wait_ge(a_lo_done, 1)
                    for name in ("hi0", "hi1"):
                        project(l, name)
                    pe.wait_ge(start_in, STARTS)
                    b = open_bank(("cmpbias",))
                    for tt in range(NT):
                        for g in range(CG):
                            at = S - 1 + tt * P - 16 * CB * g - 31
                            c = (tt * CG + g) * CB * 8
                            mm = pe.matmul(b[:, c:c + CB * 8], one_hot_c[:, at:at + P], rel_c[:, :],
                                           start=True, stop=True)
                    close_bank(mm)
                    b = open_bank(("biasrow",))
                    close_bank(pe.matmul(b[0:24, 0:REV], rel[0:BUCKETS, 0:24], one_hot[0:BUCKETS, :],
                                         start=True, stop=True))
                else:
                    heads = [(l, name) for name in projections(l)[:HEAD]]
                    behind_norm_tiles({1: 1, 2: 4, 3: 6}[l], heads, heads)
                if l < 2:
                    for name in ("hf0", "hf1", "hq0", "hq1", "kcvc"):
                        project(l, name)
                    for name in ("nq0", "nq1"):
                        project(l, name)
                        for v in LEVELS_AFTER[name]:
                            level(l, v)
                    pe.wait_ge(consts_in, CONSTS)
                    b = open_bank((l, "hid"))
                    wait_drained(pe, (l, "kcvc"))
                    for i, name in enumerate(("w1k", "w1v")):
                        t = tile_no[(l, name)]
                        pe.wait_ge(tile_loaded[t % SLOTS], 16 * (t // SLOTS + 1))
                        w = raw[:, t % SLOTS, :].rearrange("p (k c) -> p k c", k=CMP_KT)
                        for k in range(CMP_KT):
                            mm = pe.matmul(b[:, 32 * i:32 * i + 30], w[:, k, :],
                                           blk[i][:, k, :, :].rearrange("p g n -> p (g n)"),
                                           start=(k == 0), stop=(k == CMP_KT - 1))
                    close_bank(mm)
                    for v in LEVELS_AFTER["hid"]:
                        level(l, v)
                    project(l, "kskw")
                    for v in LEVELS_AFTER["kskw"]:
                        level(l, v)
                    pe.wait_ge(w_gate_split, 1)
                    few_channels((l, "gt"), [part[:, l, :, :] for part in w_gate], 24)
                    for v in LEVELS_AFTER["gt"]:
                        level(l, v)
                    b = open_bank((l, "kcv"))
                    wait_drained(pe, (l, "hid"))
                    pe.matmul(b[:, 0:30], w2[:, l, 0:P], hid[:, :], start=True, stop=True)
                    close_bank(pe.matmul(b[:, DH:2 * DH], hid_v[:, :, :].rearrange("p h n -> p (h n)"),
                                         w2[:, l, P:P + DH], start=True, stop=True))
                    project(l, "hg0")
                    for v in LEVELS_AFTER["hg0"]:
                        level(l, v)
                    wait_drained(pe, (l, "gt"))
                    turn_few((l, "gtT"), gate_rows, 24)
                    wait_drained(pe, (l, "kcv"))
                    wait_drained(pe, (l, "nq1"))
                    for odd in range(2):
                        b = open_bank((l, "cs", odd))
                        lo = DH * odd
                        for tt in range(NT):
                            for j in range(4):
                                c = (tt * 4 + j) * NCP
                                mm = pe.matmul(b[:, c:c + NC], nq[lo:lo + DH, j, tt * P:(tt + 1) * P],
                                               kc2[lo:lo + DH, j // 2, :], start=True, stop=True)
                        close_bank(mm)
                    project(l, "hg1")
                    for v in LEVELS_AFTER["hg1"]:
                        level(l, v)
                    b = open_bank((l, "vsvw"))
                    tokens(b, (l, "vsvw"), 0)
                    for v in LEVELS_AFTER["vsvw"]:
                        level(l, v)
                    close_bank(tokens(b, (l, "vsvw"), 1))
                    b = open_bank((l, "cT"))
                    pe.wait_ge(cmp_prob, l + 1)
                    for tt in range(NT):
                        mm = pe.transpose(b[:, tt * P:(tt + 1) * P], cp[:, tt, :, :].rearrange("p h n -> p (h n)"),
                                          ident[:, :])
                    close_bank(mm)
                    for tt in range(NT):
                        b = open_bank((l, "ho", tt))
                        pe.wait_ge(picked, (l + 1) * NLEV)
                        wait_drained(pe, (l, "hi1"))
                        for h in range(HG_HEADS):
                            o = b[:, h * P:(h + 1) * P]
                            if tt == 1:
                                pe.matmul(o, s_cross[:, h * P:(h + 1) * P], v_hg[:, 0, h * P:(h + 1) * P],
                                          start=True, stop=False)
                            mm = pe.matmul(o, s_hg[:, h * S + tt * P:h * S + (tt + 1) * P],
                                           v_hg[:, tt, h * P:(h + 1) * P], start=(tt == 0), stop=True)
                        close_bank(mm)
                    for tt in range(NT):
                        b = open_bank((l, "co", tt))
                        wait_drained(pe, (l, "cT"))
                        close_bank(pe.matmul(b[:, :], cpT[:, tt, :], vc8[:, :, :].rearrange("p h d -> p (h d)"),
                                             start=True, stop=True))
                    wait_drained(pe, (l, "vsvw"))
                    wait_drained(pe, (l, "kskw"))
                    attention(l)
                    for tt in range(NT):
                        b = open_bank((l, "hoT", tt))
                        wait_drained(pe, (l, "ho", tt))
                        for i in range(HG_HEADS):
                            mm = pe.transpose(b[:, i * P:(i + 1) * P], o_hg[tt][:, i * P:(i + 1) * P], ident[:, :])
                        close_bank(mm)
                    for tt in range(NT):
                        pe.wait_ge(mix_done, 2 * l * NT + NT + tt + 1)
                        transposes_out(l, 1, tt, res[:, tt, 0:512])
                else:
                    if l == 2:
                        pe.wait_ge(w_idx_split, 1)
                        few_channels((l, "kw"), w_idx, 80)
                        for j in range(4):
                            project(l, f"qi{j}")
                            if j == 0:
                                wait_drained(pe, (l, "kw"))
                                turn_few((l, "kwT"), kw_rows, 80)
                        b = open_bank((l, "kiT"))
                        pe.wait_ge(ki_normed, NT)
                        for tt in range(NT):
                            mm = pe.transpose(b[:, tt * P:(tt + 1) * P], small[:, tt, :], ident[:, :])
                        close_bank(mm)
                    for j, name in enumerate(attention_tiles()):
                        project(l, name)
                        if l == 2:
                            for i in index_heads(j):
                                b = open_bank((l, "I", i))
                                lo = DH * (i % 2)
                                wait_drained(pe, (l, "kiT"))
                                wait_drained(pe, (l, f"qi{i // 4}"))
                                pe.matmul(b[:, 0:S], qi[lo:lo + DH, i // 2, P:S], kiT[lo:lo + DH, :],
                                          start=True, stop=True)
                                close_bank(pe.matmul(b[:, S:TRI], qi[lo:lo + DH, i // 2, 0:P],
                                                     kiT[lo:lo + DH, 0:P], start=True, stop=True))
                    for name in ["v0", "v1"] + attention_tiles():
                        wait_drained(pe, (l, name))
                    attention(l)
                    for half in range(2):
                        for tt in range(NT):
                            pe.wait_ge(mix_done, (2 * l + half) * NT + tt + 1)
                            transposes_out(l, half, tt, res[:, tt, half * 512:(half + 1) * 512])
                output_projection(l)
                behind_norm_tiles(norm_after(l)[0], [(l, f"up{j}") for j in range(HEAD)],
                                  [(l, "head", j) for j in range(HEAD)])
                feed_forward(l)

        @block.scalar
        def _(act):
            step = steps(act, act_step)

            def copy_out(key, dst, src=None, scale=1.0):
                wait_full(act, key)
                act.activation(dst, bank_of(key) if src is None else src, ACT.Copy,
                               scale=scale).then_inc(*drained(key))

            def two(ap):
                return ap.rearrange("p (c t) -> p c t", c=2)

            def level_decay(l, v):
                n = l * (NLEV - 1) + v
                half = HALVES[v]
                act.wait_ge(diff_done, n)
                d = blocks(dec[v % 2], half)
                act.activation(d[:, :, half:], d[:, :, half:], ACT.Exp)
                act.activation(d[:, :, :half], d[:, :, :half], ACT.Exp, scale=-1.0).then_inc(decay_done, 1)

            def prep(l, name):
                for v in DECAYS_AFTER.get(name, ()):
                    level_decay(l, v)

            def attention(l):
                for i in range(HEADS):
                    half, h = i // 8, i % 8
                    act.wait_ge(logit_done, l * HEADS + i + 1)
                    e = lbuf[:, i % LBUFS, :]
                    act.activation(e[:, 0:S], e[:, 0:S], ACT.Exp, scale=-1.0,
                                   bias=mxn[:, half, 1, h:h + 1], accum_out=esum[:, half, 1, h:h + 1])
                    act.activation(e[:, S:TRI], e[:, S:TRI], ACT.Exp, scale=-1.0,
                                   bias=mxn[:, half, 0, h:h + 1],
                                   accum_out=esum[:, half, 0, h:h + 1]).then_inc(exp_done, 1)

            def root(n, tt):
                st = nstat[:, tt, :]
                act.wait_ge(sum_done, sum_done_at(n, tt))
                act.activation(st[:, 14:15], st[:, 13:14], ACT.Sqrt,
                               bias=(eps_ln if n < 4 else eps_rms)[:, 0:1]).then_inc(root_done, 1)

            def xT_out(n, tt):
                for q in range(2):
                    turned_high(act, (n, "xT", tt, q), a_hi[:, 4 * q:4 * q + 4, tt * P:(tt + 1) * P])

            def queries_out(l, i):
                copy_out((l, f"hq{i}"), q_t[:, i * 512:(i + 1) * 512])
                split_behind(act, (l, f"hq{i}"), split_high)

            def around_norm(l, kind, norms):
                keys, turn = tail(l, kind), norms[-1]
                act.activation(nstat[:, 0, 18:19], eps_ln[:, 0:1], ACT.Sqrt)
                root(norms[0], 0)
                split_behind(act, keys[0], split_high)
                split_behind(act, keys[1], split_high)
                if len(norms) > 1:
                    root(turn, 0)
                elif turn != 8:
                    xT_out(turn, 0)
                split_behind(act, keys[2], split_high)
                if len(norms) > 1:
                    xT_out(turn, 0)
                for n in norms:
                    root(n, 1)
                if turn != 8:
                    xT_out(turn, 1)

            def feed_forward(l):
                for j in range(HEAD):
                    copy_out((l, "head", j), head_rows[j])
                    split_behind(act, (l, f"up{j}"), split_high)
                for kind, j in ffn_order():
                    if kind == "up":
                        up(l, j)
                    if (kind != "up" or j >= HEAD) and (l, f"{kind}{j}") not in tail(l, "down"):
                        split_behind(act, (l, f"{kind}{j}"), split_high)

            def up(l, j):
                key = (l, "up", j)
                wait_full(act, key)
                b = bank_of(key)
                if j >= 2:
                    act.wait_ge(h_done, l * FT + j - 1)
                if l < 2:
                    act.activation(gate_a[j % 2], b[:, 0:S], ACT.Silu).then_inc(act_gate, 1)
                else:
                    m = l - 2
                    act.activation(cval[j % 2], b[:, 0:S], ACT.Identity, scale=conv_col[:, m, j, 2:3],
                                   bias=conv_col[:, m, j, 3:4])
                    act.activation(cgate[j % 2], b[:, S:2 * S], ACT.Identity, scale=conv_col[:, m, FT + j, 2:3],
                                   bias=conv_col[:, m, FT + j, 3:4]).then_inc(conv_in, 1)
                    act.wait_ge(conv_done, m * FT + j + 1)
                    act.activation(gate_a[j % 2], cgate[j % 2], ACT.Silu).then_inc(silu_done, 1)

            act.wait_ge(x_in, 16)
            act.activation(a_hi[:, :, :], xT0, ACT.Copy).then_inc(a_hi_done, 1)
            for i in range(PARTS):
                split_high(act, i)
            act.wait_ge(zeroed, 5)

            for l in range(LAYERS):
                if l < 2:
                    for i in range(2):
                        copy_out((l, f"hi{i}"), v_hg[:, :, i * S:(i + 1) * S], two(bank_of((l, f"hi{i}"))))
                        split_behind(act, (l, f"hi{i}"), split_high)
                    for i in range(2):
                        copy_out((l, f"hf{i}"), f_t[:, i * 512:(i + 1) * 512])
                        split_behind(act, (l, f"hf{i}"), split_high)
                    wait_drained(act, (l, "hf0"))
                    wait_drained(act, (l, "hf1"))
                    if l == 0:
                        act.wait_ge(lb_ready, 1)
                        act.activation(lb_tmp[:, 1, :], lb_tmp[:, 0, :], ACT.Abs)
                    step(act.activation(dec[0], f_t, ACT.Abs))
                    if l == 0:
                        act.activation(lb_tmp[:, 2, :], lb_tmp[:, 1, :], ACT.Exp, scale=-1.0)
                    step(act.activation(dec[0], dec[0], ACT.Exp, scale=-1.0))
                    act.activation(dec[0], dec[0], ACT.Ln, bias=1.0).then_inc(softplus_done, 1)
                    if l == 0:
                        act.activation(lb_tmp[:, 3, :], lb_tmp[:, 2, :], ACT.Ln, bias=1.0).then_inc(lb_ready, 1)
                    queries_out(l, 0)
                    if l == 1:
                        act.wait_ge(gap_done, 1)
                        step(act.activation(dec[0], dec[0], ACT.Abs))
                        step(act.activation(dec[0], dec[0], ACT.Exp, scale=-1.0))
                        act.activation(dec[0], dec[0], ACT.Ln, bias=1.0).then_inc(softplus2_done, 1)
                    act.wait_ge(kdiff_done, l + 1)
                    act.activation(k_t, k_t, ACT.Exp).then_inc(k_done, 1)
                    queries_out(l, 1)
                    prep(l, "hq1")
                    split_behind(act, (l, "kcvc"), split_high)
                    if l == 0:
                        act.wait_ge(rows_out, 16)
                    for i in range(2):
                        copy_out((l, f"nq{i}"), nq[:, 2 * i:2 * i + 2, :], two(bank_of((l, f"nq{i}"))),
                                 scale=-(DH ** -0.5))
                        prep(l, f"nq{i}")
                    key = (l, "hid")
                    wait_full(act, key)
                    act.activation(hid[:, :], bank_of(key)[:, 0:30], ACT.Gelu_apprx_tanh)
                    for g in range(2):
                        src = bank_of(key)[:, 32 + g * NC:32 + (g + 1) * NC]
                        ins = act.activation(hid_v[:, 4 * g:4 * g + 4, 0:NC], bc_mid(src, 4), ACT.Gelu_apprx_tanh)
                    ins.then_inc(*drained(key))
                    for i in range(2):
                        split_behind(act, (l, f"nq{i}"), split_high)
                    prep(l, "hid")
                    key = (l, "kskw")
                    wait_full(act, key)
                    for i, dst in enumerate((ks2, kw2)):
                        for g in range(2):
                            for lo in (0, DH):
                                ins = act.activation(dst[lo:lo + DH, g, :],
                                                     bank_of(key)[g * DH:(g + 1) * DH, i * S:(i + 1) * S], ACT.Copy)
                    ins.then_inc(*drained(key))
                    split_behind(act, key, split_high)
                    prep(l, "kskw")
                    key = (l, "gt")
                    wait_full(act, key)
                    act.activation(gate_rows, bank_of(key)[0:24, 0:S], ACT.Exp, scale=-1.0).then_inc(*drained(key))
                    prep(l, "gt")
                    for i in range(2):
                        key = (l, f"hg{i}")
                        wait_full(act, key)
                        act.activation(g_hg[:, :, i * S:(i + 1) * S], two(bank_of(key)),
                                       ACT.Silu).then_inc(*drained(key))
                        split_behind(act, key, split_high)
                        if i == 0:
                            act.wait_ge(cmp_logit, l + 1)
                            act.activation(ce[:, :, :, :], cl[:, :, :, :], ACT.Exp, scale=-1.0).then_inc(cmp_exp, 1)
                    copy_out((l, "vsvw"), v_sw[:, :, :], two(bank_of((l, "vsvw"))))
                    split_behind(act, (l, "vsvw"), split_high)
                    act.activation(nstat[:, 0, 18:19], eps_ln[:, 0:1], ACT.Sqrt)
                    for tt in range(NT):
                        key = (l, "ho", tt)
                        wait_full(act, key)
                        for h in range(HG_HEADS):
                            ins = act.activation(o_sq[tt][:, h * P:(h + 1) * P], bank_of(key)[:, h * P:(h + 1) * P],
                                                 ACT.Square, accum_out=stat[:, 4 * tt + h:4 * tt + h + 1])
                        step(ins)
                    act.activation(stat[:, 8:16], stat[:, 0:8], ACT.Sqrt, scale=1.0 / P,
                                   bias=eps_rms[:, 0:1]).then_inc(hg_rstd, 1)
                    attention(l)
                    for tt in range(NT):
                        turned_high(act, (l, "hoT", tt), a_hi[:, 0:4, tt * P:(tt + 1) * P])
                    for tt in range(NT):
                        turned_high(act, (l, "oT", 1, tt), a_hi[:, 4:8, tt * P:(tt + 1) * P])
                else:
                    for j in range(HEAD):
                        copy_out((l, f"v{j}"), v2[:, :, j * S:(j + 1) * S], two(bank_of((l, f"v{j}"))))
                        split_behind(act, (l, f"v{j}"), split_high)
                    if l == 2:
                        copy_out((l, "kw"), kw_rows, bank_of((l, "kw"))[0:80, 0:S])
                        copy_out((l, "qi0"), qi[:, 0:2, :], two(bank_of((l, "qi0"))))
                        split_behind(act, (l, "qi0"), split_high)
                        key = (l, "kwT")
                        wait_full(act, key)
                        for tt in range(NT):
                            ins = act.activation(small[:, tt, 0:80], bank_of(key)[:, tt * 80:(tt + 1) * 80], ACT.Copy)
                        ins.then_inc(*drained(key))
                        wait_drained(act, key)
                        for tt in range(NT):
                            step(act.activation(relu[0][:, 0:DH], small[:, tt, 0:DH], ACT.Square,
                                                accum_out=stat[:, tt:tt + 1]))
                        step(act.activation(stat[:, 2:4], stat[:, 0:2], ACT.Ln, scale=1.0 / DH, bias=eps_rms[:, 0:1]))
                        act.activation(stat[:, 4:6], stat[:, 2:4], ACT.Exp, scale=-0.5).then_inc(ki_rstd, 1)
                        for j in range(1, 4):
                            copy_out((l, f"qi{j}"), qi[:, 2 * j:2 * j + 2, :], two(bank_of((l, f"qi{j}"))))
                            split_behind(act, (l, f"qi{j}"), split_high)
                        copy_out((l, "kiT"), kiT, bank_of((l, "kiT"))[:, 0:S])
                    for j, name in enumerate(attention_tiles()):
                        src = two(bank_of((l, name)))
                        if name[0] == "q":
                            copy_out((l, name), q2[:, 2 * j:2 * j + 2, :], src, scale=-(DH ** -0.5))
                        elif name[0] == "k":
                            copy_out((l, name), k2[:, 2 * j - 8:2 * j - 6, :], src)
                        else:
                            copy_out((l, name), v2[:, :, (j - 6) * S:(j - 5) * S], src)
                        split_behind(act, (l, name), split_high)
                        if l == 2:
                            for i in index_heads(j):
                                key = (l, "I", i)
                                wait_full(act, key)
                                if i >= 2:
                                    act.wait_ge(relu_used, i - 1)
                                act.activation(relu[i % 2], bank_of(key)[:, 0:TRI], ACT.Relu,
                                               scale=DH ** -0.5).then_inc(*drained(key))
                    attention(l)
                    for half in range(2):
                        for tt in range(NT):
                            turned_high(act, (l, "oT", half, tt), a_hi[:, 4 * half:4 * half + 4, tt * P:(tt + 1) * P])
                split_behind(act, (l, "out0"), split_high)
                mid, end = norm_after(l)
                around_norm(l, "out", [mid])
                feed_forward(l)
                around_norm(l, "down", [3, 4] if end == 3 else [end])

        @block.vector
        def _(dve):
            step = steps(dve, dve_step)

            def level_product(l, v):
                n = l * (NLEV - 1) + v
                half = HALVES[v]
                dve.wait_ge(decay_done, n)
                if n > 2:
                    dve.wait_ge(product_done, l * NLEV + v - 1 if v > 2 else l * NLEV)
                d, o = blocks(dec[v % 2], half), blocks(lev[v % 2], half)
                dve.tensor_tensor(o[:, :, :half], d[:, :, :half], blocks(k_t, half)[:, :, :half], ALU.mult)
                dve.tensor_tensor(o[:, :, half:], d[:, :, half:], blocks(q_t, half)[:, :, half:],
                                  ALU.mult).then_inc(level_done, 1)

            def pick(l, v):
                dve.wait_ge(product_done, l * NLEV + v + 1)
                if v > 0:
                    dve.wait_ge(picked, l * NLEV + v)
                src = level_banks(v)
                if HALVES[v] == P:
                    dve.tensor_copy(s_cross, src[:, 0:512]).then_inc(picked, 1)
                else:
                    dve.copy_predicated(s_hg.rearrange("p (n t) -> p n t", t=P), bc_mid(hg_mask[:, v, :], 8),
                                        src.rearrange("p (n t) -> p n t", t=P)).then_inc(picked, 1)

            def after(l, name):
                for v in LEVELS_AFTER.get(name, ()):
                    pick(l, v)
                for v in FACTORS_AFTER.get(name, ()):
                    level_product(l, v)

            def attention(l):
                for i, (s, t, _) in enumerate(attention_steps()):
                    if s is not None:
                        half, h, _, _, _, bh, indexed = attn_io(l, s)
                        key = (l, "S", s)
                        wait_full(dve, key)
                        if s >= LBUFS:
                            wait_full(dve, (l, "T", s - LBUFS))
                        b, o = bank_of(key), lbuf[:, s % LBUFS, :]
                        if l == 0 and s == 0:
                            dve.wait_ge(bias_in, 16 * BIAS_READS)
                        if l == 3 and s == 0:
                            dve.wait_ge(bias_log, 1)
                        if indexed:
                            dve.wait_ge(bias_sel, h + 1)
                            b1, b0 = bias_s[h % 2][:, 0:S], bias_s[h % 2][:, S:TRI]
                        else:
                            b1, b0 = bias_of(bh, 1), bias_of(bh, 0)
                        dve.tensor_tensor_reduce(o[:, 0:S], b[:, 0:S], b1, 1.0, 3e38, ALU.add, ALU.min,
                                                 mxn[:, half, 1, h:h + 1])
                        step(dve.tensor_tensor_reduce(o[:, S:TRI], b[:, S:TRI], b0, 1.0, 3e38, ALU.add, ALU.min,
                                                      mxn[:, half, 0, h:h + 1]))
                        dve.nop().then_inc(logit_done, 1)
                        dve.nop().then_inc(*drained(key))
                    if t is not None:
                        key = (l, "T", t)
                        wait_full(dve, key)
                        if t >= 2:
                            dve.wait_ge(pv_done, l * HEADS + t - 1)
                        dve.tensor_copy(pT[:, t % 2, :], bank_of(key)[:, 0:TRI]).then_inc(*drained(key))
                    if l == 2 and i < 4:
                        choose(1, range(2 * i, 2 * i + 2))
                    if l == 2 and i == 4:
                        dve.tensor_scalar(unsel, score, 1.5 * NEG, -NEG, ALU.is_gt, ALU.mult).then_inc(unsel_done, 1)
                    if i == 12:
                        weigh(l, 0)
                    if i in (13, 14):
                        mix(l, 0, i - 13)
                weigh(l, 1)
                for tt in range(NT):
                    mix(l, 1, tt)

            def choose(n, times):
                part = (score[:, 0:S], score[:, S:TRI])[n]
                for i in times:
                    step(dve.max(stat[:, 8:16], part))
                    step(dve.match_replace(part, stat[:, 8:16], part, TAKEN))

            def weigh(l, half):
                dve.wait_ge(exp_done, l * HEADS + 8 * half + 8)
                w = wgt[:, half, :, :]
                step(dve.reciprocal(w.rearrange("p t h -> p (t h)"), esum[:, half, :, :].rearrange("p t h -> p (t h)")))
                if l < 2:
                    step(dve.tensor_tensor(w, w, gates[:, :, 8 + 8 * half:16 + 8 * half], ALU.mult))

            def mix(l, half, tt):
                dve.wait_ge(pv_done, l * HEADS + 8 * half + 8)
                ps = bank[:, 4 + 2 * half + tt, :].rearrange("p (h d) -> p h d", d=DH)
                w = bc_last(wgt[:, half, tt, :], DH)
                if l < 2:
                    step(dve.tensor_tensor(res_tile(tt, 1), ps, w, ALU.mult))
                    step(dve.tensor_tensor(res[:, tt, 0:512], res[:, tt, 0:512], res[:, tt, 512:1024], ALU.add))
                    dve.nop().then_inc(mix_done, 1)
                else:
                    dve.tensor_tensor(res_tile(tt, half), ps, w, ALU.mult).then_inc(mix_done, 1)

            def res_tile(tt, half):
                return res[:, tt, half * 512:(half + 1) * 512].rearrange("p (h d) -> p h d", d=DH)

            def norm(n, tt):
                st = nstat[:, tt, :]
                for hf in range(2):
                    c = half_rows(hf)
                    at = sum_of(n) * PIECES + piece(tt, hf)
                    rows = (res if n < 4 else x)[:, tt, c]
                    if n == 4:
                        dve.wait_ge(normed, normed_by(3, tt, hf))
                    else:
                        dve.wait_ge(acc_full, at)
                        acc = bank[:, 4 + 2 * tt + hf, :]
                        if n == 0:
                            dve.wait_ge(x_rows_in, 2 * 16)
                        if 0 < n < 4:
                            dve.wait_ge(normed, normed_by(n - 1, tt, hf))
                        if n < 4:
                            dve.scalar_tensor_tensor(rows, x[:, tt, c], ALPHA, acc, ALU.mult,
                                                     ALU.add).then_inc(acc_drained, 1)
                        else:
                            dve.tensor_tensor(rows, x[:, tt, c], acc, ALU.add).then_inc(acc_drained, 1)
                        dve.wait_ge(acc_drained, at)
                    ins = dve.bn_stats(st[:, 6 * hf:6 * hf + 6], rows)
                step(ins)
                if n < 4:
                    dve.bn_aggr(st[:, 12:14], st[:, 0:12]).then_inc(sum_done, 1)
                else:
                    step(dve.bn_aggr(st[:, 12:14], st[:, 0:12]))
                    dve.scalar_tensor_tensor(st[:, 13:14], st[:, 12:13], st[:, 12:13], st[:, 13:14], ALU.mult,
                                             ALU.add).then_inc(sum_done, 1)
                dve.wait_ge(root_done, sum_done_at(n, tt))
                step(dve.reciprocal(st[:, 15:16], st[:, 14:15]))
                if n == 4:
                    dve.wait_ge(gain4_in, 16)
                else:
                    dve.wait_ge(gains_in, 2 * 16 * (n + 1) if n < 4 else 16 * (8 + n - 4))
                for hf in range(2):
                    c = half_rows(hf)
                    if n < 4:
                        step(dve.scalar_tensor_tensor(res[:, tt, c], res[:, tt, c], st[:, 12:13], gains[:, 0, c],
                                                      ALU.subtract, ALU.mult))
                        dve.scalar_tensor_tensor(x[:, tt, c], res[:, tt, c], st[:, 15:16], gains[:, 1, c], ALU.mult,
                                                 ALU.add).then_inc(normed, 1)
                    else:
                        gain = gain4[:, c] if n == 4 else gains[:, 0, c]
                        dve.scalar_tensor_tensor(res[:, tt, c], x[:, tt, c], st[:, 15:16], gain, ALU.mult,
                                                 ALU.mult).then_inc(normed, 1)

            def xT_out(n, tt):
                for q in range(2):
                    part = (slice(None), slice(4 * q, 4 * q + 4), slice(tt * P, (tt + 1) * P))
                    turned_low(dve, (n, "xT", tt, q), a_lo[part], a_hi[part])

            def around_norm(l, kind, norms):
                keys, turn = tail(l, kind), norms[-1]
                for n in norms:
                    norm(n, 0)
                split_behind(dve, keys[1], split_low)
                if turn != 8:
                    xT_out(turn, 0)
                for n in norms:
                    norm(n, 1)
                if turn != 8:
                    xT_out(turn, 1)

            def feed_forward(l):
                for j in range(HEAD):
                    split_behind(dve, (l, f"up{j}"), split_low)
                for kind, j in ffn_order():
                    if kind == "up":
                        up(l, j)
                    if (kind != "up" or j >= HEAD) and (l, f"{kind}{j}") not in tail(l, "down"):
                        split_behind(dve, (l, f"{kind}{j}"), split_low)

            def up(l, j):
                key = (l, "up", j)
                b = bank_of(key)
                full = h_full[j % 2]
                if l < 2:
                    dve.wait_ge(act_gate, l * FT + j + 1)
                    dve.tensor_tensor(full, gate_a[j % 2], b[:, S:2 * S], ALU.mult).then_inc(*drained(key))
                    wait_drained(dve, key)
                else:
                    m = l - 2
                    dve.wait_ge(conv_in, m * FT + j + 1)
                    for tap in (1, 0):
                        lag = 2 - tap
                        for i, c in enumerate((cval[j % 2], cgate[j % 2])):
                            ins = dve.scalar_tensor_tensor(
                                c[:, lag:], b[:, i * S:(i + 1) * S - lag],
                                conv_col[:, m, i * FT + j, tap:tap + 1], c[:, lag:], ALU.mult, ALU.add)
                        if tap == 1:
                            step(ins)
                    ins.then_inc(conv_done, 1)
                    dve.wait_ge(conv_done, m * FT + j + 1)
                    dve.nop().then_inc(*drained(key))
                    dve.wait_ge(silu_done, m * FT + j + 1)
                    step(dve.tensor_tensor(full, gate_a[j % 2], cval[j % 2], ALU.mult))
                if j >= HSLOTS:
                    wait_used(dve, (l, f"down{(j - HSLOTS) // 2}"))
                step(dve.tensor_scalar(h_hi[:, j % HSLOTS, :], full, 1.0, None, ALU.mult))
                dve.tensor_tensor(h_lo[:, j % HSLOTS, :], full, h_hi[:, j % HSLOTS, :].bitcast(F32),
                                  ALU.subtract).then_inc(h_done, 1)

            dve.wait_ge(a_hi_done, 1)
            dve.tensor_tensor(a_lo[:, :, :], xT0, a_hi[:, :, :].bitcast(F32), ALU.subtract).then_inc(a_lo_done, 1)
            for i in range(PARTS):
                split_low(dve, i)
            def split_small(whole, parts, done):
                step(dve.tensor_scalar(parts[0], whole, 1.0, None, ALU.mult))
                dve.tensor_tensor(parts[1], whole, parts[0].bitcast(F32), ALU.subtract).then_inc(done, 1)

            def start():
                dve.wait_ge(start_in, STARTS)
                split_small(w_gate_in, [part[:, :, :, :] for part in w_gate], w_gate_split)
                step(dve.tensor_copy(hg_mask[:, :, :], mask_in))
                dve.tensor_tensor(lb_tmp[:, 0, :], lb[:, 1, :], lb[:, 0, :], ALU.subtract).then_inc(lb_ready, 1)
                key = ("cmpbias",)
                wait_full(dve, key)
                for tt in range(NT):
                    src = bank_of(key)[:, tt * CG * CB * 8:tt * CG * CB * 8 + NC * 8].rearrange("p (n h) -> p h n", h=8)
                    ins = dve.tensor_tensor(cmp_bias[:, tt, :, :], src, bc_mid(cmp_off[:, tt, :], 8), ALU.add)
                ins.then_inc(*drained(key))
                key = ("biasrow",)
                wait_full(dve, key)
                step(dve.tensor_tensor(bias_row[0:24, :], bank_of(key)[0:24, 0:REV], off_row[0:24, :], ALU.add))
                dve.nop().then_inc(bias_row_ready, 1)
                dve.nop().then_inc(*drained(key))

            for l in range(LAYERS):
                if l < 2:
                    for name in ("hi0", "hi1"):
                        split_behind(dve, (l, name), split_low)
                    if l == 0:
                        start()
                    for name in ("hf0", "hf1"):
                        split_behind(dve, (l, name), split_low)
                    dve.wait_ge(softplus_done, l + 1)
                    step(dve.scalar_tensor_tensor(b_t, f_t, 0.0, dec[0], ALU.min, ALU.subtract))
                    if l == 1:
                        step(dve.tensor_tensor(heads4(b_t), heads4(b_t), bc_last(lb_log[:, 1, :], S), ALU.add))
                        dve.tensor_tensor(heads4(dec[0]), heads4(b_t), bc_last(lb_log[:, 0, :], S),
                                          ALU.subtract).then_inc(gap_done, 1)
                    dve.tensor_tensor(k_t, b_t, f_t, ALU.subtract).then_inc(kdiff_done, 1)
                    split_behind(dve, (l, "hq0"), split_low)
                    if l == 1:
                        dve.wait_ge(kdiff_done, l + 1)
                        dve.wait_ge(softplus2_done, 1)
                        step(dve.tensor_tensor(heads4(b_t), heads4(b_t), bc_last(lb_log[:, 0, :], S), ALU.max))
                        step(dve.tensor_tensor(b_t, b_t, dec[0], ALU.add))
                    else:
                        dve.wait_ge(kdiff_done, l + 1)
                    dve.wait_ge(zeroed, 5)
                    for h in range(HG_HEADS):
                        ins = dve.tensor_tensor_scan(f_t[:, h * S:(h + 1) * S], ones[:, :], b_t[:, h * S:(h + 1) * S],
                                                     0.0, ALU.mult, ALU.add)
                    ins.then_inc(cumsum_done, 1)
                    dve.wait_ge(k_done, l + 1)
                    wait_drained(dve, (l, "hq0"))
                    wait_drained(dve, (l, "hq1"))
                    split_behind(dve, (l, "hq1"), split_low)
                    after(l, "hq1")
                    if l == 0:
                        dve.wait_ge(consts_in, CONSTS)
                        dve.wait_ge(lb_ready, 2)
                        step(dve.scalar_tensor_tensor(lb_log[:, 0, :], lb_tmp[:, 0, :], 0.0, lb_tmp[:, 3, :], ALU.min,
                                                      ALU.subtract))
                        step(dve.tensor_tensor(lb_log[:, 1, :], lb_log[:, 0, :], lb_tmp[:, 0, :], ALU.subtract))
                    key = (l, "kcvc")
                    wait_full(dve, key)
                    for i in range(2):
                        for g in range(2):
                            for par in range(2):
                                at = i * S + par
                                full = bank_of(key)
                                base = full[g * DH:(g + 1) * DH, at:at + 1]
                                src = bass.AP(base.tensor, base.offset,
                                              [list(base.ap[0]), [2, CMP_KT], [16, NC]])
                                lo = par * DH
                                ins = dve.tensor_tensor(blk[i][lo:lo + DH, :, g, :], src,
                                                        bc_last(pos[lo:lo + DH, l, i, :], NC), ALU.add)
                    ins.then_inc(*drained(key))
                    split_behind(dve, (l, "kcvc"), split_low)
                    for name in ("nq0", "nq1"):
                        after(l, name)
                    for name in ("nq0", "nq1"):
                        split_behind(dve, (l, name), split_low)
                    after(l, "hid")
                    split_behind(dve, (l, "kskw"), split_low)
                    after(l, "kskw")
                    after(l, "gt")
                    key = (l, "kcv")
                    wait_full(dve, key)
                    dve.tensor_copy(kc2[:, :, :].rearrange("p g n -> p (g n)"), bank_of(key)[:, 0:30])
                    dve.tensor_tensor(vc8[:, :, :], bc_mid(bank_of(key)[:, DH:2 * DH], 8),
                                      bc_last(head_blocks[:, :], DH), ALU.mult).then_inc(*drained(key))
                    split_behind(dve, (l, "hg0"), split_low)
                    after(l, "hg0")
                    gf = gates[:, :, :].rearrange("p t c -> p (t c)")
                    key = (l, "gtT")
                    wait_full(dve, key)
                    dve.tensor_scalar(gf, bank_of(key)[:, 0:48], 1.0, None, ALU.add).then_inc(*drained(key))
                    wait_drained(dve, key)
                    step(dve.reciprocal(gf, gf))
                    for odd in range(2):
                        key = (l, "cs", odd)
                        wait_full(dve, key)
                        src = bank_of(key)[:, 0:P].rearrange("p (t j n) -> p t j n", t=NT, j=4)[:, :, :, 0:NC]
                        for tt in range(NT):
                            ins = dve.tensor_tensor(cl[:, tt, odd::2, :], src[:, tt, :, :],
                                                    cmp_bias[:, tt, odd::2, :], ALU.add)
                        ins.then_inc(*drained(key))
                    wait_drained(dve, key)
                    c3 = cl[:, :, :, :].rearrange("p t h n -> p (t h) n")
                    e3 = ce[:, :, :, :].rearrange("p t h n -> p (t h) n")
                    step(dve.tensor_reduce(cmx[:, 0, :], c3, AX_X, ALU.min))
                    dve.tensor_tensor(c3, c3, bc_last(cmx[:, 0, :], NC), ALU.subtract).then_inc(cmp_logit, 1)
                    dve.wait_ge(cmp_exp, l + 1)
                    step(dve.tensor_reduce(cmx[:, 1, :], e3, AX_X, ALU.add))
                    step(dve.reciprocal(cmx[:, 1, :], cmx[:, 1, :]))
                    for tt in range(NT):
                        ins = dve.tensor_tensor(cmx[:, 2, 8 * tt:8 * tt + 8], cmx[:, 1, 8 * tt:8 * tt + 8],
                                                gates[:, tt, 0:8], ALU.mult)
                    step(ins)
                    step(dve.tensor_tensor(e3, e3, bc_last(cmx[:, 2, :], NC), ALU.mult))
                    for tt in range(NT):
                        ins = dve.tensor_tensor(cp[:, tt, :, 0:NC], ce[:, tt, :, :], bc_mid(cmp_on[:, tt, :], 8),
                                                ALU.mult)
                    ins.then_inc(cmp_prob, 1)
                    split_behind(dve, (l, "hg1"), split_low)
                    after(l, "hg1")
                    after(l, "vsvw")
                    split_behind(dve, (l, "vsvw"), split_low)
                    key = (l, "cT")
                    wait_full(dve, key)
                    dve.tensor_copy(cpT[:, :, :].rearrange("p t c -> p (t c)"),
                                    bank_of(key)[:, 0:2 * P]).then_inc(*drained(key))
                    dve.wait_ge(hg_rstd, l + 1)
                    step(dve.reciprocal(stat[:, 8:16], stat[:, 8:16]))
                    dve.wait_ge(g_scaled, l + 1)
                    for tt in range(NT):
                        key = (l, "ho", tt)
                        for h in range(HG_HEADS):
                            c = slice(h * P, (h + 1) * P)
                            ins = dve.scalar_tensor_tensor(o_hg[tt][:, c], bank_of(key)[:, c],
                                                           stat[:, 8 + 4 * tt + h:9 + 4 * tt + h], g_hg[:, tt, c],
                                                           ALU.mult, ALU.mult)
                        ins.then_inc(*drained(key))
                    for tt in range(NT):
                        key = (l, "co", tt)
                        wait_full(dve, key)
                        dve.tensor_copy(res[:, tt, 0:512], bank_of(key)).then_inc(*drained(key))
                    attention(l)
                    for tt in range(NT):
                        part = (slice(None), slice(0, 4), slice(tt * P, (tt + 1) * P))
                        turned_low(dve, (l, "hoT", tt), a_lo[part], a_hi[part])
                    for tt in range(NT):
                        part = (slice(None), slice(4, 8), slice(tt * P, (tt + 1) * P))
                        turned_low(dve, (l, "oT", 1, tt), a_lo[part], a_hi[part])
                else:
                    if l == 2:
                        for j in range(HEAD):
                            split_behind(dve, (l, f"v{j}"), split_low)
                        split_behind(dve, (l, "qi0"), split_low)
                        dve.wait_ge(ki_rstd, 1)
                        for tt in range(NT):
                            step(dve.tensor_scalar(gates[:, tt, 0:16], small[:, tt, DH:80], 16.0 ** -0.5, None, ALU.mult))
                            step(dve.scalar_tensor_tensor(small[:, tt, 0:DH], small[:, tt, 0:DH],
                                                          stat[:, 4 + tt:5 + tt], idx_norm[:, :], ALU.mult, ALU.mult))
                            dve.tensor_copy(small[:, tt, DH:2 * DH], small[:, tt, 0:DH]).then_inc(ki_normed, 1)
                        for j in range(1, 4):
                            split_behind(dve, (l, f"qi{j}"), split_low)
                        dve.wait_ge(score_in, 16)
                        for i in range(16):
                            if i % 3 == 0:
                                split_behind(dve, (l, attention_tiles()[i // 3]), split_low)
                            wait_drained(dve, (l, "I", i))
                            if i > 0:
                                dve.wait_ge(relu_used, i)
                            r = relu[i % 2]
                            dve.scalar_tensor_tensor(score[:, 0:S], r[:, 0:S], gates[:, 1, i:i + 1], score[:, 0:S],
                                                     ALU.mult, ALU.add)
                            dve.scalar_tensor_tensor(score[:, S:TRI], r[:, S:TRI], gates[:, 0, i:i + 1],
                                                     score[:, S:TRI], ALU.mult, ALU.add).then_inc(relu_used, 1)
                        dve.wait_ge(relu_used, 16)
                        for i, name in enumerate(attention_tiles()[6:]):
                            split_behind(dve, (l, name), split_low)
                            choose(0, range(2 * i, 2 * i + 2))
                    else:
                        for name in projections(l):
                            split_behind(dve, (l, name), split_low)
                    attention(l)
                    for half in range(2):
                        for tt in range(NT):
                            part = (slice(None), slice(4 * half, 4 * half + 4), slice(tt * P, (tt + 1) * P))
                            turned_low(dve, (l, "oT", half, tt), a_lo[part], a_hi[part])
                split_behind(dve, (l, "out0"), split_low)
                mid, end = norm_after(l)
                around_norm(l, "out", [mid])
                if l == 1:
                    dve.wait_ge(w_idx_loaded, 16)
                    split_small(w_idx_in, [part[:, :, :] for part in w_idx], w_idx_split)
                feed_forward(l)
                around_norm(l, "down", [3, 4] if end == 3 else [end])

        @block.gpsimd
        def _(pool):
            step = steps(pool, pool_step)
            pool.memset(s_hg, 0.0).then_inc(zeroed, 1)
            pool.memset(hid_v[:, :, :], 0.0).then_inc(zeroed, 1)
            pool.memset(cp[:, :, :, :], 0.0).then_inc(zeroed, 1)
            pool.memset(ones[:, :], 1.0).then_inc(zeroed, 1)
            pool.memset(eps_ln[:, :], 1e-5)
            pool.memset(eps_rms[:, :], 1e-6).then_inc(zeroed, 1)

            def load_gains(g, b):
                pool.dma_start(gains[:, 0, :], g.partition_broadcast(P)).then_inc(gains_in, 16)
                if b is not None:
                    pool.dma_start(gains[:, 1, :], b.partition_broadcast(P)).then_inc(gains_in, 16)

            def next_gains(n, g, b=None):
                pool.wait_ge(normed, n * PIECES)
                load_gains(g, b)

            def around_norm(l, kind):
                keys = tail(l, kind)
                split_behind(pool, keys[0], split_low_pool)
                split_behind(pool, keys[2], split_low_pool)

            load_gains(a["ln1_g"][0], a["ln1_b"][0])
            for l in range(2):
                pool.wait_ge(cumsum_done, l + 1)
                for v in range(1, NLEV):
                    n = l * (NLEV - 1) + v
                    half = HALVES[v]
                    if v > 2:
                        pool.wait_ge(level_done, n - 2)
                    src = blocks(f_t, half)
                    mid = src[:, :, half - 1:half].to_broadcast([P, D // (2 * half), 2 * half])
                    pool.tensor_tensor(blocks(dec[v % 2], half), src, mid, ALU.subtract).then_inc(diff_done, 1)
                    if v >= 4 and v - 4 < len(POOL_AFTER) - 1:
                        split_behind(pool, (l, POOL_AFTER[v - 4]), split_low_pool)
                split_behind(pool, (l, POOL_AFTER[-1]), split_low_pool)
                for i in range(2):
                    wait_drained(pool, (l, f"hg{i}"))
                for tt in range(NT):
                    g3 = g_hg[:, tt, :].rearrange("p (h v) -> p h v", h=HG_HEADS)
                    ins = pool.tensor_tensor(g3, g3, bc_mid(gnorm[:, l, :], HG_HEADS), ALU.mult)
                ins.then_inc(g_scaled, 1)
                around_norm(l, "out")
                next_gains(2 * l + 1, a["ln2_g"][l], a["ln2_b"][l])
                if l == 1:
                    pool.dma_start(gain4, a["rms_g"][0].partition_broadcast(P)).then_inc(gain4_in, 16)
                    pool.dma_start(w_idx_in, a["w_idx"]).then_inc(w_idx_loaded, 16)
                    pool.dma_start(score, a["causal"]).then_inc(score_in, 16)
                around_norm(l, "down")
                if l == 0:
                    next_gains(2, a["ln1_g"][1], a["ln1_b"][1])
            next_gains(5, a["rms_g"][1])
            pool.wait_ge(unsel_done, 1)
            for h in range(8):
                if h >= 2:
                    pool.wait_ge(logit_done, 2 * HEADS + 8 + h - 1)
                o = bias_s[h % 2]
                pool.tensor_tensor(o[:, 0:S], bias_of(16 + h, 1), unsel[:, 0:S], ALU.add)
                pool.tensor_tensor(o[:, S:TRI], bias_of(16 + h, 0), unsel[:, S:TRI],
                                   ALU.add).then_inc(bias_sel, 1)
            around_norm(2, "out")
            next_gains(6, a["rms_g"][2])
            pool.wait_ge(logit_done, 3 * HEADS)
            pool.dma_start(neglog, a["neglog"]).then_inc(neglog_in, 16)
            pool.wait_ge(neglog_in, 16)
            for h in range(16):
                ins = pool.tensor_tensor(bias_t[:, 8 + h, :], bias_t[:, 8 + h, :],
                                         neglog, ALU.add)
            ins.then_inc(bias_log, 1)
            around_norm(2, "down")
            next_gains(7, a["rms_g"][3])
            around_norm(3, "out")
            next_gains(8, a["final_g"])


def bucket(dist):
    n = np.maximum(dist, 0)
    exact = BUCKETS // 2
    nf = np.maximum(n, 1).astype(np.float32)
    large = exact + (np.log(nf / np.float32(exact)) / np.float32(np.log(128 / exact))
                     * np.float32(BUCKETS - exact)).astype(np.int32)
    return np.where(n < exact, n, np.minimum(large, BUCKETS - 1))


def constants():
    f = np.float32
    p = np.arange(P)
    rev = np.arange(REV) - (P - 1)
    one_hot = -((bucket(rev)[None, :] == np.arange(BUCKETS)[:, None]) & (rev >= 0)).astype(f)
    dc = np.arange(2 * S) - (S - 1)
    dc = dc[None, :] - 16 * np.arange(CB)[:, None]
    one_hot_c = -((bucket(dc)[:, None, :] == np.arange(BUCKETS)[None, :, None]) & (dc >= 0)[:, None, :]).astype(f)
    one_hot_c = one_hot_c.reshape(P, 2 * S)
    off_row = np.broadcast_to(np.where(rev >= 0, 0.0, -NEG).astype(f), (24, REV)).copy()
    masks = np.zeros((P, len(HALVES), P), np.float32)
    for v, half in enumerate(HALVES):
        if half == 0:
            masks[:, v, :] = np.eye(P, dtype=np.float32)
        elif half < P:
            same = (p[:, None] // (2 * half)) == (p[None, :] // (2 * half))
            masks[:, v, :] = same & (p[:, None] % (2 * half) < half) & (p[None, :] % (2 * half) >= half)
    t = np.arange(S).reshape(NT, P).T
    done = (np.arange(NC) * 16 + 31)[None, None, :] <= t[:, :, None]
    s = np.arange(S)
    causal = np.concatenate([np.where(s[None, :] <= P + p[:, None], 0.0, NEG),
                             np.where(s[None, :P] <= p[:, None], 0.0, NEG)], axis=1)
    dist = P + p[:, None] - s[None, :]
    count = ((dist >= 0) & (dist <= P)).astype(int) + ((dist >= 0) & (dist % 4 == 0)) + ((dist >= 0) & (dist % 16 == 0))
    log_count = np.where(count > 0, -np.log(np.maximum(count, 1)), -NEG)
    return {
        "one_hot": one_hot, "one_hot_c": one_hot_c, "off_row": off_row, "ident": np.eye(P, dtype=f),
        "hg_mask": masks,
        "cmp_off": np.where(done, 0.0, -NEG).astype(f), "cmp_on": done.astype(f),
        "head_blocks": (p[:, None] // NCP == np.arange(8)[None, :]).astype(f),
        "causal": causal.astype(f), "neglog": log_count[:, ::-1].astype(f).reshape(P, S),
    }


def col_tile(w):
    return w.reshape(KT, P, S).transpose(1, 0, 2).reshape(P, TILE)


def row_tile(w):
    return w.reshape(2, P, D).transpose(1, 0, 2).reshape(P, TILE)


def layout(i):
    cols = {}
    for l in range(2):
        w = i["w_in"][l]
        at = dict(zip(("hq", "hf", "hi", "hg", "nq", "kc", "vc", "ks", "vs", "kw", "vw", "gt"),
                      (0, 512, 1024, 1536, 2048, 2560, 2688, 2816, 2944, 3072, 3200, 3328)))
        for n in ("hq", "hf", "hi", "hg", "nq"):
            for j in range(2):
                cols[(l, f"{n}{j}")] = col_tile(w[:, at[n] + S * j:at[n] + S * (j + 1)])
        for n in ("kcvc", "kskw", "vsvw"):
            cols[(l, n)] = col_tile(np.concatenate([w[:, at[n[:2]]:at[n[:2]] + P], w[:, at[n[2:]]:at[n[2:]] + P]], 1))
        for n, src in (("w1k", "cmp_w1_k"), ("w1v", "cmp_w1_v")):
            cols[(l, n)] = i[src][l].reshape(CMP_KT, P, P).transpose(1, 0, 2).reshape(P, TILE)
        for j in range(FT):
            c = slice(j * P, (j + 1) * P)
            cols[(l, f"up{j}")] = col_tile(np.concatenate([i["w_ffn_gate"][l][:, c], i["w_ffn_up"][l][:, c]], 1))
        for r in range(4):
            cols[(l, f"out{r}")] = row_tile(i["w_out"][l][r * S:(r + 1) * S])
        for r in range(FT // 2):
            cols[(l, f"down{r}")] = row_tile(i["w_ffn_down"][l][r * S:(r + 1) * S])
    e, o = i["w_in_even_2"][0], i["w_in_odd_2"][0]
    for l, w, starts in ((2, e, {"q": (0, 1536), "k": (512, 2048), "v": (1024, 2560)}),
                         (3, o, {"q": (0, 512), "k": (1024, 1536), "v": (2048, 2560)})):
        for n, (a, b) in starts.items():
            for j in range(4):
                c = (a, b)[j // 2] + S * (j % 2)
                cols[(l, f"{n}{j}")] = col_tile(w[:, c:c + S])
        for j in range(FT):
            v = i["w_up_2"][l - 2]
            cols[(l, f"up{j}")] = col_tile(np.concatenate([v[:, j * P:(j + 1) * P],
                                                           v[:, DFF + j * P:DFF + (j + 1) * P]], 1))
        for r in range(4):
            cols[(l, f"out{r}")] = row_tile(i["w_o_2"][l - 2][r * S:(r + 1) * S])
        for r in range(FT // 2):
            cols[(l, f"down{r}")] = row_tile(i["w_down_2"][l - 2][r * S:(r + 1) * S])
    for j in range(4):
        cols[(2, f"qi{j}")] = col_tile(e[:, 3072 + S * j:3072 + S * (j + 1)])

    x = i["x"][0]
    taps = np.concatenate([i["conv_w_2"], i["conv_b_2"][:, None, :]], 1)
    w2k, w2v = i["cmp_w2_k"], i["cmp_w2_v"]
    p2 = np.stack([i["cmp_pos_k"], i["cmp_pos_v"]], 1)
    rel_c = np.zeros((CB, BUCKETS, CB, 8), np.float32)
    for n in range(CB):
        rel_c[n, :, n, :] = i["rel_bias"]
    d = {
        "rel_c": rel_c.reshape(P, CB * 8),
        "stream": np.stack([cols[k] for k in stream_order()]),
        "xT": x.T.reshape(KT, P, S).transpose(1, 0, 2), "x": x.reshape(NT, P, D).transpose(1, 0, 2),
        "rel": np.concatenate([i["rel_bias"], i["rel_bias_2"]], 1),
        "lb": i["hg_lb_param"].reshape(2, HG_HEADS, P).transpose(2, 0, 1),
        "gnorm": np.broadcast_to(i["hg_norm_w"][None], (P, 2, P)),
        "idx_norm": np.broadcast_to(i["idx_k_norm_2"], (P, DH)),
        "pos": p2.reshape(2, 2, CMP_KT, 2, DH).transpose(3, 4, 0, 1, 2).reshape(P, 2, 2, CMP_KT),
        "w2": np.concatenate([w2k, w2k, w2v], 2).transpose(1, 0, 2),
        "w_gate": i["w_in"][:, :, 3328:3352].reshape(2, KT, P, 24).transpose(2, 0, 1, 3),
        "w_idx": e[:, 4096:4176].reshape(KT, P, 80).transpose(1, 0, 2),
        "rms_g": np.stack([i["attn_norm_2"][0], i["ffn_norm_2"][0], i["attn_norm_2"][1], i["ffn_norm_2"][1]]),
        "conv_col": taps.reshape(2, 4, 2 * FT, P).transpose(3, 0, 2, 1),
        "ln1_g": i["ln1_g"], "ln1_b": i["ln1_b"], "ln2_g": i["ln2_g"], "ln2_b": i["ln2_b"],
        "final_g": i["final_norm_2"],
    }
    d.update(constants())
    return {k: np.ascontiguousarray(v) for k, v in d.items()}


def kernel(**inputs):
    import concourse.bacc as bacc
    from concourse.bass_utils import run_bass_kernel_spmd

    arrays = layout({k: np.asarray(v) for k, v in inputs.items()})
    nc = bacc.Bacc("TRN2", target_bir_lowering=False, num_devices=1)
    args = {k: nc.dram_tensor(f"in_{k}", v.shape, mybir.dt.from_np(v.dtype), kind="ExternalInput").ap()
            for k, v in arrays.items()}
    args["out"] = nc.dram_tensor("out", (P, NT, D), F32, kind="ExternalOutput").ap()
    build(nc, args)
    r = run_bass_kernel_spmd(nc, [{f"in_{k}": v for k, v in arrays.items()}], core_ids=[0])
    return r.results[0]["out"].transpose(1, 0, 2).reshape(1, S, D)
```
